# Optimizing a Trainium2 kernel written in Bass

```python
import jax, jax.numpy as jnp
from jax import lax
import numpy as np
import math

D_MODEL = 1024
BATCH = 1
SEQ = 256
DEPTH = 1

MLA_HEADS = 8
Q_LORA_RANK = 256
KV_LORA_RANK = 128
QK_NOPE_DIM = 64
QK_ROPE_DIM = 32
V_HEAD_DIM = 64
MLA_SCALE = (QK_NOPE_DIM + QK_ROPE_DIM) ** -0.5
Q_BLOCK = 128

RET_HEADS = 8
RET_HEAD_DIM = 64
RET_CHUNK = 128

D_MIX = MLA_HEADS * V_HEAD_DIM + RET_HEADS * RET_HEAD_DIM
D_FF = 2816
ROPE_THETA = 10000.0
EPS = 1e-6

IN_SIZES = (Q_LORA_RANK, KV_LORA_RANK, QK_ROPE_DIM,
            RET_HEADS * RET_HEAD_DIM, RET_HEADS * RET_HEAD_DIM,
            RET_HEADS * RET_HEAD_DIM, RET_HEADS * RET_HEAD_DIM)
D_IN = sum(IN_SIZES)
SPLIT_POINTS = tuple(int(s) for s in np.cumsum(IN_SIZES)[:-1])


def rms_norm(x, g):
    xf = x.astype(jnp.float32)
    y = xf * lax.rsqrt(jnp.mean(xf * xf, axis=-1, keepdims=True) + EPS)
    return (y * g.astype(jnp.float32)).astype(x.dtype)

def swiglu(x, w_gate, w_up, w_down):
    return (jax.nn.silu(x @ w_gate) * (x @ w_up)) @ w_down

def rope(x, pos_f):
    half = x.shape[-1] // 2
    inv = ROPE_THETA ** (-jnp.arange(half, dtype=jnp.float32) / half)
    ang = pos_f[..., None] * inv
    cos = jnp.cos(ang)[:, :, None, :]
    sin = jnp.sin(ang)[:, :, None, :]
    x1 = x[..., :half].astype(jnp.float32)
    x2 = x[..., half:].astype(jnp.float32)
    return jnp.concatenate([x1 * cos - x2 * sin, x1 * sin + x2 * cos], axis=-1).astype(x.dtype)

def mla_group(c_q, c_kv, k_pe_raw, pos_f, q_norm, w_uq, kv_norm, w_ukv):
    B, S, _ = c_q.shape
    H = MLA_HEADS
    q = (rms_norm(c_q, q_norm) @ w_uq).reshape(B, S, H, QK_NOPE_DIM + QK_ROPE_DIM)
    q_nope = q[..., :QK_NOPE_DIM]
    q_pe = rope(q[..., QK_NOPE_DIM:], pos_f)
    kv = (rms_norm(c_kv, kv_norm) @ w_ukv).reshape(B, S, H, QK_NOPE_DIM + V_HEAD_DIM)
    k_nope = kv[..., :QK_NOPE_DIM]
    v = kv[..., QK_NOPE_DIM:]
    k_pe = rope(k_pe_raw[:, :, None, :], pos_f)[:, :, 0]
    nb = S // Q_BLOCK

    def block(args):
        qn, qp = args
        s = (jnp.einsum('bqhd,bkhd->bhqk', qn, k_nope).astype(jnp.float32)
             + jnp.einsum('bqhr,bkr->bhqk', qp, k_pe).astype(jnp.float32))
        p = jax.nn.softmax(s * MLA_SCALE, axis=-1)
        return jnp.einsum('bhqk,bkhd->bqhd', p.astype(v.dtype), v)

    qn_b = q_nope.reshape(B, nb, Q_BLOCK, H, QK_NOPE_DIM).swapaxes(0, 1)
    qp_b = q_pe.reshape(B, nb, Q_BLOCK, H, QK_ROPE_DIM).swapaxes(0, 1)
    out = lax.map(block, (qn_b, qp_b))
    return out.swapaxes(0, 1).reshape(B, S, H * V_HEAD_DIM)

def retention_scan(q, k, v, log_gamma, inclusive):
    B, S, H, d = q.shape
    C = RET_CHUNK
    nc = S // C
    idx = jnp.arange(C, dtype=jnp.float32)
    rel = idx[:, None] - idx[None, :]
    mask = (rel >= 0) if inclusive else (rel > 0)
    d_inner = jnp.where(mask[None], jnp.exp(log_gamma[:, None, None] * jnp.maximum(rel, 0.0)[None]), 0.0)
    q_dec = jnp.exp(log_gamma[None, :] * (idx[:, None] + 1.0))
    k_dec = jnp.exp(log_gamma[None, :] * (C - 1.0 - idx)[:, None])
    c_dec = jnp.exp(log_gamma * C)

    def to_chunks(t):
        return t.reshape(B, nc, C, H, d).swapaxes(0, 1)

    def step(state, inp):
        qc, kc, vc = inp
        s = jnp.einsum('bihd,bjhd->bhij', qc, kc) * d_inner
        inner = jnp.einsum('bhij,bjhe->bihe', s, vc)
        cross = jnp.einsum('bihd,bhde->bihe', qc * q_dec[None, :, :, None], state)
        state = (state * c_dec[None, :, None, None]
                 + jnp.einsum('bjhd,bjhe->bhde', kc * k_dec[None, :, :, None], vc))
        return state, inner + cross

    state0 = jnp.zeros((B, H, d, d), jnp.float32)
    _, out = lax.scan(step, state0, (to_chunks(q), to_chunks(k), to_chunks(v)))
    return out.swapaxes(0, 1).reshape(B, S, H, d)

def retention_group(r_q, r_k, r_v, r_g, pos_f, decay_fwd, decay_bwd):
    B, S, _ = r_q.shape
    shp = (B, S, RET_HEADS, RET_HEAD_DIM)
    q = rope(r_q.reshape(shp), pos_f).astype(jnp.float32)
    k = rope(r_k.reshape(shp), pos_f).astype(jnp.float32) * (RET_HEAD_DIM ** -0.5)
    v = r_v.reshape(shp).astype(jnp.float32)
    lg_f = jax.nn.log_sigmoid(decay_fwd.astype(jnp.float32))
    lg_b = jax.nn.log_sigmoid(decay_bwd.astype(jnp.float32))
    fwd = retention_scan(q, k, v, lg_f, True)
    bwd = jnp.flip(retention_scan(jnp.flip(q, 1), jnp.flip(k, 1), jnp.flip(v, 1), lg_b, False), 1)
    o = fwd + bwd
    mu = jnp.mean(o, axis=-1, keepdims=True)
    var = jnp.mean(jnp.square(o - mu), axis=-1, keepdims=True)
    o = ((o - mu) * lax.rsqrt(var + EPS)).reshape(B, S, RET_HEADS * RET_HEAD_DIM)
    return (jax.nn.silu(r_g.astype(jnp.float32)) * o).astype(r_q.dtype)

def first_inputs(seed: int = 0) -> dict:
    key = jax.random.key(seed)
    ks = jax.random.split(key, 24)
    f32 = jnp.float32

    def w(k, shape, fan_in):
        return jax.random.normal(k, shape, f32) * (fan_in ** -0.5)

    def gain(k, shape):
        return 1.0 + 0.02 * jax.random.normal(k, shape, f32)

    L = DEPTH
    offset = jax.random.randint(ks[1], (BATCH, 1), 0, 4096, dtype=jnp.int32)
    positions = offset + jnp.arange(SEQ, dtype=jnp.int32)[None, :]
    decay_init = jnp.asarray(np.log(2.0 ** (5.0 + np.arange(RET_HEADS)) - 1.0), f32)
    return {
        "x": jax.random.normal(ks[0], (BATCH, SEQ, D_MODEL), f32),
        "positions": positions,
        "ffn1_norm": gain(ks[2], (L, D_MODEL)),
        "ffn1_w_gate": w(ks[3], (L, D_MODEL, D_FF), D_MODEL),
        "ffn1_w_up": w(ks[4], (L, D_MODEL, D_FF), D_MODEL),
        "ffn1_w_down": w(ks[5], (L, D_FF, D_MODEL), D_FF),
        "mix_norm": gain(ks[6], (L, D_MODEL)),
        "w_in": w(ks[7], (L, D_MODEL, D_IN), D_MODEL),
        "q_norm": gain(ks[8], (L, Q_LORA_RANK)),
        "w_uq": w(ks[9], (L, Q_LORA_RANK, MLA_HEADS * (QK_NOPE_DIM + QK_ROPE_DIM)), Q_LORA_RANK),
        "kv_norm": gain(ks[10], (L, KV_LORA_RANK)),
        "w_ukv": w(ks[11], (L, KV_LORA_RANK, MLA_HEADS * (QK_NOPE_DIM + V_HEAD_DIM)), KV_LORA_RANK),
        "ret_decay_fwd": decay_init[None, :] + 0.05 * jax.random.normal(ks[12], (L, RET_HEADS), f32),
        "ret_decay_bwd": decay_init[None, :] + 0.05 * jax.random.normal(ks[13], (L, RET_HEADS), f32),
        "w_o": w(ks[14], (L, D_MIX, D_MODEL), D_MIX),
        "ffn2_norm": gain(ks[15], (L, D_MODEL)),
        "ffn2_w_gate": w(ks[16], (L, D_MODEL, D_FF), D_MODEL),
        "ffn2_w_up": w(ks[17], (L, D_MODEL, D_FF), D_MODEL),
        "ffn2_w_down": w(ks[18], (L, D_FF, D_MODEL), D_FF),
        "final_norm": gain(ks[19], (D_MODEL,)),
    }

def first_block(x, positions, ffn1_norm, ffn1_w_gate, ffn1_w_up, ffn1_w_down, mix_norm, w_in,
              q_norm, w_uq, kv_norm, w_ukv, ret_decay_fwd, ret_decay_bwd, w_o,
              ffn2_norm, ffn2_w_gate, ffn2_w_up, ffn2_w_down, final_norm):
    pos_f = positions.astype(jnp.float32)
    h = x
    for l in range(DEPTH):
        h = h + 0.5 * swiglu(rms_norm(h, ffn1_norm[l]), ffn1_w_gate[l], ffn1_w_up[l], ffn1_w_down[l])
        n = rms_norm(h, mix_norm[l])
        proj = n @ w_in[l]
        c_q, c_kv, k_pe, r_q, r_k, r_v, r_g = jnp.split(proj, SPLIT_POINTS, axis=-1)
        a = mla_group(c_q, c_kv, k_pe, pos_f, q_norm[l], w_uq[l], kv_norm[l], w_ukv[l])
        r = retention_group(r_q, r_k, r_v, r_g, pos_f, ret_decay_fwd[l], ret_decay_bwd[l])
        h = h + jnp.concatenate([a, r], axis=-1) @ w_o[l]
        h = h + 0.5 * swiglu(rms_norm(h, ffn2_norm[l]), ffn2_w_gate[l], ffn2_w_up[l], ffn2_w_down[l])
    return rms_norm(h, final_norm)


DA_HEADS = 4
DA_HEAD_DIM = 64
DA_V_DIM = 2 * DA_HEAD_DIM
DA_QK_WIDTH = DA_HEADS * 2 * DA_HEAD_DIM
DA_WIDTH = DA_HEADS * DA_V_DIM
HB_HEADS = 4
HB_HEAD_DIM = 64
HB_WIDTH = HB_HEADS * HB_HEAD_DIM
MAX_NEG_LOGIT = 80.0
GC_HEADS = 4
GC_KEY_DIM = 32
GC_VAL_DIM = 64
GC_KEY_WIDTH = GC_HEADS * GC_KEY_DIM
GC_WIDTH = GC_HEADS * GC_VAL_DIM
GC_GATE_RANK = 16
GC_GATE_NORMALIZER = 16.0
CHUNK = 64
N_BRANCH = 3
D_FF_2 = 4 * D_MODEL
N_MOD = 6

IN_SIZES_2 = (DA_QK_WIDTH, DA_QK_WIDTH, DA_WIDTH,
            HB_WIDTH, HB_WIDTH, HB_WIDTH, HB_WIDTH, HB_WIDTH,
            GC_KEY_WIDTH, GC_KEY_WIDTH, GC_WIDTH, GC_WIDTH,
            GC_GATE_RANK, GC_GATE_RANK,
            N_BRANCH * D_MODEL)
D_IN_2 = (2 * DA_QK_WIDTH + DA_WIDTH + 5 * HB_WIDTH + 2 * GC_KEY_WIDTH + 2 * GC_WIDTH
        + 2 * GC_GATE_RANK + N_BRANCH * D_MODEL)


def rms_norm_2(x, g):
    xf = x.astype(jnp.float32)
    y = xf * lax.rsqrt(jnp.mean(xf * xf, axis=-1, keepdims=True) + EPS)
    return (y * g.astype(jnp.float32)).astype(x.dtype)

def split_cols(t, sizes):
    offs = np.cumsum(sizes)[:-1].tolist()
    return jnp.split(t, offs, axis=-1)

def to_heads(t, n_heads):
    b, s, w = t.shape
    return t.reshape(b, s, n_heads, w // n_heads).transpose(0, 2, 1, 3)

def from_heads(t):
    b, n, s, h = t.shape
    return t.transpose(0, 2, 1, 3).reshape(b, s, n * h)

def alibi_slopes(n):
    return jnp.array([2.0 ** (-8.0 * (i + 1) / n) for i in range(n)], dtype=jnp.float32)

def diff_attention(q, k, v, lam, slopes):
    b, h, _, s, d = q.shape
    nb = s // Q_BLOCK
    scale = d ** -0.5
    q_blocks = jnp.moveaxis(q.reshape(b, h, 2, nb, Q_BLOCK, d), 3, 0)
    starts = jnp.arange(nb, dtype=jnp.int32) * Q_BLOCK
    key_pos = jnp.arange(s, dtype=jnp.int32)

    def one_block(args):
        qb, start = args
        scores = jnp.einsum('bhiqd,bhikd->bhiqk', qb, k).astype(jnp.float32) * scale
        q_pos = start + jnp.arange(Q_BLOCK, dtype=jnp.int32)
        dist = jnp.abs(q_pos[:, None] - key_pos[None, :]).astype(jnp.float32)
        scores = scores - slopes[:, None, None, None] * dist
        p = jax.nn.softmax(scores, axis=-1)
        w = p[:, :, 0] - lam * p[:, :, 1]
        return jnp.einsum('bhqk,bhkv->bhqv', w.astype(v.dtype), v)

    out = lax.map(one_block, (q_blocks, starts))
    return jnp.moveaxis(out, 0, 2).reshape(b, h, s, v.shape[-1])

def chunk_scan(q, k, v, log_a):
    b, h, s, dk = q.shape
    dv = v.shape[-1]
    nc = s // CHUNK

    def to_chunks(t):
        return jnp.moveaxis(t.astype(jnp.float32).reshape(b, h, nc, CHUNK, t.shape[-1]), 2, 0)

    causal_in_chunk = jnp.tril(jnp.ones((CHUNK, CHUNK), dtype=bool))[:, :, None]

    def step(state, inp):
        qc, kc, vc, ac = inp
        cum = jnp.cumsum(ac, axis=2)
        o_inter = jnp.einsum('bhtk,bhkv->bhtv', qc * jnp.exp(cum), state)
        diff = cum[:, :, :, None, :] - cum[:, :, None, :, :]
        decay = jnp.where(causal_in_chunk, jnp.exp(jnp.where(causal_in_chunk, diff, 0.0)), 0.0)
        scores = jnp.einsum('bhtk,bhsk,bhtsk->bhts', qc, kc, decay)
        o_intra = jnp.einsum('bhts,bhsv->bhtv', scores, vc)
        last = cum[:, :, -1:, :]
        new_state = jnp.exp(last[:, :, 0, :])[..., None] * state + jnp.einsum(
            'bhsk,bhsv->bhkv', kc * jnp.exp(last - cum), vc)
        return new_state, o_inter + o_intra

    state0 = jnp.zeros((b, h, dk, dv), jnp.float32)
    _, o = lax.scan(step, state0, (to_chunks(q), to_chunks(k), to_chunks(v), to_chunks(log_a)))
    return jnp.moveaxis(o, 0, 2).reshape(b, h, s, dv)

def bidir_scan(q, k_fwd, k_bwd, v, la_fwd, la_bwd):
    flip = lambda t: jnp.flip(t, axis=2)
    fwd = chunk_scan(q, k_fwd, v, la_fwd)
    bwd = flip(chunk_scan(flip(q), flip(k_bwd), flip(v), flip(la_bwd)))
    return (fwd + bwd).astype(q.dtype)

def mixer_diff_attn(q_cols, k_cols, v_cols, lam_params, subln_g, layer_idx):
    b, s, _ = q_cols.shape

    def qk_heads(t):
        return t.reshape(b, s, DA_HEADS, 2, DA_HEAD_DIM).transpose(0, 2, 3, 1, 4)

    q = qk_heads(q_cols)
    k = qk_heads(k_cols)
    v = to_heads(v_cols, DA_HEADS)
    lam_init = 0.8 - 0.6 * math.exp(-0.3 * layer_idx)
    lp = lam_params.astype(jnp.float32)
    lam = jnp.exp(jnp.sum(lp[0] * lp[1])) - jnp.exp(jnp.sum(lp[2] * lp[3])) + lam_init
    o = diff_attention(q, k, v, lam, alibi_slopes(DA_HEADS))
    o = rms_norm_2(o, subln_g) * (1.0 - lam_init)
    return from_heads(o)

def mixer_hgrn2(q_cols, f_fwd_cols, f_bwd_cols, i_cols, g_cols, lower_bound, norm_g):
    q = jax.nn.silu(to_heads(q_cols, HB_HEADS)) * HB_HEAD_DIM ** -0.5
    v = to_heads(i_cols, HB_HEADS)

    def forget(cols, lb):
        z = to_heads(cols, HB_HEADS).astype(jnp.float32)
        lbh = lb.reshape(HB_HEADS, 1, HB_HEAD_DIM)
        log_f = jax.nn.log_sigmoid(z) + jnp.log1p(lbh * jnp.exp(jnp.minimum(-z, MAX_NEG_LOGIT)))
        k = (1.0 - lbh) * jax.nn.sigmoid(-z)
        return k, log_f

    k_f, la_f = forget(f_fwd_cols, lower_bound[0])
    k_b, la_b = forget(f_bwd_cols, lower_bound[1])
    o = rms_norm_2(bidir_scan(q, k_f, k_b, v, la_f, la_b), norm_g)
    return from_heads(o) * jax.nn.silu(g_cols)

def mixer_gla(q_cols, k_cols, v_cols, g_cols, lr_fwd, lr_bwd, gate_w2, gate_b, norm_g):
    q = to_heads(q_cols, GC_HEADS) * GC_KEY_DIM ** -0.5
    k = to_heads(k_cols, GC_HEADS)
    v = to_heads(v_cols, GC_HEADS)

    def log_decay(lr, w2, bias):
        z = (jnp.einsum('bsr,rk->bsk', lr, w2) + bias).astype(jnp.float32)
        return to_heads(jax.nn.log_sigmoid(z) / GC_GATE_NORMALIZER, GC_HEADS)

    la_f = log_decay(lr_fwd, gate_w2[0], gate_b[0])
    la_b = log_decay(lr_bwd, gate_w2[1], gate_b[1])
    o = rms_norm_2(bidir_scan(q, k, k, v, la_f, la_b), norm_g)
    return from_heads(o) * jax.nn.silu(g_cols)

def second_inputs(seed: int = 0) -> dict:
    key = jax.random.key(seed)
    ks = jax.random.split(key, 21)
    nrm = lambda k, shape, scale: jax.random.normal(k, shape, jnp.float32) * scale
    gain = lambda k, shape: 1.0 + 0.05 * jax.random.normal(k, shape, jnp.float32)
    return {
        "x": nrm(ks[0], (BATCH, SEQ, D_MODEL), 1.0),
        "c": nrm(ks[1], (BATCH, D_MODEL), 1.0),
        "ada_w": nrm(ks[2], (DEPTH, D_MODEL, N_MOD * D_MODEL), 0.5 * D_MODEL ** -0.5),
        "ada_b": nrm(ks[3], (DEPTH, N_MOD * D_MODEL), 0.02),
        "norm_mix_g": gain(ks[4], (DEPTH, D_MODEL)),
        "norm_mlp_g": gain(ks[5], (DEPTH, D_MODEL)),
        "w_in": nrm(ks[6], (DEPTH, D_MODEL, D_IN_2), D_MODEL ** -0.5),
        "diff_lambda": nrm(ks[7], (DEPTH, 4, DA_HEAD_DIM), 0.1),
        "diff_subln_g": gain(ks[8], (DEPTH, DA_V_DIM)),
        "hgrn_lb_logits": nrm(ks[9], (DEPTH, 2, HB_WIDTH), 0.1),
        "hgrn_norm_g": gain(ks[10], (DEPTH, HB_HEAD_DIM)),
        "gla_gate_w2": nrm(ks[11], (DEPTH, 2, GC_GATE_RANK, GC_KEY_WIDTH), GC_GATE_RANK ** -0.5),
        "gla_gate_b": nrm(ks[12], (DEPTH, 2, GC_KEY_WIDTH), 0.1),
        "gla_norm_g": gain(ks[13], (DEPTH, GC_VAL_DIM)),
        "w_up_a": nrm(ks[14], (DEPTH, DA_WIDTH, D_MODEL), DA_WIDTH ** -0.5),
        "w_up_b": nrm(ks[15], (DEPTH, HB_WIDTH, D_MODEL), HB_WIDTH ** -0.5),
        "w_up_c": nrm(ks[16], (DEPTH, GC_WIDTH, D_MODEL), GC_WIDTH ** -0.5),
        "w_out": nrm(ks[17], (DEPTH, D_MODEL, D_MODEL), D_MODEL ** -0.5),
        "mlp_w1": nrm(ks[18], (DEPTH, D_MODEL, D_FF_2), D_MODEL ** -0.5),
        "mlp_w2": nrm(ks[19], (DEPTH, D_FF_2, D_MODEL), D_FF_2 ** -0.5),
        "final_norm_g": gain(ks[20], (D_MODEL,)),
    }

def second_block(x, c, ada_w, ada_b, norm_mix_g, norm_mlp_g, w_in, diff_lambda, diff_subln_g,
              hgrn_lb_logits, hgrn_norm_g, gla_gate_w2, gla_gate_b, gla_norm_g,
              w_up_a, w_up_b, w_up_c, w_out, mlp_w1, mlp_w2, final_norm_g):
    lb_w = jax.nn.softmax(hgrn_lb_logits.astype(jnp.float32), axis=0)
    lower_bounds = jnp.cumsum(lb_w, axis=0) - lb_w[0:1]
    cond = jax.nn.silu(c)
    for l in range(DEPTH):
        mod = cond @ ada_w[l] + ada_b[l]
        sh_m, sc_m, gt_m, sh_f, sc_f, gt_f = [t[:, None, :] for t in jnp.split(mod, N_MOD, axis=-1)]

        h = rms_norm_2(x, norm_mix_g[l]) * (1.0 + sc_m) + sh_m
        proj = jnp.einsum('bsd,de->bse', h, w_in[l])
        (a_q, a_k, a_v, b_q, b_ff, b_fb, b_i, b_g,
         c_q, c_k, c_v, c_g, c_lrf, c_lrb, gates) = split_cols(proj, IN_SIZES_2)
        o_a = mixer_diff_attn(a_q, a_k, a_v, diff_lambda[l], diff_subln_g[l], l)
        o_b = mixer_hgrn2(b_q, b_ff, b_fb, b_i, b_g, lower_bounds[l], hgrn_norm_g[l])
        o_c = mixer_gla(c_q, c_k, c_v, c_g, c_lrf, c_lrb, gla_gate_w2[l], gla_gate_b[l], gla_norm_g[l])
        g_a, g_b, g_c = jnp.split(jax.nn.sigmoid(gates), N_BRANCH, axis=-1)
        merged = g_a * (o_a @ w_up_a[l]) + g_b * (o_b @ w_up_b[l]) + g_c * (o_c @ w_up_c[l])
        x = x + gt_m * (merged @ w_out[l])

        h = rms_norm_2(x, norm_mlp_g[l]) * (1.0 + sc_f) + sh_f
        x = x + gt_f * (jnp.square(jax.nn.relu(h @ mlp_w1[l])) @ mlp_w2[l])
    return rms_norm_2(x, final_norm_g)


def setup_inputs(seed=0):
    out = dict(first_inputs(seed))
    for name, value in second_inputs(seed + 1).items():
        if name != "x":
            out[name + "_2"] = value
    return out


def reference(
    x, positions, ffn1_norm, ffn1_w_gate, ffn1_w_up, ffn1_w_down, mix_norm, w_in, q_norm, w_uq,
    kv_norm, w_ukv, ret_decay_fwd, ret_decay_bwd, w_o, ffn2_norm, ffn2_w_gate, ffn2_w_up,
    ffn2_w_down, final_norm, c_2, ada_w_2, ada_b_2, norm_mix_g_2, norm_mlp_g_2, w_in_2,
    diff_lambda_2, diff_subln_g_2, hgrn_lb_logits_2, hgrn_norm_g_2, gla_gate_w2_2, gla_gate_b_2,
    gla_norm_g_2, w_up_a_2, w_up_b_2, w_up_c_2, w_out_2, mlp_w1_2, mlp_w2_2, final_norm_g_2,
):
    x = first_block(
        x, positions, ffn1_norm, ffn1_w_gate, ffn1_w_up, ffn1_w_down, mix_norm, w_in, q_norm,
        w_uq, kv_norm, w_ukv, ret_decay_fwd, ret_decay_bwd, w_o, ffn2_norm, ffn2_w_gate,
        ffn2_w_up, ffn2_w_down, final_norm,
    )
    return second_block(
        x, c_2, ada_w_2, ada_b_2, norm_mix_g_2, norm_mlp_g_2, w_in_2, diff_lambda_2,
        diff_subln_g_2, hgrn_lb_logits_2, hgrn_norm_g_2, gla_gate_w2_2, gla_gate_b_2,
        gla_norm_g_2, w_up_a_2, w_up_b_2, w_up_c_2, w_out_2, mlp_w1_2, mlp_w2_2, final_norm_g_2,
    )


_drawn_inputs = setup_inputs


def setup_inputs(seed=0):
    import zlib

    import numpy as np

    out = dict(_drawn_inputs(seed))
    spreads = {}
    factors = {'ffn1_norm': 5.267,
     'mix_norm': 3.255,
     'q_norm': 8.0,
     'kv_norm': 8.0,
     'ffn2_norm': 7.475,
     'final_norm': 2.731,
     'norm_mix_g_2': 3.759,
     'diff_subln_g_2': 51.918,
     'hgrn_norm_g_2': 8.0,
     'gla_gate_w2_2': 3.125,
     'gla_gate_b_2': 8.0,
     'gla_norm_g_2': 8.0,
     'norm_mlp_g_2': 8.0}
    for name, (base, spread) in spreads.items():
        noise = np.random.default_rng([zlib.crc32(name.encode()), seed]).standard_normal(out[name].shape)
        drawn = base * np.exp(spread * noise) if base else spread * noise
        out[name] = __import__('jax').numpy.asarray(drawn.astype(out[name].dtype))
    for name, factor in factors.items():
        out[name] = (out[name] * factor).astype(out[name].dtype)
    return out
```

```python
from contextlib import ExitStack

import numpy as np

import concourse.bass as bass
from concourse import mybir

F32 = mybir.dt.float32
F32R = mybir.dt.float32r
I32 = mybir.dt.int32
U8 = mybir.dt.uint8
ALU = mybir.AluOpType
ACT = mybir.ActivationFunctionType
AX = mybir.AxisListType

P = 128
S = 256
M = S // P
D = 1024
KD = D // P
FF = 2816
KF = FF // P
NFULL = FF // 512
FF2 = 4096
KF2 = FF2 // P
EPS = 1e-6
UC = 2048
RAW = 4
SPLIT = 2

H = 8
QR, KVR, ROPE, NOPE, VD = 256, 128, 32, 64, 64
QK = NOPE + ROPE
C0 = QR + KVR + ROPE
MLA_SCALE = QK ** -0.5
HD = 64
ROPE_THETA = 10000.0
TURN = 2 * float(np.pi)
TURN1, TURN2 = 6.28125, 0.0019350051879882812
TURN3 = TURN - TURN1 - TURN2
ROUND = 1.5 * 2 ** 23

DH = 4
NMOD = 6
LR = 16
LAM_INIT = 0.8 - 0.6 * float(np.exp(-0.3 * 0))

U_FFN = 4 * NFULL + 2 + KF // 2
U_F1 = 0
U_IN = U_F1 + U_FFN
U_UQ = U_IN + 10
U_UKV = U_UQ + 1
U_O = U_UKV + 1
U_F2 = U_O + 4
U_IN2 = U_F2 + U_FFN
U_LR = U_IN2 + 14
U_GATES = U_LR + 1
U_UP = U_GATES + 12
U_OUT = U_UP + 4
U_W1 = U_OUT + 4
U_W2 = U_W1 + 16
U_END = U_W2 + KF2 // 2

R_G1, R_MIX, R_G2, R_GM2, R_GF2, R_ADAB, R_C, R_POS, R_Q, R_KV, R_LB, R_GB = (
    0, 8, 16, 24, 32, 40, 88, 96, 98, 100, 101, 105)
NROW = 107
ROWS = [("ffn1_norm", R_G1, KD), ("mix_norm", R_MIX, KD), ("ffn2_norm", R_G2, KD), ("norm_mix_g_2", R_GM2, KD),
        ("norm_mlp_g_2", R_GF2, KD), ("ada_b_2", R_ADAB, 6 * KD), ("c_2", R_C, KD), ("q_norm", R_Q, 2),
        ("kv_norm", R_KV, 1), ("hgrn_lb_logits_2", R_LB, 4), ("gla_gate_b_2", R_GB, 2)]
C_LR = 3 * 512 + 5 * 256 + 2 * 128 + 2 * 256

LEVELS = 9
HEAD_ORDER = (0, 1, 2, 3, 4, 5, 6, 7)


def head_place(hh):
    if hh < DH:
        return (0, 2, 1, 3)[hh], 0, hh // 2, 64 * (hh % 2), 64
    return hh - DH, 1, 2, 32 * (hh - DH), 32


def build(nc, a, out):
    with ExitStack() as ctx:
        top = [(nc.sbuf_base + 63) // 64 * 64]

        def at(name, shape, dt, offset):
            return nc.alloc_sbuf_tensor_at(name, shape, dt, offset=offset)

        def size(shape, dt):
            return int(np.prod(shape[1:])) * {F32: 4, F32R: 4, I32: 4, U8: 1}[dt]

        def sb(name, shape, dt=F32):
            t = at(name, shape, dt, top[0])
            top[0] += (size(shape, dt) + 31) // 32 * 32
            return t

        raw = sb("raw", [P, RAW, UC])
        w_hi = sb("w_hi", [P, SPLIT, UC], F32R)
        w_lo = sb("w_lo", [P, SPLIT, UC], F32R)
        x = sb("x_res", [P, M, D])
        xT_hi = sb("xT_hi", [P, KD, S], F32R)
        xT_lo = sb("xT_lo", [P, KD, S], F32R)
        ident = sb("ident", [P, P])
        ones = sb("ones", [P, P])
        norm_row = sb("norm_row", [P, D])
        gt_row = sb("gt_row", [P, 2, D])
        chunk_at = top[0]
        chunk = sb("chunk", [P, 2, M, 512])
        xn = at("xn", [P, M, D], F32, chunk_at)
        prob = at("prob", [P, 2, M, S], F32, chunk_at)
        probT = at("probT", [P, 2, M, S], F32, chunk_at + 4096)
        dmap = at("dmap", [P, 2, M, S], F32, chunk_at)
        dmapT = at("dmapT", [P, M, S], F32, chunk_at + 4096)
        dist = sb("dist", [P, M, S])
        masks = sb("masks", [P, 7, P], U8)
        trig = sb("trig", [P, 2, M, 48])
        trig_r = sb("trig_r", [P, 2, M, 32])
        rows = sb("rows", [NROW, P])
        pos_i = sb("pos_i", [P, P], I32)
        cols = sb("cols", [P, NROW])
        cond = sb("cond", [P, KD])
        modc = sb("modc", [P, NMOD, KD])
        scale_m = sb("scale_m", [P, KD])
        scale_f = sb("scale_f", [P, KD])
        lgd = sb("lgd", [P, 2, H])
        lgt = sb("lgt", [P, 2, H])
        gate2 = sb("gate2", [2 * LR, 2, P])
        lrT = sb("lrT", [2 * LR, S])
        lb = sb("lb", [P, 2, 2])
        lb1 = sb("lb1", [P, 2, 2])
        lbt = sb("lbt", [P, 2, 2])
        lamp = sb("lamp", [P, 4, 64])
        lamt = sb("lamt", [P, 2, 64])
        lams = sb("lams", [P, 4])
        headg = sb("headg", [P, 2, 64])
        subg = sb("subg", [P, P])
        eps = sb("eps", [P, 1])
        one = sb("one", [P, 1])
        ss = sb("ss", [P, M])
        rms = sb("rms", [P, M])
        rstd = sb("rstd", [P, M])
        cs = sb("cs", [P, M, 2])
        crms = sb("crms", [P, M, 2])
        crstd = sb("crstd", [P, M, 2])
        mx = sb("mx", [P, 2, M])
        rowsum = sb("rowsum", [P, M, H])
        rinv = sb("rinv", [P, M, H])
        gsum = sb("gsum", [P, M, H])
        gvar = sb("gvar", [P, M, H])
        grms = sb("grms", [P, M, H])
        grstd = sb("grstd", [P, M, H])
        dl = sb("dl", [P, 2, M])
        dr = sb("dr", [P, 2, M])
        region = (top[0] + 63) // 64 * 64
        KB = 1024

        def place(name, shape, kb, dt=F32):
            o = region + int(kb * KB)
            assert o + size(shape, dt) <= nc.sbuf_usable_end, (name, o + size(shape, dt) - nc.sbuf_usable_end)
            return at(name, shape, dt, o)

        fT_hi = place("fT_hi", [P, KF, S], 0, F32R)
        fT_lo = place("fT_lo", [P, KF, S], 22, F32R)
        acc = place("acc", [P, NMOD * D], 44)
        ada_raw = place("ada_raw", [P, 2, 1536], 68)
        rqk = place("rqk", [P, 2, M, 512], 0)
        kT = place("kT", [QK, H, S], 0)
        qf = place("qf", [P, M, H * QK], 8)
        mix_a = place("mix_a", [P, M, 512], 8)
        kf = place("kf", [P, M, H * QK], 14)
        v1 = place("v1", [P, M, H * VD], 20)
        rv = place("rv", [P, M, H * HD], 24)
        sgr = place("sgr", [P, M, H * HD], 28)
        mix_r = place("mix_r", [P, M, 512], 32)
        rqkT = place("rqkT", [P, 2, 4, S], 36)
        qT = place("qT", [QK, H, S], 36)
        p0 = place("p0", [P, M, C0], 68)
        decay = place("decay", [P, 2, 384], 71.5)
        cT_hi = place("cT_hi", [P, 3, S], 74.5, F32R)
        cT_lo = place("cT_lo", [P, 3, S], 77.5, F32R)
        reach = place("reach", [P, 2, 384], 80.5)
        rpT = place("rpT", [P, 2, 2, S], 83.5)
        tmp_r = place("tmp_r", [P, 2, M, S], 83.5)
        inv = place("inv", [P, 48], 0.25)
        ang = place("ang", [P, 2, M, 48], 1)
        turns = place("turns", [P, 2, M, 48], 2)
        nturn = place("nturn", [P, 2, M, 48], 3)
        idx_i = place("idx_i", [P, 2, P], 4, I32)
        idx_x = place("idx_x", [P, P], 5, I32)
        rel = place("rel", [P, 384], 6)
        dist_r = place("dist_r", [P, M, S], 8)
        gates = place("gates", [P, M, 3 * D], 0)
        aqT = place("aqT", [P, DH, S], 24)
        akT = place("akT", [P, DH, S], 28)
        near = place("near", [P, 4, 512], 24)
        av = place("av", [P, M, 512], 32)
        zz = place("zz", [P, 2, 3, S], 36)
        xx = place("xx", [P, 2, 3, S], 36)
        ee = place("ee", [P, 2, 3, S], 42)
        eqk = place("eqk", [P, 2, 3, S], 42)
        far = place("far", [P, 4, 512], 36)
        ll = place("ll", [P, 2, 3, S], 48)
        qt = place("qt", [P, 3, S], 54)
        kk = place("kk", [P, 2, 3, S], 57)
        v2 = place("v2", [P, M, 512], 63)
        og = place("og", [P, M, 512], 67)
        qkh = place("qkh", [P, 2, 2, 3, S], 71)
        omix_a = place("omix_a", [P, M, 512], 83)
        omix_r = place("omix_r", [P, M, 512], 71)
        biased = place("biased", [P, 2, S], 83)
        part = place("part", [P, M, D], 24)
        hT_hi = place("hT_hi", [P, KF2, S], 0, F32R)
        hT_lo = place("hT_lo", [P, KF2, S], 32, F32R)
        part2 = place("part2", [P, M, D], 64)

        pj = ctx.enter_context(nc.psum_tensor("pj", [P, 4, 512], F32))
        aux = ctx.enter_context(nc.psum_tensor("aux", [P, 4, 512], F32))

        named = {}

        def sig(name):
            if name not in named:
                named[name] = ctx.enter_context(nc.semaphore(name))
            return named[name]

        landed = [sig(f"landed{i}") for i in range(RAW)]
        hi_ready = sig("hi_ready")
        lo_ready = sig("lo_ready")
        unit_done = sig("unit_done")

        def width(c):
            return {U_IN: 4 * C0, U_IN + 1: 4 * C0, U_UQ: 2 * H * QK, U_UKV: D, U_LR: KD * P}.get(c, UC)

        def slot(tensor, c, blocks, n):
            return tensor[:, c % tensor.shape[1], 0:blocks * n].rearrange("p (k n) -> p k n", k=blocks)

        def blocks_of(w):
            return w.rearrange("l (k p) n -> p (l k) n", p=P)

        w_gate = [blocks_of(a["ffn1_w_gate"]), blocks_of(a["ffn2_w_gate"])]
        w_up = [blocks_of(a["ffn1_w_up"]), blocks_of(a["ffn2_w_up"])]
        w_down = [blocks_of(a["ffn1_w_down"]), blocks_of(a["ffn2_w_down"])]
        w_in, w_in2 = blocks_of(a["w_in"]), blocks_of(a["w_in_2"])
        w_uq, w_ukv, w_o = blocks_of(a["w_uq"]), blocks_of(a["w_ukv"]), blocks_of(a["w_o"])
        w_ups = [blocks_of(a["w_up_a_2"]), blocks_of(a["w_up_b_2"]), blocks_of(a["w_up_c_2"])]
        w_out, w_1, w_2 = blocks_of(a["w_out_2"]), blocks_of(a["mlp_w1_2"]), blocks_of(a["mlp_w2_2"])
        w_ada = blocks_of(a["ada_w_2"])

        block = ctx.enter_context(nc.Block())

        @block.sync
        def _(sp):
            def load(c, pieces, i=0):
                if c >= RAW or not isinstance(i, int):
                    sp.wait_ge(lo_ready, c + 4 * i - RAW + 1)
                for dst, src in pieces:
                    sp.dma_start(dst, src).then_inc(landed[c % RAW], 16)

            def kind_a(c, w, k0, col, n=512):
                s = slot(raw, c, 4, n)
                return [(s[:, j:j + 2, :], w[:, k0 + j:k0 + j + 2, bass.ds(col, n)]) for j in (0, 2)]

            def kind_b(c, w, k0, n=D):
                s = slot(raw, c, 2, n)
                return [(s[:, j, :], w[:, k0 + j, 0:n]) for j in (0, 1)]

            def ada(k, q, i=0):
                n = 4 * k + q
                sp.wait_ge(sig("ada_free"), n + 4 * i + 1)
                sp.dma_start(ada_raw[:, q % 2, :], w_ada[:, k + i, q * 1536:(q + 1) * 1536])\
                    .then_inc(sig(f"ada_landed{q % 2}"), 16)

            def ffn(f, u0):
                def chunk_loads(i, with_ada):
                    for w, c in ((w_gate[f], u0), (w_up[f], u0 + 2)):
                        for half in range(2):
                            load(c + half, kind_a(c + half, w, 4 * half, 512 * i), i)
                            if with_ada:
                                ada(4 * f - 1, c + half - u0, i)

                chunk_loads(0, False)
                with sp.Fori(1, NFULL) as i:
                    chunk_loads(i, True)
                for half in range(2):
                    c = u0 + 4 * NFULL + half
                    s = slot(raw, c, 4, 512)
                    load(c, [(s[:, :, 256 * n:256 * n + 256], w[f][:, 4 * half:4 * half + 4, 512 * NFULL:FF])
                             for n, w in enumerate((w_gate, w_up))])
                for d in range(KF // 2):
                    c = u0 + 4 * NFULL + 2 + d
                    load(c, kind_b(c, w_down[f], 2 * d))

            sp.dma_start(x[:, :, :], a["x"].rearrange("b (m p) d -> p (b m) d", p=P)).then_inc(sig("x_in"), 16)

            def row_load(name, r, n):
                v = a[name]
                axes = " ".join(f"d{i}" for i in range(len(v.shape)))
                flat = v.rearrange(f"{axes} -> ({axes})").rearrange("(r p) -> r p", p=P)
                sp.dma_start(rows[r:r + n, :], flat).then_inc(sig("rows_in"), 16)

            for name, r, n in ROWS:
                row_load(name, r, n)
            sp.dma_start(pos_i[R_POS:R_POS + M, :], a["positions"].rearrange("b (m p) -> (b m) p", p=P))\
                .then_inc(sig("pos_in"), 16)

            def spread(dst, src):
                sp.dma_start(dst, src.partition_broadcast(P)).then_inc(sig("spread_in"), 16)

            spread(inv[:, :], a["inv_freq"][0, :])
            spread(lgd[:, 0, :], a["ret_decay_fwd"][0, :])
            spread(lgd[:, 1, :], a["ret_decay_bwd"][0, :])
            spread(lamp[:, :, :].rearrange("p a b -> p (a b)"), a["diff_lambda_2"].rearrange("l a b -> (l a b)"))
            spread(headg[:, 0, :], a["hgrn_norm_g_2"][0, :])
            spread(headg[:, 1, :], a["gla_norm_g_2"][0, :])
            spread(subg[:, :], a["diff_subln_g_2"][0, :])
            spread(norm_row[:, :], a["final_norm"])
            spread(gt_row[:, 0, :], a["ada_b_2"][0, 2 * D:3 * D])
            spread(gt_row[:, 1, :], a["ada_b_2"][0, 5 * D:6 * D])
            sp.wait_ge(sig("gate2_zero"), 1)
            for d in range(2):
                sp.dma_start(gate2[LR * d:LR * d + LR, d, :], a["gla_gate_w2_2"][0, d, :, :])\
                    .then_inc(sig("gate2_in"), 16)

            ffn(0, U_F1)
            for j in range(5):
                n, col = (C0, 0) if j == 0 else (512, C0 + 512 * (j - 1))
                for half in range(2):
                    c = U_IN + 2 * j + half
                    load(c, kind_a(c, w_in, 4 * half, col, n))
            load(U_UQ, kind_b(U_UQ, w_uq, 0, H * QK))
            s = raw[:, U_UKV % RAW, :]
            load(U_UKV, [(s[:, n:n + 512], w_ukv[:, 0, n:n + 512]) for n in (0, 512)])
            for d in range(4):
                load(U_O + d, kind_b(U_O + d, w_o, 2 * d))
            ffn(1, U_F2)
            for j in range(7):
                for half in range(2):
                    c = U_IN2 + 2 * j + half
                    load(c, kind_a(c, w_in2, 4 * half, 512 * j))
            s = slot(raw, U_LR, KD, P)
            load(U_LR, [(s[:, k:k + 4, :], w_in2[:, k:k + 4, C_LR:C_LR + P]) for k in (0, 4)])
            for j in range(6):
                for half in range(2):
                    c = U_GATES + 2 * j + half
                    load(c, kind_a(c, w_in2, 4 * half, C_LR + 2 * LR + 512 * j))
            for c, n, k in ((U_UP, 0, 0), (U_UP + 1, 0, 2), (U_UP + 2, 1, 0), (U_UP + 3, 2, 0)):
                load(c, kind_b(c, w_ups[n], k))
            for d in range(4):
                load(U_OUT + d, kind_b(U_OUT + d, w_out, 2 * d))
            sp.wait_ge(sig("normed"), 1)
            sp.dma_start(norm_row[:, :], a["final_norm_g_2"].partition_broadcast(P)).then_inc(sig("row2_in"), 16)
            with sp.Fori(0, KF2 // 8) as i:
                for job in range(2):
                    for half in range(2):
                        c = U_W1 + 2 * job + half
                        load(c, kind_a(c, w_1, 4 * half, 1024 * i + 512 * job), i)
            for d in range(KF2 // 2):
                load(U_W2 + d, kind_b(U_W2 + d, w_2, 2 * d))
            sp.wait_ge(sig("y_ready"), 1)
            sp.dma_start(out.rearrange("b (m p) d -> p (b m) d", p=P), x[:, :, :]).then_inc(sig("out_done"), 16)
            sp.wait_ge(sig("out_done"), 16)

        @block.tensor
        def _(pe):
            def three(dst, l_hi, l_lo, r_hi, r_lo, first, last):
                pe.matmul(dst, l_hi, r_hi, start=first, stop=False)
                pe.matmul(dst, l_hi, r_lo, start=False, stop=False)
                return pe.matmul(dst, l_lo, r_hi, start=False, stop=last)

            def unit_a(c, pair, k0, first, last, n=512, i=0):
                pe.wait_ge(lo_ready, c + 4 * i + 1)
                hi, lo = slot(w_hi, c, 4, n), slot(w_lo, c, 4, n)
                for m in range(M):
                    for j in range(4):
                        k = k0 + j
                        mm = three(pj[:, 2 * pair + m, 0:n], xT_hi[:, k, m * P:(m + 1) * P],
                                   xT_lo[:, k, m * P:(m + 1) * P], hi[:, j, :], lo[:, j, :],
                                   first and j == 0, last and j == 3)
                mm.then_inc(unit_done, 1)

            def job(c, pair, n=512):
                unit_a(c, pair, 0, True, False, n)
                unit_a(c + 1, pair, 4, False, True, n)

            def unit_b(c, hi_T, lo_T, k0, first, last, free=None, nk=2, n=512):
                pe.wait_ge(lo_ready, c + 1)
                hi, lo = slot(w_hi, c, nk, 2 * n), slot(w_lo, c, nk, 2 * n)
                for h in (1, 0):
                    if free:
                        free(h)
                    for m in range(M):
                        for j in range(nk):
                            k = k0 + j
                            mm = three(pj[:, 2 * h + m, 0:n], hi_T[:, k, m * P:(m + 1) * P],
                                       lo_T[:, k, m * P:(m + 1) * P], hi[:, j, h * n:(h + 1) * n],
                                       lo[:, j, h * n:(h + 1) * n], first and j == 0, last and j == nk - 1)
                    if h == 1 and last:
                        mm.then_inc(sig("half1"), 1)
                mm.then_inc(unit_done, 1)

            def turn(src, banks=range(4)):
                for b in banks:
                    for kk_ in range(2):
                        for m in range(M):
                            mm = pe.transpose(aux[:, b, kk_ * S + m * P:kk_ * S + (m + 1) * P],
                                              src(2 * b + kk_, m), ident[:, :])
                    mm.then_inc(sig("turned"), 1)

            def ffn(f, u0):
                n = (NFULL + 1) * f

                def hidden_turn(blocks, i):
                    pe.wait_ge(sig("h_ready"), n + i)
                    for j in range(blocks):
                        for m in range(M):
                            mm = pe.transpose(aux[:, j // 2, (j % 2) * S + m * P:(j % 2) * S + (m + 1) * P],
                                              chunk[:, 1, m, j * P:(j + 1) * P], ident[:, :])
                    mm.then_inc(sig("h_turned"), 1)

                def chunk_of(i, first):
                    if not first:
                        pe.wait_ge(sig("silu_done"), n + i)
                    unit_a(u0, 0, 0, True, False, i=i)
                    if not first:
                        hidden_turn(4, i)
                    unit_a(u0 + 1, 0, 4, False, True, i=i)
                    unit_a(u0 + 2, 1, 0, True, False, i=i)
                    unit_a(u0 + 3, 1, 4, False, True, i=i)

                chunk_of(0, True)
                with pe.Fori(1, NFULL) as i:
                    chunk_of(i, False)
                t = u0 + 4 * NFULL
                pe.wait_ge(sig("silu_done"), n + NFULL)
                unit_a(t, 0, 0, True, False)
                hidden_turn(4, NFULL)
                unit_a(t + 1, 0, 4, False, True)

                def read_out(h):
                    pe.wait_ge(sig("h_ready"), n + NFULL + (h == 0))

                for d in range(KF // 2):
                    if d == 1:
                        hidden_turn(2, NFULL + 1)
                        if f == 1:
                            modulation()
                    if d == 2 * NFULL:
                        pe.wait_ge(sig("hT_lo"), n + NFULL + 1)
                    elif d == 0:
                        pe.wait_ge(sig("hT_lo"), n + NFULL)
                    unit_b(t + 2 + d, fT_hi, fT_lo, 2 * d, d == 0, d == KF // 2 - 1, read_out if d == 0 else None)

            def modulation():
                pe.wait_ge(sig("ada_free"), 2 + 4 * KD)
                for t in range(NMOD * KD):
                    if t // KD in (0, 1, 3, 4):
                        mm = pe.matmul(aux[:, 2, t:t + 1], acc[:, t * P:(t + 1) * P], ones[:, 0:1],
                                       start=True, stop=True)
                mm.then_inc(sig("mod_sum"), 1)
                for n in range(4):
                    if n:
                        pe.wait_ge(sig("gt_done"), n)
                    o = (2 if n < 2 else 5) * D + (n % 2) * 512
                    pe.matmul(aux[:, 3, :], ones[:, :], acc[:, o:o + 512], start=True, stop=True)\
                        .then_inc(sig("gt_sum"), 1)

            pe.wait_ge(sig("ident_ready"), 2)
            pe.wait_ge(sig("consts"), 1)
            pe.wait_ge(sig("rows_in"), 16 * len(ROWS))
            pe.wait_ge(sig("pos_row"), 1)
            pe.transpose(aux[:, 3, 0:NROW], rows[:, :], ident[0:NROW, 0:NROW]).then_inc(sig("cols_turned"), 1)

            pe.wait_ge(sig("x_in"), 16)
            pe.wait_ge(sig("cols_ready"), 1)
            turn(lambda k, m: x[:, m, k * P:(k + 1) * P])
            pe.wait_ge(sig("xT_lo"), KD)
            ffn(0, U_F1)

            pe.wait_ge(sig("x_ready"), 1)
            turn(lambda k, m: x[:, m, k * P:(k + 1) * P], (2, 3))
            pe.wait_ge(sig("x_ready"), 2)
            turn(lambda k, m: x[:, m, k * P:(k + 1) * P], (0, 1))
            pe.wait_ge(sig("xT_lo"), 2 * KD)
            job(U_IN, 0, C0)
            job(U_IN + 2, 1)
            pe.wait_ge(sig("p0_ready"), 1)
            for k in range(3):
                for m in range(M):
                    mm = pe.transpose(aux[:, k // 2, (k % 2) * S + m * P:(k % 2) * S + (m + 1) * P],
                                      p0[:, m, k * P:(k + 1) * P], ident[:, :])
            mm.then_inc(sig("c_turned"), 1)
            job(U_IN + 4, 0)
            pe.wait_ge(sig("rot"), 1)
            job(U_IN + 6, 1)
            pe.wait_ge(sig("cT_lo"), 3)

            def ret_turn(n):
                for g in range(4):
                    for m in range(M):
                        mm = pe.transpose(aux[:, 2 * n + g // 2, (g % 2) * S + m * P:(g % 2) * S + (m + 1) * P],
                                          rqk[:, n, m, g * P:(g + 1) * P], ident[:, :])
                mm.then_inc(sig("ret_turned"), 1)

            ret_turn(0)
            pe.wait_ge(sig("rot"), 2)
            job(U_IN + 8, 0)
            ret_turn(1)

            def pairs_read(h):
                pe.wait_ge(sig("rv_ready") if h else sig("sgr_ready"), 1)

            unit_b(U_UQ, cT_hi, cT_lo, 0, True, True, pairs_read, n=384)
            pe.wait_ge(sig("qf_ready"), 1)
            unit_b(U_UKV, cT_hi, cT_lo, 2, True, True, nk=1)

            pe.wait_ge(sig("rqkT_q"), 1)
            pe.wait_ge(sig("rqkT_k"), 1)

            def ret_scores(h):
                if h >= 2:
                    pe.wait_ge(sig("rpT_ready"), h - 1)
                r, g = HD * (h % 2), h // 2
                for jt in range(M):
                    mm = pe.matmul(aux[:, h % 2, jt * S:(jt + 1) * S], rqkT[r:r + HD, 1, g, jt * P:(jt + 1) * P],
                                   rqkT[r:r + HD, 0, g, :], start=True, stop=True)
                mm.then_inc(sig("ret_scored"), 1)

            def ret_values(h):
                pe.wait_ge(sig("rpT_ready"), h + 1)
                if h == 0:
                    pe.wait_ge(sig("kv_ready"), 1)
                for m in range(M):
                    for jt in range(M):
                        mm = pe.matmul(pj[:, 2 + m, h * HD:(h + 1) * HD], rpT[:, h % 2, jt, m * P:(m + 1) * P],
                                       rv[:, jt, h * HD:(h + 1) * HD], start=(jt == 0), stop=(jt == 1))
                mm.then_inc(sig("ret_valued"), 1)

            for s in range(H + 1):
                if s < H:
                    ret_scores(s)
                if s >= 1:
                    ret_values(s - 1)

            def mla_turn(n, src, ready, value):
                for b in range(4):
                    if b == 0:
                        pe.wait_ge(sig(ready), value)
                    if n:
                        pe.wait_ge(sig("qT_ready"), b + 1)
                    for hh in range(2):
                        for m in range(M):
                            h = 2 * b + hh
                            mm = pe.transpose(aux[0:QK, b, hh * S + m * P:hh * S + (m + 1) * P],
                                              src[:, m, h * QK:(h + 1) * QK], ident[:, :])
                    mm.then_inc(sig("mla_turned"), 1)

            pe.wait_ge(sig("rpT_ready"), H)
            mla_turn(0, qf, "q_rot", 1)
            mla_turn(1, kf, "kf_ready", 1)

            def mla_scores(h):
                if h < 2:
                    pe.wait_ge(sig("kT_ready"), 4)
                else:
                    pe.wait_ge(sig("mla_exp"), h - 1)
                for m in range(M):
                    mm = pe.matmul(aux[:, h % 2, m * S:(m + 1) * S], qT[0:QK, h, m * P:(m + 1) * P],
                                   kT[0:QK, h, :], start=True, stop=True)
                mm.then_inc(sig("mla_scored"), 1)

            def mla_prob_turn(h):
                pe.wait_ge(sig("mla_exp"), h + 1)
                if h >= 2:
                    pe.wait_ge(sig("probT_ready"), h - 1)
                for kt in range(M):
                    for m in range(M):
                        mm = pe.transpose(aux[:, 2 + h % 2, kt * S + m * P:kt * S + (m + 1) * P],
                                          prob[:, h % 2, m, kt * P:(kt + 1) * P], ident[:, :])
                mm.then_inc(sig("prob_turned"), 1)

            def mla_values(h):
                pe.wait_ge(sig("probT_ready"), h + 1)
                for m in range(M):
                    for kt in range(M):
                        mm = pe.matmul(pj[:, m, h * VD:(h + 1) * VD], probT[:, h % 2, kt, m * P:(m + 1) * P],
                                       v1[:, kt, h * VD:(h + 1) * VD], start=(kt == 0), stop=(kt == 1))
                mm.then_inc(sig("mla_valued"), 1)

            for s in range(H + 2):
                if s < H:
                    mla_scores(s)
                if 1 <= s <= H:
                    mla_prob_turn(s - 1)
                if s >= 2:
                    mla_values(s - 2)

            pe.wait_ge(sig("mix_ready"), 2)
            turn(lambda k, m: (mix_a if k < 4 else mix_r)[:, m, (k % 4) * P:(k % 4 + 1) * P])
            pe.wait_ge(sig("xT_lo"), 3 * KD)
            for d in range(4):
                unit_b(U_O + d, xT_hi, xT_lo, 2 * d, d == 0, d == 3)

            pe.wait_ge(sig("x_ready"), 3)
            turn(lambda k, m: x[:, m, k * P:(k + 1) * P], (2, 3))
            pe.wait_ge(sig("x_ready"), 4)
            turn(lambda k, m: x[:, m, k * P:(k + 1) * P], (0, 1))
            pe.wait_ge(sig("xT_lo"), 4 * KD)
            ffn(1, U_F2)

            pe.wait_ge(sig("xn_ready"), 1)
            turn(lambda k, m: xn[:, m, k * P:(k + 1) * P])
            pe.wait_ge(sig("xT_lo"), 5 * KD)

            def blocks_turn(buf, col0, n, banks, value):
                pe.wait_ge(sig("staged"), value)
                for j in range(n):
                    for m in range(M):
                        mm = pe.transpose(aux[:, banks[j // 2], (j % 2) * S + m * P:(j % 2) * S + (m + 1) * P],
                                          chunk[:, buf, m, col0 + j * P:col0 + (j + 1) * P], ident[:, :])
                mm.then_inc(sig("blocks_turned"), 1)

            c = U_IN2
            job(c, 0)
            job(c + 2, 1)
            blocks_turn(0, 0, 4, (0, 1), 1)
            job(c + 4, 0)
            blocks_turn(1, 0, 4, (2, 3), 2)
            job(c + 6, 1)
            pe.wait_ge(sig("staged"), 3)
            job(c + 8, 0)
            pe.wait_ge(sig("turned_read"), 1)
            blocks_turn(0, 0, 4, (0, 1), 4)
            job(c + 10, 1)
            pe.wait_ge(sig("turned_read"), 2)
            blocks_turn(1, 0, 2, (2,), 5)
            job(c + 12, 0)
            blocks_turn(0, 0, 2, (3,), 6)
            pe.wait_ge(lo_ready, U_LR + 1)
            pe.wait_ge(sig("turned_read"), 3)
            hi, lo = slot(w_hi, U_LR, KD, P), slot(w_lo, U_LR, KD, P)
            for k in range(KD):
                mm = three(aux[:, 0, 0:S], hi[:, k, :], lo[:, k, :], xT_hi[:, k, :], xT_lo[:, k, :],
                           k == 0, k == KD - 1)
            mm.then_inc(unit_done, 1)
            pe.wait_ge(sig("lrT_ready"), 1)
            pe.wait_ge(sig("gate2_in"), 32)
            for d in range(2):
                mm = pe.matmul(aux[:, 1, d * S:(d + 1) * S], gate2[0:2 * LR, d, :], lrT[0:2 * LR, :],
                               start=True, stop=True)
            mm.then_inc(sig("gla_z"), 1)

            def diff_scores(h):
                if h == 0:
                    pe.wait_ge(sig("gla_z_read"), 1)
                    pe.wait_ge(sig("turned_read"), 5)
                else:
                    pe.wait_ge(sig("biased"), h)
                for j in range(2):
                    for m in range(M):
                        mm = pe.matmul(aux[:, j, m * S:(m + 1) * S], aqT[64 * j:64 * j + 64, h, m * P:(m + 1) * P],
                                       akT[64 * j:64 * j + 64, h, :], start=True, stop=True)
                mm.then_inc(sig("diff_scored"), 1)

            def diff_turn(h):
                pe.wait_ge(sig("diff_w"), h + 1)
                if h:
                    pe.wait_ge(sig("dmapT_ready"), h)
                for kt in range(M):
                    for m in range(M):
                        mm = pe.transpose(aux[:, 2, kt * S + m * P:kt * S + (m + 1) * P],
                                          dmap[:, 0, m, kt * P:(kt + 1) * P], ident[:, :])
                mm.then_inc(sig("diff_turned"), 1)

            def diff_values(h):
                pe.wait_ge(sig("dmapT_ready"), h + 1)
                if h:
                    pe.wait_ge(sig("oa_copied"), h)
                for m in range(M):
                    for kt in range(M):
                        mm = pe.matmul(aux[:, 3, m * P:(m + 1) * P], dmapT[:, kt, m * P:(m + 1) * P],
                                       av[:, kt, h * P:(h + 1) * P], start=(kt == 0), stop=(kt == 1))
                mm.then_inc(sig("diff_valued"), 1)

            def level_scores(n):
                pe.wait_ge(sig("qk_ready"), n + 1)
                if n == 0:
                    pe.wait_ge(sig("oa_copied"), DH)
                else:
                    pe.wait_ge(sig("level_read"), n)
                for hh in HEAD_ORDER:
                    bank, kind, g, r, kd = head_place(hh)
                    for m in range(M):
                        km = 1 - m if n == LEVELS - 1 else m
                        col = kind * S + m * P
                        mm = pe.matmul(aux[:, bank, col:col + P], qkh[r:r + kd, n % 2, 1, g, km * P:(km + 1) * P],
                                       qkh[r:r + kd, n % 2, 0, g, m * P:(m + 1) * P], start=True, stop=True)
                mm.then_inc(sig("level_scored"), 1)

            def gate_unit(s):
                if s % 2 == 0:
                    j = s // 2
                    pe.wait_ge(sig("staged"), 7 if j == 0 else 6)
                    if j >= 2:
                        pe.wait_ge(sig("gates_raw"), j - 1)
                unit_a(U_GATES + s, (s // 2) % 2, 4 * (s % 2), s % 2 == 0, s % 2 == 1)

            for s in range(12):
                gate_unit(s)
                if s < DH:
                    diff_scores(s)
                if 1 <= s <= DH:
                    diff_turn(s - 1)
                if 2 <= s <= DH + 1:
                    diff_values(s - 2)
                if s >= 6:
                    level_scores(s - 6)
            for n in range(6, LEVELS):
                level_scores(n)
            pe.wait_ge(sig("far_ready"), 1)
            for hh in HEAD_ORDER:
                bank, kind, g, r, kd = head_place(hh)
                for m in range(M):
                    col = kind * S + m * P
                    dst = aux[:, m, hh * HD:(hh + 1) * HD]
                    pe.matmul(dst, near[:, bank, col:col + P], v2[:, m, hh * HD:(hh + 1) * HD],
                              start=True, stop=False)
                    mm = pe.matmul(dst, far[:, bank, col:col + P], v2[:, 1 - m, hh * HD:(hh + 1) * HD],
                                   start=False, stop=True)
            mm.then_inc(sig("rec_valued"), 1)

            pe.wait_ge(sig("omix_ready"), 2)
            turn(lambda k, m: (omix_a if k < 4 else omix_r)[:, m, (k % 4) * P:(k % 4 + 1) * P])
            pe.wait_ge(sig("xT_lo"), 6 * KD)
            pe.wait_ge(sig("gates_raw"), 6)

            def branch_free(n):
                def free(h):
                    if n:
                        pe.wait_ge(sig("branch_read"), 2 * n - 1 if h else 2 * n)
                return free

            unit_b(U_UP, xT_hi, xT_lo, 0, True, False)
            unit_b(U_UP + 1, xT_hi, xT_lo, 2, False, True)
            unit_b(U_UP + 2, xT_hi, xT_lo, 4, True, True, branch_free(1))
            unit_b(U_UP + 3, xT_hi, xT_lo, 6, True, True, branch_free(2))
            pe.wait_ge(sig("merged"), 2)
            turn(lambda k, m: xn[:, m, k * P:(k + 1) * P])
            pe.wait_ge(sig("xT_lo"), 7 * KD)
            for d in range(4):
                unit_b(U_OUT + d, xT_hi, xT_lo, 2 * d, d == 0, d == 3)

            pe.wait_ge(sig("xn_ready"), 2)
            turn(lambda k, m: xn[:, m, k * P:(k + 1) * P])
            pe.wait_ge(sig("xT_lo"), 8 * KD)

            def mlp_turn(par, i, n):
                pe.wait_ge(sig("sq_ready"), n + 2 * i)
                for j in range(4):
                    for m in range(M):
                        mm = pe.transpose(aux[:, 2 * par + j // 2, (j % 2) * S + m * P:(j % 2) * S + (m + 1) * P],
                                          chunk[:, par, m, j * P:(j + 1) * P], ident[:, :])
                mm.then_inc(sig("sq_turned"), 1)

            def mlp_jobs(i, first):
                for par in range(2):
                    c = U_W1 + 2 * par
                    prev = not (first and par == 0)
                    unit_a(c, par, 0, True, False, i=i)
                    if prev:
                        mlp_turn(1 - par, i, par)
                    unit_a(c + 1, par, 4, False, True, i=i)

            mlp_jobs(0, True)
            with pe.Fori(1, KF2 // 8) as i:
                mlp_jobs(i, False)
            for d in range(KF2 // 2):
                if d == 1:
                    mlp_turn(1, 0, KF2 // 4)
                if d == KF2 // 2 - 2:
                    pe.wait_ge(sig("sqT_lo"), KF2 // 4)
                elif d == 0:
                    pe.wait_ge(sig("sqT_lo"), KF2 // 4 - 1)
                unit_b(U_W2 + d, hT_hi, hT_lo, 2 * d, d == 0, d == KF2 // 2 - 1,
                       (lambda h: pe.wait_ge(sig("sq_ready"), KF2 // 4)) if d == 0 else None)

        @block.scalar
        def _(act):
            steps = [0]

            def step(ins):
                steps[0] += 1
                ins.then_inc(sig("act_step"), 1)

            def settle():
                act.wait_ge(sig("act_step"), steps[0])

            def split(c, i=0):
                act.wait_ge(landed[c % RAW], 32 * (c // RAW + 1) + 32 * i)
                if c >= SPLIT or not isinstance(i, int):
                    act.wait_ge(unit_done, c + 4 * i - SPLIT + 1)
                n = width(c)
                act.activation(w_hi[:, c % SPLIT, 0:n], raw[:, c % RAW, 0:n], ACT.Copy).then_inc(hi_ready, 1)

            def operand(t, gain=None, bias=None, order=(0, 1, 2, 3)):
                for n, b in enumerate(order):
                    act.wait_ge(sig("turned"), 4 * t + n + 1)
                    for k in (2 * b, 2 * b + 1):
                        src, dst = aux[:, b, (k % 2) * S:(k % 2 + 1) * S], xT_hi[:, k, :]
                        if bias is not None:
                            ins = act.activation(dst, src, ACT.Identity, bias=bias[:, k:k + 1], scale=gain[:, k:k + 1])
                        elif gain is not None:
                            ins = act.activation(dst, src, ACT.Copy, scale=gain[:, k:k + 1])
                        else:
                            ins = act.activation(dst, src, ACT.Copy)
                        ins.then_inc(sig("xT_hi"), 1)

            def stats(n, src):
                if n:
                    act.wait_ge(sig("rstd_ready"), n)
                for m in range(M):
                    step(act.activation(xn[:, m, :], src[:, m, :], ACT.Square, accum_out=ss[:, m:m + 1]))
                settle()
                act.activation(rms[:, :], ss[:, :], ACT.Sqrt, bias=eps[:, 0:1], scale=1.0 / D)\
                    .then_inc(sig("rms_ready"), 1)

            def ffn(f, u0, t_stats):
                n = (NFULL + 1) * f

                def silu(i, cols=512):
                    for m in range(M):
                        ins = act.activation(chunk[:, 0, m, 0:cols], pj[:, m, 0:cols], ACT.Silu,
                                             scale=rstd[:, m:m + 1])
                    ins.then_inc(sig("silu_done"), 1)

                def hidden(blocks, i):
                    act.wait_ge(sig("h_turned"), n + i)
                    start = 4 * i - 4
                    act.activation(fT_hi[:, bass.ds(start, blocks), :],
                                   aux[:, 0:2, :].rearrange("p b (k s) -> p (b k) s", k=2)[:, 0:blocks, :],
                                   ACT.Copy).then_inc(sig("hT_hi"), 1)

                split(u0 + 1)
                stats(t_stats, x)
                split(u0 + 2)
                split(u0 + 3)
                act.wait_ge(sig("rstd_ready"), t_stats + 1)
                silu(0)
                with act.Fori(1, NFULL) as i:
                    split(u0, i)
                    split(u0 + 1, i)
                    split(u0 + 2, i)
                    hidden(4, i)
                    split(u0 + 3, i)
                    act.wait_ge(sig("h_ready"), n + i)
                    silu(i)
                t = u0 + 4 * NFULL
                split(t)
                split(t + 1)
                hidden(4, NFULL)
                split(t + 2)
                act.wait_ge(unit_done, t + 2)
                act.wait_ge(sig("h_ready"), n + NFULL)
                silu(NFULL, 256)
                split(t + 3)
                hidden(2, NFULL + 1)
                for d in range(2, KF // 2):
                    split(t + 2 + d)

            split(U_F1)
            act.wait_ge(sig("consts"), 1)
            act.wait_ge(sig("cols_ready"), 1)
            act.activation(cond[:, :], cols[:, R_C:R_C + KD], ACT.Silu).then_inc(sig("cond_ready"), 1)
            operand(0, cols[:, R_G1:R_G1 + KD])
            act.wait_ge(sig("angles"), 1)
            ins = act.activation(trig[:, :, :, :].rearrange("p a m n -> p (a m n)"),
                                ang[:, :, :, :].rearrange("p a m n -> p (a m n)"), ACT.Sin)
            ins.then_inc(sig("trig_ready"), 1)
            act.wait_ge(sig("logs_in"), 1)
            step(act.activation(lgt[:, :, :], lgt[:, :, :], ACT.Exp, scale=-1.0))
            step(act.activation(lams[:, 0:2], lams[:, 0:2], ACT.Exp))
            step(act.activation(lbt[:, :, :], lbt[:, :, :], ACT.Exp))
            settle()
            act.activation(lgt[:, :, :], lgt[:, :, :], ACT.Ln, bias=one[:, 0:1]).then_inc(sig("logs_out"), 1)
            ffn(0, U_F1, 0)

            split(U_IN)
            operand(1, cols[:, R_MIX:R_MIX + KD], order=(2, 3, 0, 1))
            split(U_IN + 1)
            stats(1, x)
            split(U_IN + 2)
            split(U_IN + 3)
            act.wait_ge(sig("rstd_ready"), 2)
            for m in range(M):
                ins = act.activation(p0[:, m, :], pj[:, m, 0:C0], ACT.Copy, scale=rstd[:, m:m + 1])
            ins.then_inc(sig("p0_ready"), 1)
            act.wait_ge(sig("p0_ready"), 1)
            for m in range(M):
                step(act.activation(sgr[:, m, 0:QR], p0[:, m, 0:QR], ACT.Square, accum_out=cs[:, m, 0:1]))
                step(act.activation(sgr[:, m, QR:QR + KVR], p0[:, m, QR:QR + KVR], ACT.Square,
                                    accum_out=cs[:, m, 1:2]))
            settle()
            step(act.activation(crms[:, :, 0], cs[:, :, 0], ACT.Sqrt, bias=eps[:, 0:1], scale=1.0 / QR))
            act.activation(crms[:, :, 1], cs[:, :, 1], ACT.Sqrt, bias=eps[:, 0:1], scale=1.0 / KVR)\
                .then_inc(sig("crms_ready"), 1)
            split(U_IN + 4)
            split(U_IN + 5)
            act.wait_ge(sig("c_turned"), 1)
            for k in range(3):
                act.activation(cT_hi[:, k, :], aux[:, k // 2, (k % 2) * S:(k % 2 + 1) * S], ACT.Copy,
                               scale=cols[:, R_Q + k:R_Q + k + 1]).then_inc(sig("cT_hi"), 1)
            split(U_IN + 6)
            split(U_IN + 7)
            split(U_IN + 8)
            act.wait_ge(unit_done, U_IN + 8)
            for m in range(M):
                ins = act.activation(rv[:, m, :], pj[:, 2 + m, :], ACT.Copy, scale=rstd[:, m:m + 1])
            ins.then_inc(sig("rv_ready"), 1)
            act.wait_ge(sig("ret_turned"), 1)
            act.activation(rqkT[:, 0, :, :].rearrange("p g s -> p (g s)"),
                           aux[:, 0:2, :].rearrange("p b n -> p (b n)"), ACT.Copy).then_inc(sig("rqkT_q"), 1)
            split(U_IN + 9)
            split(U_UQ)
            split(U_UKV)
            for m in range(M):
                ins = act.activation(sgr[:, m, :], pj[:, m, :], ACT.Silu, scale=rstd[:, m:m + 1])
            ins.then_inc(sig("sgr_ready"), 1)
            split(U_O)
            act.wait_ge(sig("crstd_ready"), 1)
            for m in range(M):
                ins = act.activation(qf[:, m, :].rearrange("p (h n) -> p h n", h=2), pj[:, m:4:2, 0:384], ACT.Copy,
                                    scale=crstd[:, m, 0:1])
            ins.then_inc(sig("qf_ready"), 1)
            split(U_O + 1)
            for m in range(M):
                src = pj[:, m:4:2, :].rearrange("p a (h n) -> p a h n", n=P)
                kdst = kf[:, m, :].rearrange("p (a h n) -> p a h n", a=2, n=QK)[:, :, :, 0:NOPE]
                vdst = v1[:, m, :].rearrange("p (a h n) -> p a h n", a=2, n=VD)
                ins = act.activation(kdst, src[:, :, :, 0:NOPE], ACT.Copy, scale=crstd[:, m, 1:2])
                ins = act.activation(vdst, src[:, :, :, NOPE:P], ACT.Copy, scale=crstd[:, m, 1:2])
            ins.then_inc(sig("kv_ready"), 1)
            for h in range(H):
                act.wait_ge(sig("decay_log"), h + 1)
                act.activation(decay[:, h % 2, :], decay[:, h % 2, :], ACT.Exp).then_inc(sig("decay_ready"), 1)
            for b in range(4):
                act.wait_ge(sig("mla_turned"), b + 1)
                act.activation(qT[0:QK, 2 * b:2 * b + 2, :].rearrange("p h s -> p (h s)"), aux[0:QK, b, :], ACT.Copy)\
                    .then_inc(sig("qT_ready"), 1)
            act.wait_ge(sig("centred"), 1)
            act.activation(tmp_r[:, :, :, :].rearrange("p a m s -> p (a m s)"),
                           mix_r[:, :, :].rearrange("p m n -> p (m n)"), ACT.Square).then_inc(sig("gn_square"), 1)
            act.wait_ge(sig("gvar_ready"), 1)
            act.activation(grms[:, :, :], gvar[:, :, :], ACT.Sqrt, bias=eps[:, 0:1], scale=1.0 / HD)\
                .then_inc(sig("grms_ready"), 1)
            for h in range(H):
                act.wait_ge(sig("mla_max"), h + 1)
                if h >= 2:
                    act.wait_ge(sig("prob_turned"), h - 1)
                for m in range(M):
                    ins = act.activation(prob[:, h % 2, m, :], aux[:, h % 2, m * S:(m + 1) * S], ACT.Exp,
                                         bias=mx[:, h % 2, m:m + 1], accum_out=rowsum[:, m, h:h + 1])
                ins.then_inc(sig("mla_exp"), 1)
            operand(2)
            split(U_O + 2)
            split(U_O + 3)

            split(U_F2)
            operand(3, cols[:, R_G2:R_G2 + KD], order=(2, 3, 0, 1))
            ffn(1, U_F2, 2)

            split(U_IN2)
            act.wait_ge(sig("x_ready"), 6)
            stats(3, x)
            act.wait_ge(sig("normed"), 1)
            stats(4, x)
            operand(4, scale_m[:, :], modc[:, 0, :])
            split(U_IN2 + 1)

            def stage(dst, pair, c0, c1, func=ACT.Copy):
                return act.activation(dst, pj[:, 2 * pair:2 * pair + 2, c0:c1], func)

            c = U_IN2
            split(c + 2)
            split(c + 3)
            ins = stage(chunk[:, 0, :, :], 0, 0, 512)
            ins.then_inc(sig("staged"), 1)
            split(c + 4)
            split(c + 5)
            ins = stage(chunk[:, 1, :, :], 1, 0, 512)
            ins.then_inc(sig("staged"), 1)
            split(c + 6)
            split(c + 7)
            ins = stage(av[:, :, :], 0, 0, 512)
            ins.then_inc(sig("staged"), 1)
            split(c + 8)
            split(c + 9)
            act.wait_ge(sig("blocks_turned"), 1)
            ins = stage(chunk[:, 0, :, :], 1, 0, 512)
            ins.then_inc(sig("staged"), 1)
            split(c + 10)
            split(c + 11)
            act.wait_ge(sig("blocks_turned"), 2)
            ins = stage(chunk[:, 1, :, 0:S], 0, 0, S)
            ins = stage(v2[:, :, 0:S], 0, S, 2 * S)
            ins.then_inc(sig("staged"), 1)
            act.wait_ge(sig("blocks_turned"), 3)
            act.activation(qt[:, 0:2, :].rearrange("p g s -> p (g s)"), aux[:, 0, :], ACT.Silu)\
                .then_inc(sig("q_silu"), 1)
            split(c + 12)
            split(c + 13)
            ins = stage(og[:, :, 0:S], 1, 0, S, ACT.Silu)
            ins = stage(chunk[:, 0, :, 0:S], 1, S, 2 * S)
            ins.then_inc(sig("staged"), 1)
            split(U_LR)
            split(U_GATES)
            ins = stage(v2[:, :, S:2 * S], 0, 0, S)
            ins = stage(og[:, :, S:2 * S], 0, S, 2 * S, ACT.Silu)
            ins.then_inc(sig("staged"), 1)
            split(U_GATES + 1)
            act.activation(lrT[:, :], aux[0:2 * LR, 0, 0:S], ACT.Copy).then_inc(sig("lrT_ready"), 1)
            act.wait_ge(sig("gla_z"), 1)
            for d in range(2):
                ins = act.activation(zz[:, d, 2, :], aux[:, 1, d * S:(d + 1) * S], ACT.Identity,
                                    bias=cols[:, R_GB + d:R_GB + d + 1])
            ins.then_inc(sig("gla_z_read"), 1)

            def flat(t):
                return t.rearrange("p d g s -> p (d g s)")

            def diff_exp(h):
                act.wait_ge(sig("diff_max"), h + 1)
                for j in range(2):
                    for m in range(M):
                        ins = act.activation(dmap[:, j, m, :], dmap[:, j, m, :], ACT.Exp, bias=dl[:, j, m:m + 1],
                                            accum_out=dr[:, j, m:m + 1])
                ins.then_inc(sig("diff_exp"), 1)

            def diff_copies(h):
                act.wait_ge(sig("diff_turned"), h + 1)
                if h:
                    act.wait_ge(sig("diff_valued"), h)
                act.activation(dmapT[:, :, :].rearrange("p k s -> p (k s)"), aux[:, 2, :], ACT.Copy)\
                    .then_inc(sig("dmapT_ready"), 1)

            def diff_out(h):
                act.wait_ge(sig("diff_valued"), h + 1)
                act.activation(omix_a[:, :, h * P:(h + 1) * P], aux[:, 3, 0:S].rearrange("p (m n) -> p m n", m=2),
                               ACT.Copy).then_inc(sig("oa_copied"), 1)

            def gates_copy(j):
                act.activation(gates[:, :, j * 512:(j + 1) * 512], pj[:, 2 * (j % 2):2 * (j % 2) + 2, :], ACT.Copy)\
                    .then_inc(sig("gates_raw"), 1)

            def halves(t, lvl):
                v = t.rearrange("p g (b e n) -> p (g b) e n", e=2, n=2 ** (lvl - 1))
                return v[:, :, 0, :], v[:, :, 1, :]

            def level_exps(lvl):
                act.wait_ge(sig("sums_ready"), lvl)
                if lvl >= 2:
                    act.wait_ge(sig("qk_ready"), lvl)
                qe, ke = eqk[:, 0, :, :], eqk[:, 1, :, :]
                (pf_l, pf_r), (sb_l, sb_r) = halves(ll[:, 0, :, :], lvl), halves(ll[:, 1, :, :], lvl)
                (sf_l, sf_r), (pb_l, pb_r) = halves(xx[:, 0, :, :], lvl), halves(xx[:, 1, :, :], lvl)
                (q_l, q_r), (k_l, k_r) = halves(qe, lvl), halves(ke, lvl)
                for dst, src in ((q_r, pf_r), (q_l, sb_l), (k_l, sf_l), (k_r, pb_r)):
                    ins = act.activation(dst, src, ACT.Exp)
                ins.then_inc(sig("exps_ready"), 1)

            for s in range(4):
                diff_exp(s)
                split(U_GATES + s + 2)
                if s >= 1:
                    diff_copies(s - 1)
                if s >= 2:
                    diff_out(s - 2)
                if s % 2 == 0 and s:
                    gates_copy(s // 2 - 1)
            act.wait_ge(sig("abs_z"), 1)
            step(act.activation(flat(ee[:, :, :, :]), flat(ee[:, :, :, :]), ACT.Exp, scale=-1.0))
            settle()
            act.activation(flat(ee[:, :, :, :]), flat(ee[:, :, :, :]), ACT.Ln, bias=one[:, 0:1])\
                .then_inc(sig("softplus"), 1)
            diff_copies(3)
            diff_out(2)
            act.wait_ge(sig("log_k"), 1)
            ins = act.activation(kk[:, :, 0:2, :], kk[:, :, 0:2, :], ACT.Exp)
            ins = act.activation(ee[:, :, 0:2, :], ee[:, :, 0:2, :], ACT.Exp)
            ins.then_inc(sig("k_exp"), 1)
            act.wait_ge(sig("lb_term"), 1)
            act.activation(ee[:, :, 0:2, :], ee[:, :, 0:2, :], ACT.Ln, bias=one[:, 0:1]).then_inc(sig("lb_log"), 1)
            split(U_GATES + 6)
            gates_copy(1)
            diff_out(3)
            split(U_GATES + 7)
            for lvl in range(1, LEVELS):
                level_exps(lvl)
                u = U_GATES + 7 + lvl
                if lvl <= 4:
                    split(u)
                    if lvl == 1:
                        gates_copy(2)
                    if lvl == 3:
                        gates_copy(3)
                elif lvl == 5:
                    split(U_UP)
                    gates_copy(4)
                elif lvl == 6:
                    split(U_UP + 1)
                    gates_copy(5)
            act.wait_ge(sig("level_scored"), LEVELS)
            for n in range(2):
                ins = act.activation(far[:, 2 * n:2 * n + 2, :], aux[:, 2 * n:2 * n + 2, :], ACT.Copy)
            ins.then_inc(sig("far_ready"), 1)
            for n in range(3):
                v = gates[:, :, n * D:(n + 1) * D]
                act.activation(v, v, ACT.Sigmoid).then_inc(sig("gates_ready"), 1)
            act.wait_ge(sig("rec_valued"), 1)
            act.activation(xn[:, :, 0:512], omix_a[:, :, :], ACT.Square).then_inc(sig("head_square"), 1)
            act.activation(xn[:, :, 512:D], aux[:, 0:2, :], ACT.Square).then_inc(sig("head_square"), 1)
            act.wait_ge(sig("head_sums"), 2)
            step(act.activation(grms[:, :, 0:DH], gvar[:, :, 0:DH], ACT.Sqrt, bias=eps[:, 0:1], scale=1.0 / P))
            settle()
            act.activation(rinv[:, :, :], gsum[:, :, :], ACT.Sqrt, bias=eps[:, 0:1], scale=1.0 / HD)\
                .then_inc(sig("head_rms"), 1)
            operand(5)
            split(U_UP + 2)
            split(U_UP + 3)
            split(U_OUT)
            operand(6)
            split(U_OUT + 1)
            split(U_OUT + 2)
            split(U_OUT + 3)

            split(U_W1)
            act.wait_ge(sig("x_ready"), 8)
            stats(5, x)
            operand(7, scale_f[:, :], modc[:, 3, :])
            split(U_W1 + 1)

            def relu(par):
                act.activation(chunk[:, par, :, :], pj[:, 2 * par:2 * par + 2, :], ACT.Relu)\
                    .then_inc(sig("relu_done"), 1)

            def sq_hi(par, i, n):
                act.wait_ge(sig("sq_turned"), n + 2 * i)
                act.activation(hT_hi[:, bass.ds(4 * (n + 2 * i) - 4, 4), :],
                               aux[:, 2 * par:2 * par + 2, :].rearrange("p b (k s) -> p (b k) s", k=2),
                               ACT.Copy).then_inc(sig("sqT_hi"), 1)

            def mlp_pair(i, first):
                for par in range(2):
                    c = U_W1 + 2 * par
                    if not (first and par == 0):
                        split(c, i)
                        act.wait_ge(unit_done, c + 4 * i)
                        if not (first and par == 1):
                            act.wait_ge(sig("sq_turned"), 2 * i + par - 1)
                        relu(1 - par)
                        split(c + 1, i)
                        sq_hi(1 - par, i, par)

            mlp_pair(0, True)
            with act.Fori(1, KF2 // 8) as i:
                mlp_pair(i, False)
            split(U_W2)
            act.wait_ge(unit_done, U_W2)
            act.wait_ge(sig("sq_turned"), KF2 // 4 - 1)
            relu(1)
            split(U_W2 + 1)
            sq_hi(1, 0, KF2 // 4)
            for d in range(2, KF2 // 2):
                split(U_W2 + d)
            act.wait_ge(sig("x_ready"), 10)
            stats(6, x)

        @block.vector
        def _(dve):
            steps = [0]

            def step(ins):
                steps[0] += 1
                ins.then_inc(sig("dve_step"), 1)

            def settle():
                dve.wait_ge(sig("dve_step"), steps[0])

            def split(c, i=0):
                dve.wait_ge(hi_ready, c + 4 * i + 1)
                n = width(c)
                dve.tensor_tensor(w_lo[:, c % SPLIT, 0:n], raw[:, c % RAW, 0:n],
                                  w_hi[:, c % SPLIT, 0:n].bitcast(F32), ALU.subtract).then_inc(lo_ready, 1)

            def operand(t, gain=None, bias=None, order=(0, 1, 2, 3)):
                n = 0
                for b in order:
                    for k in (2 * b, 2 * b + 1):
                        n += 1
                        src = aux[:, b, (k % 2) * S:(k % 2 + 1) * S]
                        hi, dst = xT_hi[:, k, :].bitcast(F32), xT_lo[:, k, :]
                        dve.wait_ge(sig("xT_hi"), KD * t + (n + 1) // 2 * 2)
                        if bias is not None:
                            if n > 2:
                                dve.wait_ge(sig("xT_lo"), KD * t + n - 2)
                            step(dve.tensor_scalar(biased[:, k % 2, :], src, gain[:, k:k + 1], bias[:, k:k + 1],
                                                   ALU.mult, ALU.add))
                            settle()
                            ins = dve.tensor_tensor(dst, biased[:, k % 2, :], hi, ALU.subtract)
                        else:
                            if gain is not None:
                                ins = dve.scalar_tensor_tensor(dst, src, gain[:, k:k + 1], hi, ALU.mult, ALU.subtract)
                            else:
                                ins = dve.tensor_tensor(dst, src, hi, ALU.subtract)
                        ins.then_inc(sig("xT_lo"), 1)

            def rstd_of(n):
                dve.wait_ge(sig("rms_ready"), n + 1)
                dve.reciprocal(rstd[:, :], rms[:, :]).then_inc(sig("rstd_ready"), 1)

            def halves_of_x(h):
                return x[:, :, 512 * h:512 * h + 512], pj[:, 2 * h:2 * h + 2, :]

            def residual(n_half1, last_unit, factor):
                for h in (1, 0):
                    if h:
                        dve.wait_ge(sig("half1"), n_half1)
                    else:
                        dve.wait_ge(unit_done, last_unit + 1)
                    dst, src = halves_of_x(h)
                    dve.scalar_tensor_tensor(dst, src, factor, dst, ALU.mult, ALU.add).then_inc(sig("x_ready"), 1)

            def modulation():
                dve.wait_ge(sig("mod_sum"), 1)
                for g in (0, 3):
                    ins = dve.tensor_tensor(modc[:, g:g + 2, :].rearrange("p g k -> p (g k)"),
                                            aux[:, 2, KD * g:KD * (g + 2)],
                                            cols[:, R_ADAB + KD * g:R_ADAB + KD * (g + 2)], ALU.add)
                step(ins)
                settle()
                for dst, g, r in ((scale_m, 1, R_GM2), (scale_f, 4, R_GF2)):
                    dve.scalar_tensor_tensor(dst[:, :], modc[:, g, :], 1.0, cols[:, r:r + KD], ALU.add, ALU.mult)
                for n in range(4):
                    dve.wait_ge(sig("gt_sum"), n + 1)
                    dst = gt_row[:, n // 2, (n % 2) * 512:(n % 2) * 512 + 512]
                    dve.tensor_tensor(dst, dst, aux[:, 3, :], ALU.add).then_inc(sig("gt_done"), 1)

            def ffn(f, u0, t_stats):
                n = (NFULL + 1) * f

                def product(i, cols=512, c0=0, pair=1):
                    dve.wait_ge(sig("silu_done"), n + i)
                    for m in range(M):
                        ins = dve.scalar_tensor_tensor(chunk[:, 1, m, 0:cols], pj[:, 2 * pair + m, c0:c0 + cols],
                                                       rstd[:, m:m + 1], chunk[:, 0, m, 0:cols], ALU.mult, ALU.mult)
                    ins.then_inc(sig("h_ready"), 1)

                def hidden(blocks, i):
                    dve.wait_ge(sig("hT_hi"), n + i)
                    start = 4 * i - 4
                    dve.tensor_tensor(fT_lo[:, bass.ds(start, blocks), :],
                                      aux[:, 0:2, :].rearrange("p b (k s) -> p (b k) s", k=2)[:, 0:blocks, :],
                                      fT_hi[:, bass.ds(start, blocks), :].bitcast(F32),
                                      ALU.subtract).then_inc(sig("hT_lo"), 1)

                def ada(q, i):
                    dve.wait_ge(sig(f"ada_landed{q % 2}"), 16 * (2 * (4 * f - 1) + q // 2 + 1) + 32 * i)
                    dst = acc[:, q * 1536:(q + 1) * 1536]
                    dve.scalar_tensor_tensor(dst, ada_raw[:, q % 2, :], cond[:, bass.ds(4 * f - 1 + i, 1)], dst,
                                             ALU.mult, ALU.add).then_inc(sig("ada_free"), 1)

                split(u0 + 1)
                rstd_of(t_stats)
                split(u0 + 2)
                split(u0 + 3)
                with dve.Fori(1, NFULL) as i:
                    split(u0, i)
                    dve.wait_ge(unit_done, u0 + 4 * i)
                    product(i)
                    ada(0, i)
                    split(u0 + 1, i)
                    ada(1, i)
                    split(u0 + 2, i)
                    hidden(4, i)
                    ada(2, i)
                    split(u0 + 3, i)
                    ada(3, i)
                t = u0 + 4 * NFULL
                split(t)
                dve.wait_ge(unit_done, t)
                product(NFULL)
                split(t + 1)
                hidden(4, NFULL)
                split(t + 2)
                product(NFULL + 1, 256, 256, 0)
                split(t + 3)
                hidden(2, NFULL + 1)
                if f == 1:
                    modulation()
                for d in range(2, KF // 2):
                    split(t + 2 + d)

            split(U_F1)
            dve.wait_ge(sig("pos_in"), 16)
            dve.tensor_copy(rows[R_POS:R_POS + M, :], pos_i[R_POS:R_POS + M, :]).then_inc(sig("pos_row"), 1)
            dve.wait_ge(sig("cols_turned"), 1)
            dve.tensor_copy(cols[:, :], aux[:, 3, 0:NROW]).then_inc(sig("cols_ready"), 1)
            operand(0, cols[:, R_G1:R_G1 + KD])

            dve.wait_ge(sig("spread_in"), 16 * 10)
            for m in range(M):
                for a_ in range(2):
                    ins = dve.tensor_scalar(ang[:, a_, m, :], inv[:, :], cols[:, R_POS + m:R_POS + m + 1], None, ALU.mult)
            step(ins)
            settle()
            step(dve.tensor_scalar(turns[:, 0, :, :], ang[:, 0, :, :], 1 / TURN, None, ALU.mult))
            step(dve.tensor_scalar(turns[:, 1, :, :], ang[:, 1, :, :], 1 / TURN, 0.25, ALU.mult, ALU.add))
            settle()
            step(dve.tensor_scalar(nturn[:, :, :, :], turns[:, :, :, :], ROUND, None, ALU.add))
            settle()
            step(dve.tensor_scalar(nturn[:, :, :, :], nturn[:, :, :, :], -ROUND, None, ALU.add))
            settle()
            for part_of_turn in (TURN1, TURN2, TURN3):
                step(dve.scalar_tensor_tensor(ang[:, :, :, :], nturn[:, :, :, :], -part_of_turn, ang[:, :, :, :],
                                              ALU.mult, ALU.add))
                settle()
            step(dve.tensor_scalar(ang[:, 1, :, :], ang[:, 1, :, :], float(np.pi / 2), None, ALU.add))
            settle()
            dve.tensor_scalar(ang[:, :, :, :], ang[:, :, :, :], 3.1415925, -3.1415925, ALU.min, ALU.max)\
                .then_inc(sig("angles"), 1)

            dve.scalar_tensor_tensor(lgt[:, :, :], lgd[:, :, :], -1.0, lgd[:, :, :], ALU.mult, ALU.max)
            step(dve.tensor_tensor(lamt[:, :, :], lamp[:, 0:4:2, :], lamp[:, 1:4:2, :], ALU.mult))
            lb_cols = cols[:, R_LB:R_LB + 4].rearrange("p (d g) -> p d g", d=2)
            dve.tensor_tensor(lbt[:, :, :], lb_cols, lb_cols, ALU.subtract)
            settle()
            dve.tensor_reduce(lams[:, 0:2], lamt[:, :, :], AX.X, ALU.add).then_inc(sig("logs_in"), 1)
            dve.wait_ge(sig("ramps"), 1)
            dve.scalar_tensor_tensor(dist[:, :, :], dist_r[:, :, :], -1.0, dist_r[:, :, :], ALU.mult, ALU.max)
            dve.tensor_scalar(reach[:, 0, :], rel[:, :], 0.0, None, ALU.max)
            dve.tensor_scalar(reach[:, 1, :], rel[:, :], -1.0, 0.0, ALU.mult, ALU.max)
            dve.tensor_scalar(subg[:, :], subg[:, :], 1.0 - LAM_INIT, None, ALU.mult)
            step(dve.tensor_tensor(idx_x[:, :], idx_i[:, 0, :], idx_i[:, 1, :], ALU.bitwise_xor))
            settle()
            for lvl in range(7):
                dve.tensor_scalar(masks[:, lvl, :], idx_x[:, :], float(2 ** lvl), None, ALU.is_ge)
            dve.wait_ge(sig("logs_out"), 1)
            step(dve.scalar_tensor_tensor(lgd[:, :, :], lgd[:, :, :], 0.0, lgt[:, :, :], ALU.min, ALU.subtract))
            dve.scalar_tensor_tensor(lams[:, 2:3], lams[:, 1:2], -LAM_INIT, lams[:, 0:1], ALU.add, ALU.subtract)
            step(dve.reciprocal(lb1[:, :, :], lbt[:, :, :]))
            settle()
            step(dve.tensor_tensor(lbt[:, :, :], lbt[:, :, :], lb1[:, :, :], ALU.mult))
            settle()
            step(dve.tensor_tensor(lb[:, :, :], lbt[:, :, :], lbt[:, :, :], ALU.subtract))
            settle()
            step(dve.tensor_scalar(lb1[:, :, :], lb[:, :, :], -1.0, 1.0, ALU.mult, ALU.add))
            dve.wait_ge(sig("cond_ready"), 1)
            ffn(0, U_F1, 0)

            split(U_IN)
            residual(1, U_IN - 1, 0.5)
            operand(1, cols[:, R_MIX:R_MIX + KD], order=(2, 3, 0, 1))
            split(U_IN + 1)
            rstd_of(1)
            dve.wait_ge(sig("trig_ready"), 1)
            dve.wait_ge(sig("rstd_ready"), 2)
            for m in range(M):
                ins = dve.tensor_scalar(trig_r[:, :, m, :], trig[:, :, m, 0:32], rstd[:, m:m + 1], None, ALU.mult)
            step(ins)
            split(U_IN + 2)
            split(U_IN + 3)

            def rotate(o1, o2, x1, x2, sin, cos, t1, t2):
                settle()
                step(dve.tensor_tensor(t1, x2, sin, ALU.mult))
                step(dve.tensor_tensor(t2, x1, sin, ALU.mult))
                settle()
                step(dve.tensor_tensor(o1, x1, cos, ALU.mult))
                step(dve.tensor_tensor(o2, x2, cos, ALU.mult))
                settle()
                dve.tensor_tensor(o1, o1, t1, ALU.subtract)
                return dve.tensor_tensor(o2, o2, t2, ALU.add)

            dve.wait_ge(sig("p0_ready"), 1)
            k1, k2 = p0[:, :, QR + KVR:QR + KVR + 16], p0[:, :, QR + KVR + 16:C0]
            step(rotate(k1, k2, k1, k2, trig[:, 0, :, 32:48], trig[:, 1, :, 32:48], tmp_r[:, 0, :, 0:16],
                        tmp_r[:, 1, :, 0:16]))
            dve.wait_ge(sig("crms_ready"), 1)
            step(dve.reciprocal(crstd[:, :, :], crms[:, :, :]))
            settle()
            dve.tensor_scalar(crstd[:, :, 0], crstd[:, :, 0], MLA_SCALE, None, ALU.mult).then_inc(sig("crstd_ready"), 1)
            split(U_IN + 4)
            split(U_IN + 5)
            for k in range(3):
                dve.wait_ge(sig("cT_hi"), max(k + 1, 2))
                dve.scalar_tensor_tensor(cT_lo[:, k, :], aux[:, k // 2, (k % 2) * S:(k % 2 + 1) * S],
                                         cols[:, R_Q + k:R_Q + k + 1], cT_hi[:, k, :].bitcast(F32),
                                         ALU.mult, ALU.subtract).then_inc(sig("cT_lo"), 1)

            def rotate_ret(n):
                src = pj[:, 2:4, :] if n == 0 else pj[:, 0:2, :]
                s4 = src.rearrange("p m (h n) -> p m h n", n=HD)
                o4 = rqk[:, n, :, :].rearrange("p m (h n) -> p m h n", n=HD)

                def heads(t):
                    return t.unsqueeze(2).to_broadcast([P, M, H, 32])

                def temp(k):
                    return tmp_r[:, k, :, :].rearrange("p m (h n) -> p m h n", n=32)

                rotate(o4[:, :, :, 0:32], o4[:, :, :, 32:64], s4[:, :, :, 0:32], s4[:, :, :, 32:64],
                       heads(trig_r[:, 0, :, :]), heads(trig_r[:, 1, :, :]), temp(0), temp(1)).then_inc(sig("rot"), 1)

            dve.wait_ge(unit_done, U_IN + 4)
            rotate_ret(0)
            split(U_IN + 6)
            split(U_IN + 7)
            dve.wait_ge(unit_done, U_IN + 6)
            dve.wait_ge(sig("rot"), 1)
            rotate_ret(1)
            split(U_IN + 8)
            split(U_IN + 9)
            split(U_UQ)
            dve.wait_ge(sig("ret_turned"), 2)
            dve.tensor_copy(rqkT[:, 1, :, :].rearrange("p g s -> p (g s)"),
                            aux[:, 2:4, :].rearrange("p b n -> p (b n)")).then_inc(sig("rqkT_k"), 1)
            split(U_UKV)
            split(U_O)
            dve.wait_ge(sig("qf_ready"), 1)
            q4 = qf[:, :, :].rearrange("p m (h n) -> p m h n", n=QK)

            def mla_heads(t):
                return t.unsqueeze(2).to_broadcast([P, M, H, 16])

            def mla_temp(k):
                return tmp_r[:, k, :, 0:128].rearrange("p m (h n) -> p m h n", n=16)

            q1, q2 = q4[:, :, :, NOPE:NOPE + 16], q4[:, :, :, NOPE + 16:QK]
            rotate(q1, q2, q1, q2, mla_heads(trig[:, 0, :, 32:48]), mla_heads(trig[:, 1, :, 32:48]),
                   mla_temp(0), mla_temp(1)).then_inc(sig("q_rot"), 1)
            split(U_O + 1)
            dve.wait_ge(sig("kv_ready"), 1)
            dve.tensor_copy(kf[:, :, :].rearrange("p m (h n) -> p m h n", n=QK)[:, :, :, NOPE:QK],
                            p0[:, :, QR + KVR:C0].unsqueeze(2).to_broadcast([P, M, H, ROPE]))\
                .then_inc(sig("kf_ready"), 1)

            def decay_log(h):
                step(dve.tensor_scalar(decay[:, h % 2, :], reach[:, 0, :], lgd[:, 0, h:h + 1], None, ALU.mult))
                settle()
                dve.scalar_tensor_tensor(decay[:, h % 2, :], reach[:, 1, :], lgd[:, 1, h:h + 1], decay[:, h % 2, :],
                                         ALU.mult, ALU.add).then_inc(sig("decay_log"), 1)

            decay_log(0)
            dve.wait_ge(sig("q_rot"), 1)
            for h in range(H):
                if h + 1 < H:
                    if h:
                        dve.wait_ge(sig("rpT_ready"), h)
                    decay_log(h + 1)
                dve.wait_ge(sig("decay_ready"), h + 1)
                dve.wait_ge(sig("ret_scored"), h + 1)
                if h >= 2:
                    dve.wait_ge(sig("ret_valued"), h - 1)
                for jt in range(M):
                    ins = dve.scalar_tensor_tensor(rpT[:, h % 2, jt, :], aux[:, h % 2, jt * S:(jt + 1) * S], HD ** -0.5,
                                                   decay[:, h % 2, P * (1 - jt):P * (1 - jt) + S], ALU.mult, ALU.mult)
                ins.then_inc(sig("rpT_ready"), 1)

            def heads64(t):
                return t.unsqueeze(3).to_broadcast([P, M, H, HD])

            r4 = pj[:, 2:4, :].rearrange("p m (h n) -> p m h n", n=HD)
            mr4 = mix_r[:, :, :].rearrange("p m (h n) -> p m h n", n=HD)
            dve.wait_ge(sig("ret_valued"), H)
            step(dve.tensor_reduce(gsum[:, :, :], r4, AX.X, ALU.add))
            settle()
            step(dve.tensor_scalar(gsum[:, :, :], gsum[:, :, :], -1.0 / HD, None, ALU.mult))
            settle()
            dve.tensor_tensor(mr4, r4, heads64(gsum[:, :, :]), ALU.add).then_inc(sig("centred"), 1)
            for b in range(4):
                dve.wait_ge(sig("mla_turned"), 5 + b)
                dve.tensor_copy(kT[0:QK, 2 * b:2 * b + 2, :].rearrange("p h s -> p (h s)"), aux[0:QK, b, :])\
                    .then_inc(sig("kT_ready"), 1)
            dve.wait_ge(sig("gn_square"), 1)
            dve.tensor_reduce(gvar[:, :, :].rearrange("p m h -> p (m h)"),
                              tmp_r[:, :, :, :].rearrange("p a m s -> p (a m s)").rearrange("p (x n) -> p x n", n=HD),
                              AX.X, ALU.add).then_inc(sig("gvar_ready"), 1)

            def mla_max(h):
                dve.wait_ge(sig("mla_scored"), h + 1)
                dve.tensor_reduce(mx[:, h % 2, :], aux[:, h % 2, :].rearrange("p (m s) -> p m s", m=M), AX.X, ALU.max,
                                  negate=True).then_inc(sig("mla_max"), 1)

            def mla_prob(h):
                dve.wait_ge(sig("prob_turned"), h + 1)
                if h >= 2:
                    dve.wait_ge(sig("mla_valued"), h - 1)
                dve.tensor_copy(probT[:, h % 2, :, :].rearrange("p k s -> p (k s)"), aux[:, 2 + h % 2, :])\
                    .then_inc(sig("probT_ready"), 1)

            for s in range(H + 1):
                if s < H:
                    mla_max(s)
                if s >= 1:
                    mla_prob(s - 1)
                if s == 1:
                    dve.wait_ge(sig("grms_ready"), 1)
                    dve.wait_ge(sig("centred"), 1)
                    step(dve.reciprocal(grstd[:, :, :], grms[:, :, :]))
                    settle()
                    step(dve.tensor_tensor(mr4, mr4, heads64(grstd[:, :, :]), ALU.mult))
                    settle()
                    dve.tensor_tensor(mix_r[:, :, :], mix_r[:, :, :], sgr[:, :, :], ALU.mult)\
                        .then_inc(sig("mix_ready"), 1)
            dve.wait_ge(sig("mla_valued"), H)
            step(dve.reciprocal(rinv[:, :, :], rowsum[:, :, :]))
            settle()
            dve.tensor_tensor(mix_a[:, :, :].rearrange("p m (h n) -> p m h n", n=HD),
                              pj[:, 0:2, :].rearrange("p m (h n) -> p m h n", n=HD), heads64(rinv[:, :, :]),
                              ALU.mult).then_inc(sig("mix_ready"), 1)
            operand(2)
            split(U_O + 2)
            split(U_O + 3)
            split(U_F2)
            residual(4, U_O + 3, 1.0)

            operand(3, cols[:, R_G2:R_G2 + KD], order=(2, 3, 0, 1))
            ffn(1, U_F2, 2)

            split(U_IN2)
            residual(5, U_IN2 - 1, 0.5)
            rstd_of(3)
            dve.wait_ge(sig("rstd_ready"), 4)
            for m in range(M):
                ins = dve.scalar_tensor_tensor(x[:, m, :], x[:, m, :], rstd[:, m:m + 1], norm_row[:, :], ALU.mult,
                                               ALU.mult)
            ins.then_inc(sig("normed"), 1)

            def normalise(n, ready):
                rstd_of(n)
                dve.wait_ge(sig("rstd_ready"), n + 1)
                for m in range(M):
                    ins_ = dve.tensor_scalar(xn[:, m, :], x[:, m, :], rstd[:, m:m + 1], None, ALU.mult)
                ins_.then_inc(sig("xn_ready"), 1)

            normalise(4, 1)
            operand(4, scale_m[:, :], modc[:, 0, :])
            c = U_IN2
            for n in range(1, 6):
                split(c + n)

            def banks(b):
                return aux[:, b:b + 2, :].rearrange("p b n -> p (b n)")

            dve.wait_ge(sig("blocks_turned"), 1)
            dve.tensor_scalar(aqT[:, :, :].rearrange("p h s -> p (h s)"), banks(0), HD ** -0.5, None, ALU.mult)\
                .then_inc(sig("turned_read"), 1)
            split(c + 6)
            split(c + 7)
            dve.wait_ge(sig("blocks_turned"), 2)
            dve.tensor_copy(akT[:, :, :].rearrange("p h s -> p (h s)"), banks(2)).then_inc(sig("turned_read"), 1)
            for n in range(8, 12):
                split(c + n)
            dve.wait_ge(sig("blocks_turned"), 3)
            dve.tensor_copy(zz[:, 0, 0:2, :].rearrange("p g s -> p (g s)"), aux[:, 1, :])
            dve.wait_ge(sig("q_silu"), 1)
            dve.tensor_scalar(qt[:, 0:2, :], qt[:, 0:2, :], HD ** -0.5, None, ALU.mult).then_inc(sig("turned_read"), 1)
            split(c + 12)
            split(c + 13)
            dve.wait_ge(sig("blocks_turned"), 4)
            dve.tensor_copy(zz[:, 1, 0:2, :].rearrange("p g s -> p (g s)"), aux[:, 2, :])\
                .then_inc(sig("turned_read"), 1)
            split(U_LR)
            dve.wait_ge(sig("blocks_turned"), 5)
            dve.tensor_scalar(qt[:, 2, :], aux[:, 3, 0:S], 32 ** -0.5, None, ALU.mult)
            for d in range(2):
                ins = dve.tensor_copy(kk[:, d, 2, :], aux[:, 3, S:2 * S])
            ins.then_inc(sig("turned_read"), 1)
            split(U_GATES)
            split(U_GATES + 1)

            def diff_softmax(h):
                dve.wait_ge(sig("diff_scored"), h + 1)
                if h:
                    dve.wait_ge(sig("diff_turned"), h)
                dve.scalar_tensor_tensor(dmap[:, :, :, :].rearrange("p j m s -> p j (m s)"),
                                         dist[:, :, :].rearrange("p m s -> p (m s)").unsqueeze(1)
                                         .to_broadcast([P, 2, M * S]),
                                         -(2.0 ** (-8.0 * (h + 1) / DH)), aux[:, 0:2, :], ALU.mult, ALU.add)\
                    .then_inc(sig("biased"), 1)
                dve.wait_ge(sig("biased"), h + 1)
                dve.tensor_reduce(dl[:, :, :], dmap[:, :, :, :], AX.X, ALU.max, negate=True)\
                    .then_inc(sig("diff_max"), 1)
                dve.wait_ge(sig("diff_exp"), h + 1)
                step(dve.reciprocal(dr[:, :, :], dr[:, :, :]))
                settle()
                step(dve.tensor_scalar(dr[:, 1, :], dr[:, 1, :], lams[:, 2:3], None, ALU.mult))
                for m in range(M):
                    step(dve.tensor_scalar(dmap[:, 0, m, :], dmap[:, 0, m, :], dr[:, 0, m:m + 1], None, ALU.mult))
                settle()
                for m in range(M):
                    ins_ = dve.scalar_tensor_tensor(dmap[:, 0, m, :], dmap[:, 1, m, :], dr[:, 1, m:m + 1],
                                                    dmap[:, 0, m, :], ALU.mult, ALU.add)
                ins_.then_inc(sig("diff_w"), 1)

            for s in range(DH):
                diff_softmax(s)
                split(U_GATES + s + 2)

            step(dve.scalar_tensor_tensor(ee[:, :, :, :], zz[:, :, :, :], -1.0, zz[:, :, :, :], ALU.mult, ALU.max))
            ins = dve.tensor_copy(qkh[:, 0, 0, :, :], qt[:, :, :])
            ins.then_inc(sig("abs_z"), 1)
            dve.wait_ge(sig("softplus"), 1)
            step(dve.scalar_tensor_tensor(ll[:, :, :, :], zz[:, :, :, :], 0.0, ee[:, :, :, :], ALU.min, ALU.subtract))
            settle()
            dve.tensor_tensor(kk[:, :, 0:2, :], ll[:, :, 0:2, :], zz[:, :, 0:2, :], ALU.subtract)
            dve.tensor_scalar(ee[:, :, 0:2, :], zz[:, :, 0:2, :], -1.0, 80.0, ALU.mult, ALU.min)\
                .then_inc(sig("log_k"), 1)
            step(dve.tensor_scalar(ll[:, :, 2, :], ll[:, :, 2, :], 1.0 / 16.0, None, ALU.mult))
            dve.wait_ge(sig("k_exp"), 1)

            for dst, by, last in ((kk, lb1, False), (ee, lb, True)):
                for d in range(2):
                    ins = dve.tensor_tensor(dst[:, d, 0:2, :], dst[:, d, 0:2, :],
                                            by[:, d, :].unsqueeze(2).to_broadcast([P, 2, S]), ALU.mult)
                if last:
                    ins.then_inc(sig("lb_term"), 1)
                else:
                    step(ins)
            dve.memset(xx[:, :, :, :], 0.0)
            settle()
            dve.tensor_tensor(qkh[:, 0, 1, :, :], kk[:, 0, :, :], kk[:, 1, :, :], ALU.add).then_inc(sig("qk_ready"), 1)
            dve.wait_ge(sig("lb_log"), 1)
            dve.tensor_tensor(ll[:, :, 0:2, :], ll[:, :, 0:2, :], ee[:, :, 0:2, :], ALU.add)\
                .then_inc(sig("sums_ready"), 1)
            split(U_GATES + 6)
            split(U_GATES + 7)

            def read_level(n):
                dve.wait_ge(sig("level_scored"), n + 1)
                if n == 0:
                    ins_ = dve.tensor_copy(near[:, :, :], aux[:, :, :])
                else:
                    dve.wait_ge(sig("level_read"), n)
                    ins_ = dve.copy_predicated(near[:, :, :].rearrange("p b (x t) -> p (b x) t", t=P),
                                               masks[:, n - 1, :].unsqueeze(1).to_broadcast([P, 16, P]),
                                               aux[:, :, :].rearrange("p b (x t) -> p (b x) t", t=P))
                ins_.then_inc(sig("level_read"), 1)

            def halves(t, lvl):
                v = t.rearrange("p g (b e n) -> p (g b) e n", e=2, n=2 ** (lvl - 1))
                return v[:, :, 0, :], v[:, :, 1, :]

            for lvl in range(1, LEVELS):
                dve.wait_ge(sig("exps_ready"), lvl)
                if lvl >= 2:
                    dve.wait_ge(sig("level_scored"), lvl - 1)
                b = lvl % 2
                dve.tensor_tensor(qkh[:, b, 0, :, :], qt[:, :, :], eqk[:, 0, :, :], ALU.mult)
                (o_l, o_r), (e_l, e_r) = halves(qkh[:, b, 1, :, :], lvl), halves(eqk[:, 1, :, :], lvl)
                dve.tensor_tensor(o_l, halves(kk[:, 0, :, :], lvl)[0], e_l, ALU.mult)
                dve.tensor_tensor(o_r, halves(kk[:, 1, :, :], lvl)[1], e_r, ALU.mult).then_inc(sig("qk_ready"), 1)
                read_level(lvl - 1)
                u = U_GATES + 7 + lvl
                if lvl <= 4:
                    split(u)
                elif lvl <= 6:
                    split(U_UP + lvl - 5)

            for n in range(2):
                v = og[:, :, n * S:(n + 1) * S].rearrange("p m (h n) -> p m h n", n=HD)
                ins = dve.tensor_tensor(v, v, headg[:, n, :].unsqueeze(1).unsqueeze(1).to_broadcast([P, M, DH, HD]),
                                        ALU.mult)
            step(ins)
            dve.wait_ge(sig("head_square"), 1)
            dve.tensor_reduce(gvar[:, :, 0:DH], xn[:, :, 0:512].rearrange("p m (h n) -> p m h n", n=P), AX.X, ALU.add)\
                .then_inc(sig("head_sums"), 1)
            dve.wait_ge(sig("head_square"), 2)
            dve.tensor_reduce(gsum[:, :, :], xn[:, :, 512:D].rearrange("p m (h n) -> p m h n", n=HD), AX.X, ALU.add)\
                .then_inc(sig("head_sums"), 1)
            dve.wait_ge(sig("head_rms"), 1)
            step(dve.reciprocal(grstd[:, :, 0:DH], grms[:, :, 0:DH]))
            step(dve.reciprocal(gvar[:, :, :], rinv[:, :, :]))
            settle()
            oa = omix_a[:, :, :].rearrange("p m (h n) -> p m h n", n=P)
            orec = omix_r[:, :, :].rearrange("p m (h n) -> p m h n", n=HD)
            step(dve.tensor_tensor(oa, oa, grstd[:, :, 0:DH].unsqueeze(3).to_broadcast([P, M, DH, P]), ALU.mult))
            step(dve.tensor_tensor(orec, aux[:, 0:2, :].rearrange("p m (h n) -> p m h n", n=HD),
                                   heads64(gvar[:, :, :]), ALU.mult))
            settle()
            dve.tensor_tensor(oa, oa, subg[:, :].unsqueeze(1).unsqueeze(1).to_broadcast([P, M, DH, P]), ALU.mult)\
                .then_inc(sig("omix_ready"), 1)
            dve.tensor_tensor(omix_r[:, :, :], omix_r[:, :, :], og[:, :, :], ALU.mult)\
                .then_inc(sig("omix_ready"), 1)
            operand(5)
            split(U_UP + 2)

            def branch(n):
                dve.wait_ge(sig("gates_ready"), n + 1)
                for h in (1, 0):
                    if h:
                        dve.wait_ge(sig("half1"), 6 + n)
                    else:
                        dve.wait_ge(unit_done, U_UP + 2 + n)
                    src = pj[:, 2 * h:2 * h + 2, :]
                    g = gates[:, :, n * D + 512 * h:n * D + 512 * h + 512]
                    dst = xn[:, :, 512 * h:512 * h + 512]
                    k = 2 * n + (h == 0) + 1
                    if n == 0:
                        dve.tensor_tensor(dst, src, g, ALU.mult).then_inc(sig("branch_read"), 1)
                    else:
                        dve.tensor_tensor(g, src, g, ALU.mult).then_inc(sig("branch_read"), 1)
                        dve.wait_ge(sig("branch_read"), k)
                        ins_ = dve.tensor_tensor(dst, dst, g, ALU.add)
                        if n == 2:
                            ins_.then_inc(sig("merged"), 1)
                        else:
                            step(ins_)

            branch(0)
            split(U_UP + 3)
            branch(1)
            settle()
            branch(2)
            split(U_OUT)
            operand(6)
            for d in range(1, 4):
                split(U_OUT + d)
            split(U_W1)

            def gated_residual(n, n_half1, last_unit, temp):
                for h in (1, 0):
                    if h:
                        dve.wait_ge(sig("half1"), n_half1)
                    else:
                        dve.wait_ge(unit_done, last_unit + 1)
                    dst, src = halves_of_x(h)
                    t = temp[:, :, 512 * h:512 * h + 512]
                    g = gt_row[:, n, 512 * h:512 * h + 512].unsqueeze(1).to_broadcast([P, M, 512])
                    step(dve.tensor_tensor(t, src, g, ALU.mult))
                    settle()
                    dve.tensor_tensor(dst, dst, t, ALU.add).then_inc(sig("x_ready"), 1)

            gated_residual(0, 9, U_OUT + 3, part)

            normalise(5, 2)
            operand(7, scale_f[:, :], modc[:, 3, :])
            split(U_W1 + 1)

            def square(par, i, n):
                dve.wait_ge(sig("relu_done"), n + 2 * i)
                v = chunk[:, par, :, :]
                dve.tensor_tensor(v, v, v, ALU.mult).then_inc(sig("sq_ready"), 1)

            def sq_lo(par, i, n):
                dve.wait_ge(sig("sqT_hi"), n + 2 * i)
                at_ = bass.ds(4 * (n + 2 * i) - 4, 4)
                dve.tensor_tensor(hT_lo[:, at_, :],
                                  aux[:, 2 * par:2 * par + 2, :].rearrange("p b (k s) -> p (b k) s", k=2),
                                  hT_hi[:, at_, :].bitcast(F32), ALU.subtract).then_inc(sig("sqT_lo"), 1)

            def mlp_pair(i, first):
                for par in range(2):
                    c_ = U_W1 + 2 * par
                    if not (first and par == 0):
                        split(c_, i)
                        square(1 - par, i, par)
                        split(c_ + 1, i)
                        sq_lo(1 - par, i, par)

            mlp_pair(0, True)
            with dve.Fori(1, KF2 // 8) as i:
                mlp_pair(i, False)
            split(U_W2)
            square(1, 0, KF2 // 4)
            split(U_W2 + 1)
            sq_lo(1, 0, KF2 // 4)
            for d in range(2, KF2 // 2):
                split(U_W2 + d)
            gated_residual(1, 10, U_W2 + KF2 // 2 - 1, part2)
            rstd_of(6)
            dve.wait_ge(sig("rstd_ready"), 7)
            dve.wait_ge(sig("row2_in"), 16)
            for m in range(M):
                ins = dve.scalar_tensor_tensor(x[:, m, :], x[:, m, :], rstd[:, m:m + 1], norm_row[:, :], ALU.mult,
                                               ALU.mult)
            ins.then_inc(sig("y_ready"), 1)

        @block.gpsimd
        def _(pool):
            steps = [0]

            def step(ins):
                steps[0] += 1
                ins.then_inc(sig("pool_step"), 1)

            def settle():
                pool.wait_ge(sig("pool_step"), steps[0])

            pool.memset(ident[:, :], 1.0).then_inc(sig("ident_ready"), 1)
            pool.wait_ge(sig("ident_ready"), 1)
            pool.affine_select(ident[:, :], ident[:, :], pattern=[[-1, P]], compare_op=ALU.is_equal, fill=0.0, base=0,
                               channel_multiplier=1).then_inc(sig("ident_ready"), 1)
            pool.memset(ones[:, :], 1.0)
            pool.memset(one[:, :], 1.0)
            pool.memset(eps[:, :], EPS).then_inc(sig("consts"), 1)
            pool.memset(gate2[:, :, :], 0.0).then_inc(sig("gate2_zero"), 1)
            pool.iota(rel[:, :], pattern=[[1, 3 * P]], base=-P, channel_multiplier=-1,
                      allow_small_or_imprecise_dtypes=True)
            pool.iota(dist_r[:, :, :], pattern=[[-P, M], [1, S]], base=0, channel_multiplier=-1,
                      allow_small_or_imprecise_dtypes=True)
            pool.iota(idx_i[:, 0, :], pattern=[[0, P]], base=0, channel_multiplier=1)
            pool.iota(idx_i[:, 1, :], pattern=[[1, P]], base=0, channel_multiplier=0).then_inc(sig("ramps"), 1)
            pool.memset(acc[:, :], 0.0).then_inc(sig("ada_free"), 2)

            def halves(t, lvl):
                v = t.rearrange("p g (b e n) -> p (g b) e n", e=2, n=2 ** (lvl - 1))
                return v[:, :, 0, :], v[:, :, 1, :]

            for lvl in range(1, LEVELS - 1):
                n = 2 ** (lvl - 1)
                pool.wait_ge(sig("exps_ready"), lvl)
                (f_l, f_r), (b_l, b_r) = halves(ll[:, 0, :, :], lvl), halves(ll[:, 1, :, :], lvl)
                xf_l, xb_r = halves(xx[:, 0, :, :], lvl)[0], halves(xx[:, 1, :, :], lvl)[1]
                shape = [P, 3 * S // (2 * n), n]
                pool.tensor_tensor(xf_l, xf_l, f_r[:, :, n - 1:n].to_broadcast(shape), ALU.add)
                step(pool.tensor_tensor(xb_r, xb_r, b_l[:, :, 0:1].to_broadcast(shape), ALU.add))
                settle()
                pool.tensor_tensor(f_r, f_r, f_l[:, :, n - 1:n].to_broadcast(shape), ALU.add)
                pool.tensor_tensor(b_l, b_l, b_r[:, :, 0:1].to_broadcast(shape), ALU.add)\
                    .then_inc(sig("sums_ready"), 1)


_INS = [
    "x", "positions", "ffn1_norm", "ffn1_w_gate", "ffn1_w_up", "ffn1_w_down", "mix_norm", "w_in", "q_norm",
    "w_uq", "kv_norm", "w_ukv", "ret_decay_fwd", "ret_decay_bwd", "w_o", "ffn2_norm", "ffn2_w_gate",
    "ffn2_w_up", "ffn2_w_down", "final_norm", "c_2", "ada_w_2", "ada_b_2", "norm_mix_g_2", "norm_mlp_g_2",
    "w_in_2", "diff_lambda_2", "diff_subln_g_2", "hgrn_lb_logits_2", "hgrn_norm_g_2", "gla_gate_w2_2",
    "gla_gate_b_2", "gla_norm_g_2", "w_up_a_2", "w_up_b_2", "w_up_c_2", "w_out_2", "mlp_w1_2", "mlp_w2_2",
    "final_norm_g_2", "inv_freq"]


def kernel(**inputs):
    import numpy as _np
    import concourse.bacc as _bacc
    from concourse import mybir as _mybir
    from concourse.bass_utils import run_bass_kernel_spmd as _run

    inv_freq = _np.concatenate([_np.float32(ROPE_THETA) ** (-_np.arange(n, dtype=_np.float32) / _np.float32(n))
                                for n in (HD // 2, ROPE // 2)]).astype(_np.float32)[None, :]
    nc = _bacc.Bacc("TRN2", target_bir_lowering=False, num_devices=1)
    arrays, args = {}, {}
    for name in _INS:
        v = inv_freq if name == "inv_freq" else _np.ascontiguousarray(inputs[name])
        arrays[f"in_{name}_dram"] = v
        args[name] = nc.dram_tensor(f"in_{name}_dram", v.shape, _mybir.dt.from_np(v.dtype), kind="ExternalInput").ap()
    out = nc.dram_tensor("out_0_dram", (1, S, D), F32, kind="ExternalOutput").ap()
    build(nc, args, out)
    r = _run(nc, [arrays], core_ids=[0])
    return r.results[0]["out_0_dram"]
```

```python
from contextlib import ExitStack

import numpy as np

import concourse.bass as bass
from concourse import mybir

F32 = mybir.dt.float32
F32R = mybir.dt.float32r
I32 = mybir.dt.int32
U8 = mybir.dt.uint8
ALU = mybir.AluOpType
ACT = mybir.ActivationFunctionType
AX = mybir.AxisListType

P = 128
S = 256
M = S // P
D = 1024
KD = D // P
FF = 2816
KF = FF // P
NFULL = FF // 512
FF2 = 4096
KF2 = FF2 // P
EPS = 1e-6
UC = 2048
RAW = 4
SPLIT = 2

H = 8
QR, KVR, ROPE, NOPE, VD = 256, 128, 32, 64, 64
QK = NOPE + ROPE
C0 = QR + KVR + ROPE
MLA_SCALE = QK ** -0.5
HD = 64
ROPE_THETA = 10000.0
TURN = 2 * float(np.pi)
TURN1, TURN2 = 6.28125, 0.0019350051879882812
TURN3 = TURN - TURN1 - TURN2
ROUND = 1.5 * 2 ** 23

DH = 4
NMOD = 6
LR = 16
LAM_INIT = 0.8 - 0.6 * float(np.exp(-0.3 * 0))

U_FFN = 4 * NFULL + 2 + KF // 2
U_F1 = 0
U_IN = U_F1 + U_FFN
U_UQ = U_IN + 10
U_UKV = U_UQ + 1
U_O = U_UKV + 1
U_F2 = U_O + 4
U_IN2 = U_F2 + U_FFN
U_LR = U_IN2 + 8
U_ATT = U_LR + 1
U_GATES = U_ATT + 6
U_UP = U_GATES + 12
U_OUT = U_UP + 4
U_W1 = U_OUT + 4
U_W2 = U_W1 + 16
U_END = U_W2 + KF2 // 2

R_G1, R_MIX, R_G2, R_GM2, R_GF2, R_ADAB, R_C, R_POS, R_Q, R_KV, R_LB, R_GB, R_SUB = (
    0, 8, 16, 24, 32, 40, 88, 96, 98, 100, 101, 105, 107)
NROW = 108
ROWS = [("ffn1_norm", R_G1, KD), ("mix_norm", R_MIX, KD), ("ffn2_norm", R_G2, KD), ("norm_mix_g_2", R_GM2, KD),
        ("norm_mlp_g_2", R_GF2, KD), ("ada_b_2", R_ADAB, 6 * KD), ("c_2", R_C, KD), ("q_norm", R_Q, 2),
        ("kv_norm", R_KV, 1), ("hgrn_lb_logits_2", R_LB, 4), ("gla_gate_b_2", R_GB, 2),
        ("diff_subln_g_2", R_SUB, 1)]
C_LR = 3 * 512 + 5 * 256 + 2 * 128 + 2 * 256

K_HALVES = ((0, 4), (4, 0))

LEVELS = 9
HEAD_ORDER = (0, 1, 2, 3, 4, 5, 6, 7)


def head_place(hh):
    if hh < DH:
        return (0, 2, 1, 3)[hh], 0, hh // 2, 64 * (hh % 2), 64
    return hh - DH, 1, 2, 32 * (hh - DH), 32


def build(nc, a, out):
    with ExitStack() as ctx:
        top = [(nc.sbuf_base + 63) // 64 * 64]

        def at(name, shape, dt, offset):
            return nc.alloc_sbuf_tensor_at(name, shape, dt, offset=offset)

        def size(shape, dt):
            return int(np.prod(shape[1:])) * {F32: 4, F32R: 4, I32: 4, U8: 1}[dt]

        def sb(name, shape, dt=F32):
            t = at(name, shape, dt, top[0])
            top[0] += (size(shape, dt) + 31) // 32 * 32
            return t

        raw = sb("raw", [P, RAW, UC])
        w_hi = sb("w_hi", [P, SPLIT, UC], F32R)
        w_lo = sb("w_lo", [P, SPLIT, UC], F32R)
        x = sb("x_res", [P, M, D])
        xT_hi = sb("xT_hi", [P, KD, S], F32R)
        xT_lo = sb("xT_lo", [P, KD, S], F32R)
        ident = sb("ident", [P, P])
        ones = sb("ones", [P, P])
        norm_row_at = top[0]
        norm_row = sb("norm_row", [P, D])
        gt_row = sb("gt_row", [P, 2, D])
        chunk_at = top[0]
        chunk = sb("chunk", [P, 2, M, 512])
        xn = at("xn", [P, M, D], F32, chunk_at)
        prob = at("prob", [P, 2, M, S], F32, chunk_at)
        probT = at("probT", [P, 2, M, S], F32, chunk_at + 4096)
        dmap = at("dmap", [P, 2, M, S], F32, chunk_at)
        dmapT = at("dmapT", [P, M, S], F32, chunk_at + 4096)
        akT = at("akT", [P, DH, S], F32, norm_row_at)
        dist = sb("dist", [P, M, S])
        masks = sb("masks", [P, 7, P], U8)
        trig = sb("trig", [P, 2, M, 48])
        trig_r = sb("trig_r", [P, 2, M, 32])
        rows = sb("rows", [NROW, P])
        cols = sb("cols", [P, NROW])
        cond = sb("cond", [P, KD])
        modc = sb("modc", [P, NMOD, KD])
        scale_m = sb("scale_m", [P, KD])
        scale_f = sb("scale_f", [P, KD])
        lgd = sb("lgd", [P, 2, H])
        lgt = sb("lgt", [P, 2, H])
        gate2 = sb("gate2", [2 * LR, 2, P])
        lrT = sb("lrT", [2 * LR, S])
        lb = sb("lb", [P, 2, 2])
        lb1 = sb("lb1", [P, 2, 2])
        lbt = sb("lbt", [P, 2, 2])
        lamp = sb("lamp", [P, 4, 64])
        lamt = sb("lamt", [P, 2, 64])
        lams = sb("lams", [P, 4])
        headg = sb("headg", [P, 2, 64])
        subg = sb("subg", [P, KD])
        eps = sb("eps", [P, 1])
        root_of_one = sb("root_of_one", [P, 1])
        one = sb("one", [P, 1])
        ss = sb("ss", [P, 2, 2, M])
        tot = sb("tot", [P, 2, M])
        rms = sb("rms", [P, M])
        rms2 = sb("rms2", [P, 2, M])
        ms = sb("ms", [P, 2, M])
        rstd = sb("rstd", [P, M])
        rstd2 = sb("rstd2", [P, 2, M])
        cs = sb("cs", [P, M, 2])
        crms = sb("crms", [P, M, 2])
        crstd = sb("crstd", [P, M, 2])
        mx = sb("mx", [P, 2, M])
        rowsum = sb("rowsum", [P, M, H])
        rinv = sb("rinv", [P, M, H])
        gsum = sb("gsum", [P, M, H])
        gvar = sb("gvar", [P, M, H])
        grms = sb("grms", [P, M, H])
        grstd = sb("grstd", [P, M, H])
        dl = sb("dl", [P, 2, M])
        dr = sb("dr", [P, 2, M])
        region = (top[0] + 63) // 64 * 64
        KB = 1024

        def place(name, shape, kb, dt=F32):
            o = region + int(kb * KB)
            assert o + size(shape, dt) <= nc.sbuf_usable_end, (name, o + size(shape, dt) - nc.sbuf_usable_end)
            return at(name, shape, dt, o)

        fT_hi = place("fT_hi", [P, KF, S], 0, F32R)
        fT_lo = place("fT_lo", [P, KF, S], 22, F32R)
        acc = place("acc", [P, NMOD * D], 44)
        ada_raw = place("ada_raw", [P, 2, 1536], 68)
        scratch = place("scratch", [P, M, D], 68)
        scratch2 = place("scratch2", [P, M, 512], 76)
        rqk = place("rqk", [P, 2, M, 512], 0)
        kT = place("kT", [QK, H, S], 0)
        qf = place("qf", [P, M, H * QK], 8)
        mix_a = place("mix_a", [P, M, 512], 8)
        kf = place("kf", [P, M, H * QK], 14)
        v1 = place("v1", [P, M, H * VD], 20)
        rv = place("rv", [P, M, H * HD], 24)
        sgr = place("sgr", [P, M, H * HD], 28)
        mix_r = place("mix_r", [P, M, 512], 32)
        rqkT = place("rqkT", [P, 2, 4, S], 36)
        qT = place("qT", [QK, H, S], 36)
        p0 = place("p0", [P, M, C0], 68)
        decay = place("decay", [P, 2, 384], 71.5)
        cT_hi = place("cT_hi", [P, 3, S], 74.5, F32R)
        cT_lo = place("cT_lo", [P, 3, S], 77.5, F32R)
        reach = place("reach", [P, 2, 384], 80.5)
        rpT = place("rpT", [P, 2, 2, S], 83.5)
        tmp_r = place("tmp_r", [P, 2, M, S], 83.5)
        inv = place("inv", [P, 48], 0.25)
        ang = place("ang", [P, 2, M, 48], 1)
        turns = place("turns", [P, 2, M, 48], 2)
        nturn = place("nturn", [P, 2, M, 48], 3)
        idx_i = place("idx_i", [P, 2, P], 4, I32)
        idx_x = place("idx_x", [P, P], 5, I32)
        rel = place("rel", [P, 384], 6)
        pos_i = place("pos_i", [P, P], 12, I32)
        dist_r = place("dist_r", [P, M, S], 8)
        gates = place("gates", [P, M, 3 * D], 0)
        aqT = place("aqT", [P, DH, S], 83)
        near = place("near", [P, 4, 512], 24)
        av = place("av", [P, M, 512], 32)
        zz = place("zz", [P, 2, 3, S], 36)
        xx = place("xx", [P, 2, 3, S], 36)
        ee = place("ee", [P, 2, 3, S], 42)
        eqk = place("eqk", [P, 2, 3, S], 42)
        far = place("far", [P, 4, 512], 36)
        ll = place("ll", [P, 2, 3, S], 48)
        qt = place("qt", [P, 3, S], 54)
        kk = place("kk", [P, 2, 3, S], 57)
        v2 = place("v2", [P, M, 512], 63)
        og = place("og", [P, M, 512], 67)
        qkh = place("qkh", [P, 2, 2, 3, S], 71)
        omix_a = place("omix_a", [P, M, 512], 75)
        omix_r = place("omix_r", [P, M, 512], 71)
        biased = place("biased", [P, KD, S], 44)
        sq_r = place("sq_r", [P, M, 512], 36)
        sq_a = place("sq_a", [P, M, 512], 40)
        merged = place("merged", [P, M, D], 24)
        part = place("part", [P, M, D], 24)
        hT_hi = place("hT_hi", [P, KF2, S], 0, F32R)
        hT_lo = place("hT_lo", [P, KF2, S], 32, F32R)
        part2 = place("part2", [P, M, D], 76)

        pj = ctx.enter_context(nc.psum_tensor("pj", [P, 4, 512], F32))
        aux = ctx.enter_context(nc.psum_tensor("aux", [P, 4, 512], F32))

        named = {}

        def sig(name):
            if name not in named:
                named[name] = ctx.enter_context(nc.semaphore(name))
            return named[name]

        landed = [sig(f"landed{i}") for i in range(RAW)]
        hi_ready = sig("hi_ready")
        lo_ready = sig("lo_ready")
        unit_done = sig("unit_done")

        def width(c):
            return {U_IN + 6: 4 * C0, U_IN + 7: 4 * C0, U_UQ: 2 * H * QK, U_UKV: D, U_LR: KD * P}.get(c, UC)

        def slot(tensor, c, blocks, n):
            return tensor[:, c % tensor.shape[1], 0:blocks * n].rearrange("p (k n) -> p k n", k=blocks)

        def blocks_of(w):
            return w.rearrange("l (k p) n -> p (l k) n", p=P)

        w_gate = [blocks_of(a["ffn1_w_gate"]), blocks_of(a["ffn2_w_gate"])]
        w_up = [blocks_of(a["ffn1_w_up"]), blocks_of(a["ffn2_w_up"])]
        w_down = [blocks_of(a["ffn1_w_down"]), blocks_of(a["ffn2_w_down"])]
        w_in, w_in2 = blocks_of(a["w_in"]), blocks_of(a["w_in_2"])
        w_uq, w_ukv, w_o = blocks_of(a["w_uq"]), blocks_of(a["w_ukv"]), blocks_of(a["w_o"])
        w_ups = [blocks_of(a["w_up_a_2"]), blocks_of(a["w_up_b_2"]), blocks_of(a["w_up_c_2"])]
        w_out, w_1, w_2 = blocks_of(a["w_out_2"]), blocks_of(a["mlp_w1_2"]), blocks_of(a["mlp_w2_2"])
        w_ada = blocks_of(a["ada_w_2"])

        block = ctx.enter_context(nc.Block())

        @block.sync
        def _(sp):
            def load(c, pieces, i=0):
                if c >= RAW or not isinstance(i, int):
                    sp.wait_ge(lo_ready, c + 4 * i - RAW + 1)
                for dst, src in pieces:
                    sp.dma_start(dst, src).then_inc(landed[c % RAW], 16)

            def kind_a(c, w, k0, col, n=512):
                s = slot(raw, c, 4, n)
                return [(s[:, j:j + 2, :], w[:, k0 + j:k0 + j + 2, bass.ds(col, n)]) for j in (0, 2)]

            def kind_b(c, w, k0, n=D):
                s = slot(raw, c, 2, n)
                return [(s[:, j, :], w[:, k0 + j, 0:n]) for j in (0, 1)]

            def ada(k, q, n, i=0):
                sp.wait_ge(sig("ada_free"), n + 1 + 2 * i)
                sp.dma_start(ada_raw[:, q % 2, :], w_ada[:, k + i, q * 1536:(q + 1) * 1536])\
                    .then_inc(sig(f"ada_landed{q % 2}"), 16)

            def ffn(f, u0):
                def chunk_loads(i, with_ada):
                    for w, c in ((w_gate[f], u0), (w_up[f], u0 + 2)):
                        for half in range(2):
                            k0 = 4 * half if with_ada else K_HALVES[f][half]
                            load(c + half, kind_a(c + half, w, k0, 512 * i), i)
                            if with_ada and half == 0:
                                q = (c - u0) // 2
                                ada(4 * f - 1, q, 16 * f - 2 + q, i)

                chunk_loads(0, False)
                if f == 0:
                    vectors()
                with sp.Fori(1, NFULL) as i:
                    chunk_loads(i, True)
                for half in range(2):
                    c = u0 + 4 * NFULL + half
                    s = slot(raw, c, 4, 512)
                    load(c, [(s[:, :, 256 * n:256 * n + 256], w[f][:, 4 * half:4 * half + 4, 512 * NFULL:FF])
                             for n, w in enumerate((w_gate, w_up))])
                for d in range(KF // 2):
                    c = u0 + 4 * NFULL + 2 + d
                    load(c, kind_b(c, w_down[f], 2 * d))
                    if d < 8:
                        ada(4 * f + d // 2, 2 + d % 2, 16 * f + 8 + d)

            def row_load(name, r, n):
                v = a[name]
                axes = " ".join(f"d{i}" for i in range(len(v.shape)))
                flat = v.rearrange(f"{axes} -> ({axes})").rearrange("(r p) -> r p", p=P)
                sp.dma_start(rows[r:r + n, :], flat).then_inc(sig("rows_in"), 16)

            sp.dma_start(x[:, :, :], a["x"].rearrange("b (m p) d -> p (b m) d", p=P)).then_inc(sig("x_in"), 16)
            for name, r, n in ROWS:
                row_load(name, r, n)
            sp.dma_start(pos_i[R_POS:R_POS + M, :], a["positions"].rearrange("b (m p) -> (b m) p", p=P))\
                .then_inc(sig("pos_in"), 16)

            def spread(dst, src, done="spread_in"):
                sp.dma_start(dst, src.partition_broadcast(P)).then_inc(sig(done), 16)

            def vectors():
                spreads()
                sp.wait_ge(sig("gate2_zero"), 1)
                for d in range(2):
                    sp.dma_start(gate2[LR * d:LR * d + LR, d, :], a["gla_gate_w2_2"][0, d, :, :])\
                        .then_inc(sig("gate2_in"), 16)

            def spreads():
                spread(inv[:, :], a["inv_freq"][0, :])
                spread(lgd[:, 0, :], a["ret_decay_fwd"][0, :])
                spread(lgd[:, 1, :], a["ret_decay_bwd"][0, :])
                spread(lamp[:, :, :].rearrange("p a b -> p (a b)"), a["diff_lambda_2"].rearrange("l a b -> (l a b)"))
                spread(headg[:, 0, :], a["hgrn_norm_g_2"][0, :])
                spread(headg[:, 1, :], a["gla_norm_g_2"][0, :])

            ffn(0, U_F1)
            spread(norm_row[:, :], a["final_norm"], "gains_in")
            spread(gt_row[:, 0, :], a["ada_b_2"][0, 2 * D:3 * D], "gains_in")
            spread(gt_row[:, 1, :], a["ada_b_2"][0, 5 * D:6 * D], "gains_in")
            for j, (n, col) in enumerate([(512, C0), (512, C0 + 512), (512, C0 + 1024), (C0, 0), (512, C0 + 1536)]):
                for half in range(2):
                    c = U_IN + 2 * j + half
                    load(c, kind_a(c, w_in, K_HALVES[1][half], col, n))
            load(U_UQ, kind_b(U_UQ, w_uq, 0, H * QK))
            s = raw[:, U_UKV % RAW, :]
            load(U_UKV, [(s[:, n:n + 512], w_ukv[:, 0, n:n + 512]) for n in (0, 512)])
            for d in range(4):
                load(U_O + d, kind_b(U_O + d, w_o, 2 * ((d + 2) % 4)))
            ffn(1, U_F2)
            for j in range(7):
                for half in range(2):
                    c = U_IN2 + 2 * j + half if j < 4 else U_ATT + 2 * (j - 4) + half
                    load(c, kind_a(c, w_in2, 4 * half, 512 * ((j + 3) % 7)))
                if j == 3:
                    s = slot(raw, U_LR, KD, P)
                    load(U_LR, [(s[:, k:k + 4, :], w_in2[:, k:k + 4, C_LR:C_LR + P]) for k in (0, 4)])
            for j in range(6):
                for half in range(2):
                    c = U_GATES + 2 * j + half
                    load(c, kind_a(c, w_in2, 4 * half, C_LR + 2 * LR + 512 * j))
            for c, n, k in ((U_UP, 1, 0), (U_UP + 1, 2, 0), (U_UP + 2, 0, 0), (U_UP + 3, 0, 2)):
                load(c, kind_b(c, w_ups[n], k))
            for d in range(4):
                load(U_OUT + d, kind_b(U_OUT + d, w_out, 2 * ((d + 2) % 4)))
            sp.wait_ge(sig("diff_scored"), DH)
            sp.dma_start(norm_row[:, :], a["final_norm_g_2"].partition_broadcast(P)).then_inc(sig("row2_in"), 16)
            with sp.Fori(0, KF2 // 8) as i:
                for job in range(2):
                    for half in range(2):
                        c = U_W1 + 2 * job + half
                        load(c, kind_a(c, w_1, 4 * half, 1024 * i + 512 * job), i)
            for d in range(KF2 // 2):
                load(U_W2 + d, kind_b(U_W2 + d, w_2, 2 * d))
            sp.wait_ge(sig("y_ready"), 1)
            sp.dma_start(out.rearrange("b (m p) d -> p (b m) d", p=P), x[:, :, :]).then_inc(sig("out_done"), 16)
            sp.wait_ge(sig("out_done"), 16)

        @block.tensor
        def _(pe):
            def three(dst, l_hi, l_lo, r_hi, r_lo, first, last):
                pe.matmul(dst, l_hi, r_hi, start=first, stop=False)
                pe.matmul(dst, l_hi, r_lo, start=False, stop=False)
                return pe.matmul(dst, l_lo, r_hi, start=False, stop=last)

            def unit_a(c, pair, k0, first, last, n=512, i=0, operand=None):
                pe.wait_ge(lo_ready, c + 4 * i + 1)
                hi, lo = slot(w_hi, c, 4, n), slot(w_lo, c, 4, n)
                for m in range(M):
                    for j in range(4):
                        k = k0 + j
                        if operand is not None and m == 0:
                            pe.wait_ge(sig("xT_lo"), operand + j + 1)
                        mm = three(pj[:, 2 * pair + m, 0:n], xT_hi[:, k, m * P:(m + 1) * P],
                                   xT_lo[:, k, m * P:(m + 1) * P], hi[:, j, :], lo[:, j, :],
                                   first and j == 0, last and j == 3)
                mm.then_inc(unit_done, 1)

            def job(c, pair, n=512, halves=K_HALVES[0], t=None):
                unit_a(c, pair, halves[0], True, False, n, operand=None if t is None else KD * t)
                unit_a(c + 1, pair, halves[1], False, True, n, operand=None if t is None else KD * t + 4)

            def unit_b(c, hi_T, lo_T, k0, first, last, free=None, nk=2, n=512, order=(1, 0),
                       operand=None):
                pe.wait_ge(lo_ready, c + 1)
                hi, lo = slot(w_hi, c, nk, 2 * n), slot(w_lo, c, nk, 2 * n)
                for h in order:
                    if free:
                        free(h)
                    for m in range(M):
                        for j in range(nk):
                            k = k0 + j
                            if operand is not None and h == order[0] and m == 0:
                                pe.wait_ge(sig("xT_lo"), operand + j + 1)
                            mm = three(pj[:, 2 * h + m, 0:n], hi_T[:, k, m * P:(m + 1) * P],
                                       lo_T[:, k, m * P:(m + 1) * P], hi[:, j, h * n:(h + 1) * n],
                                       lo[:, j, h * n:(h + 1) * n], first and j == 0, last and j == nk - 1)
                    if h == 1 and last:
                        mm.then_inc(sig("half1"), 1)
                mm.then_inc(unit_done, 1)

            def turn(src, banks=range(4), into=aux):
                for b in banks:
                    for kk_ in range(2):
                        for m in range(M):
                            mm = pe.transpose(into[:, b, kk_ * S + m * P:kk_ * S + (m + 1) * P],
                                              src(2 * b + kk_, m), ident[:, :])
                    mm.then_inc(sig("turned"), 1)

            def turn_xn(first):
                for m in range(M):
                    pe.wait_ge(sig("xn_ready"), first + m)
                    for b in range(4):
                        for k in (2 * b, 2 * b + 1):
                            mm = pe.transpose(aux[:, b, (k % 2) * S + m * P:(k % 2) * S + (m + 1) * P],
                                              xn[:, m, k * P:(k + 1) * P], ident[:, :])
                        if m == M - 1:
                            mm.then_inc(sig("turned"), 1)

            def ffn(f, u0, t_x):
                n = (NFULL + 1) * f

                def hidden_turn(blocks, i):
                    pe.wait_ge(sig("h_ready"), n + i)
                    for j in range(blocks):
                        for m in range(M):
                            mm = pe.transpose(aux[:, j // 2, (j % 2) * S + m * P:(j % 2) * S + (m + 1) * P],
                                              chunk[:, 1, m, j * P:(j + 1) * P], ident[:, :])
                    mm.then_inc(sig("h_turned"), 1)

                def chunk_of(i, first):
                    k_first, k_second = K_HALVES[f if first else 0]
                    if not first:
                        pe.wait_ge(sig("silu_done"), n + i)
                    unit_a(u0, 0, k_first, True, False, i=i, operand=KD * t_x if first else None)
                    if not first:
                        hidden_turn(4, i)
                    unit_a(u0 + 1, 0, k_second, False, True, i=i, operand=KD * t_x + 4 if first else None)
                    unit_a(u0 + 2, 1, k_first, True, False, i=i)
                    unit_a(u0 + 3, 1, k_second, False, True, i=i)

                chunk_of(0, True)
                with pe.Fori(1, NFULL) as i:
                    chunk_of(i, False)
                t = u0 + 4 * NFULL
                pe.wait_ge(sig("silu_done"), n + NFULL)
                unit_a(t, 0, 0, True, False)
                hidden_turn(4, NFULL)
                unit_a(t + 1, 0, 4, False, True)

                def read_out(h):
                    pe.wait_ge(sig("h_ready"), n + NFULL + (h == 0))

                for d in range(KF // 2):
                    if d == 1:
                        hidden_turn(2, NFULL + 1)
                    if f == 1 and d == 7:
                        mod_columns()
                    if f == 1 and d >= 7:
                        gate_rows(d - 7)
                    if d in (0, 2 * NFULL - 2, 2 * NFULL):
                        pe.wait_ge(sig("hT_lo"), n + max(NFULL - 1, d // 2 + 1))
                    unit_b(t + 2 + d, fT_hi, fT_lo, 2 * d, d == 0, d == KF // 2 - 1, read_out if d == 0 else None)

            def mod_columns():
                pe.wait_ge(sig("ada_free"), 2 + 4 * KD)
                for t in range(NMOD * KD):
                    if t // KD in (0, 1, 3, 4):
                        mm = pe.matmul(aux[:, 2, t:t + 1], acc[:, t * P:(t + 1) * P], ones[:, 0:1],
                                       start=True, stop=True)
                mm.then_inc(sig("mod_sum"), 1)

            def gate_rows(n):
                if n:
                    pe.wait_ge(sig("gt_done"), n)
                o = (2 if n < 2 else 5) * D + (n % 2) * 512
                pe.matmul(aux[:, 3, :], ones[:, :], acc[:, o:o + 512], start=True, stop=True)\
                    .then_inc(sig("gt_sum"), 1)

            pe.wait_ge(sig("ident_ready"), 2)
            pe.wait_ge(sig("consts"), 1)
            pe.wait_ge(sig("rows_in"), 16 * len(ROWS))
            pe.wait_ge(sig("pos_row"), 1)
            pe.transpose(pj[:, 0, 0:NROW], rows[:, :], ident[0:NROW, 0:NROW]).then_inc(sig("cols_turned"), 1)

            pe.wait_ge(sig("x_in"), 16)
            turn(lambda k, m: x[:, m, k * P:(k + 1) * P])
            ffn(0, U_F1, 0)

            pe.wait_ge(sig("x_ready"), 1)
            turn(lambda k, m: x[:, m, k * P:(k + 1) * P], (2, 3))
            pe.wait_ge(sig("x_ready"), 2)
            turn(lambda k, m: x[:, m, k * P:(k + 1) * P], (0, 1))
            job(U_IN, 0, 512, K_HALVES[1], 1)
            job(U_IN + 2, 1, halves=K_HALVES[1])
            k_first, k_second = K_HALVES[1]

            def ret_turn(n):
                for g in range(4):
                    for m in range(M):
                        mm = pe.transpose(aux[:, 2 * n + g // 2, (g % 2) * S + m * P:(g % 2) * S + (m + 1) * P],
                                          rqk[:, n, m, g * P:(g + 1) * P], ident[:, :])
                mm.then_inc(sig("ret_turned"), 1)

            def ret_scores(h):
                if h == 0:
                    pe.wait_ge(sig("rqkT_q"), 1)
                    pe.wait_ge(sig("rqkT_k"), 1)
                elif h >= 2:
                    pe.wait_ge(sig("rpT_ready"), h - 1)
                r, g = HD * (h % 2), h // 2
                for jt in range(M):
                    mm = pe.matmul(aux[:, h % 2, jt * S:(jt + 1) * S], rqkT[r:r + HD, 1, g, jt * P:(jt + 1) * P],
                                   rqkT[r:r + HD, 0, g, :], start=True, stop=True)
                mm.then_inc(sig("ret_scored"), 1)

            def ret_values(h):
                pe.wait_ge(sig("rpT_ready"), h + 1)
                if h == 0:
                    pe.wait_ge(sig("rv_ready"), 1)
                for m in range(M):
                    for jt in range(M):
                        mm = pe.matmul(aux[:, 2 + m, h * HD:(h + 1) * HD], rpT[:, h % 2, jt, m * P:(m + 1) * P],
                                       rv[:, jt, h * HD:(h + 1) * HD], start=(jt == 0), stop=(jt == 1))
                mm.then_inc(sig("ret_valued"), 1)

            def ret_step(s):
                if s < H:
                    ret_scores(s)
                if s >= 1:
                    ret_values(s - 1)

            pe.wait_ge(sig("rot"), 1)
            unit_a(U_IN + 4, 0, k_first, True, False)
            ret_turn(0)
            unit_a(U_IN + 5, 0, k_second, False, True)
            pe.wait_ge(sig("rot"), 2)
            ret_turn(1)
            unit_a(U_IN + 6, 1, k_first, True, False, C0)
            ret_step(0)
            unit_a(U_IN + 7, 1, k_second, False, True, C0)
            ret_step(1)
            unit_a(U_IN + 8, 0, k_first, True, False)
            pe.wait_ge(sig("p0_ready"), 1)
            for k in range(3):
                for m in range(M):
                    mm = pe.transpose(pj[:, 2 + k // 2, (k % 2) * S + m * P:(k % 2) * S + (m + 1) * P],
                                      p0[:, m, k * P:(k + 1) * P], ident[:, :])
            mm.then_inc(sig("c_turned"), 1)
            ret_step(2)
            unit_a(U_IN + 9, 0, k_second, False, True)
            ret_step(3)
            ret_step(4)
            pe.wait_ge(sig("cT_lo"), 3)

            def r_g_read(h):
                if h == 0:
                    pe.wait_ge(sig("sgr_ready"), 1)

            unit_b(U_UQ, cT_hi, cT_lo, 0, True, True, r_g_read, n=384)
            ret_step(5)
            ret_step(6)
            ret_step(7)
            ret_step(8)
            pe.wait_ge(sig("qf_ready"), 1)
            unit_b(U_UKV, cT_hi, cT_lo, 2, True, True, nk=1)

            def mla_turn(n, src, ready, value):
                for b in range(4):
                    if b == 0:
                        pe.wait_ge(sig(ready), value)
                    if n:
                        pe.wait_ge(sig("qT_ready"), b + 1)
                    elif b == 2:
                        pe.wait_ge(sig("centred"), 1)
                    for hh in range(2):
                        for m in range(M):
                            h = 2 * b + hh
                            mm = pe.transpose(aux[0:QK, b, hh * S + m * P:hh * S + (m + 1) * P],
                                              src[:, m, h * QK:(h + 1) * QK], ident[:, :])
                    mm.then_inc(sig("mla_turned"), 1)

            pe.wait_ge(sig("rpT_ready"), H)
            mla_turn(0, qf, "q_rot", 1)
            mla_turn(1, kf, "kf_ready", 1)

            pe.wait_ge(sig("kv_ready"), 1)

            def mla_scores(h):
                if h < 2:
                    pe.wait_ge(sig("kT_ready"), 4)
                else:
                    pe.wait_ge(sig("mla_exp"), h - 1)
                for m in range(M):
                    mm = pe.matmul(aux[:, h % 2, m * S:(m + 1) * S], qT[0:QK, h, m * P:(m + 1) * P],
                                   kT[0:QK, h, :], start=True, stop=True)
                mm.then_inc(sig("mla_scored"), 1)

            def mla_prob_turn(h):
                pe.wait_ge(sig("mla_exp"), h + 1)
                if h >= 2:
                    pe.wait_ge(sig("probT_ready"), h - 1)
                for kt in range(M):
                    for m in range(M):
                        mm = pe.transpose(aux[:, 2 + h % 2, kt * S + m * P:kt * S + (m + 1) * P],
                                          prob[:, h % 2, m, kt * P:(kt + 1) * P], ident[:, :])
                mm.then_inc(sig("prob_turned"), 1)

            def mla_values(h):
                pe.wait_ge(sig("probT_ready"), h + 1)
                for m in range(M):
                    for kt in range(M):
                        mm = pe.matmul(pj[:, m, h * VD:(h + 1) * VD], probT[:, h % 2, kt, m * P:(m + 1) * P],
                                       v1[:, kt, h * VD:(h + 1) * VD], start=(kt == 0), stop=(kt == 1))
                mm.then_inc(sig("mla_valued"), 1)

            for s in range(H + 2):
                if s < H:
                    mla_scores(s)
                if 1 <= s <= H:
                    mla_prob_turn(s - 1)
                if s >= 2:
                    mla_values(s - 2)
                if s == H:
                    pe.wait_ge(sig("mix_ready"), 1)
                    turn(lambda k, m: mix_r[:, m, k * P:(k + 1) * P], (0, 1))

            pe.wait_ge(sig("mix_ready"), 2)
            turn(lambda k, m: mix_a[:, m, (k - 4) * P:(k - 3) * P], (2, 3))
            for d in range(4):
                unit_b(U_O + d, xT_hi, xT_lo, 2 * d, d == 0, d == 3, operand=2 * KD + 2 * d)

            pe.wait_ge(sig("x_ready"), 3)
            turn(lambda k, m: x[:, m, k * P:(k + 1) * P], (2, 3))
            pe.wait_ge(sig("x_ready"), 4)
            turn(lambda k, m: x[:, m, k * P:(k + 1) * P], (0, 1))
            ffn(1, U_F2, 3)

            turn_xn(1)
            def blocks_turn(buf, col0, n, banks, value):
                pe.wait_ge(sig("staged"), value)
                for j in range(n):
                    for m in range(M):
                        mm = pe.transpose(aux[:, banks[j // 2], (j % 2) * S + m * P:(j % 2) * S + (m + 1) * P],
                                          chunk[:, buf, m, col0 + j * P:col0 + (j + 1) * P], ident[:, :])
                mm.then_inc(sig("blocks_turned"), 1)

            c = U_IN2
            job(c, 0, t=4)
            job(c + 2, 1)
            blocks_turn(0, 0, 4, (0, 1), 1)
            job(c + 4, 0)
            blocks_turn(1, 0, 2, (2,), 2)
            job(c + 6, 1)
            blocks_turn(0, 0, 2, (3,), 3)
            pe.wait_ge(lo_ready, U_LR + 1)
            pe.wait_ge(sig("turned_read"), 1)
            hi, lo = slot(w_hi, U_LR, KD, P), slot(w_lo, U_LR, KD, P)
            for k in range(KD):
                mm = three(aux[:, 0, 0:S], hi[:, k, :], lo[:, k, :], xT_hi[:, k, :], xT_lo[:, k, :],
                           k == 0, k == KD - 1)
            mm.then_inc(unit_done, 1)
            c = U_ATT
            unit_a(c, 0, 0, True, False)
            pe.wait_ge(sig("lrT_ready"), 1)
            pe.wait_ge(sig("gate2_in"), 32)
            for d in range(2):
                mm = pe.matmul(aux[:, 1, d * S:(d + 1) * S], gate2[0:2 * LR, d, :], lrT[0:2 * LR, :],
                               start=True, stop=True)
            mm.then_inc(sig("gla_z"), 1)
            unit_a(c + 1, 0, 4, False, True)
            pe.wait_ge(sig("staged"), 4)
            unit_a(c + 2, 1, 0, True, False)
            pe.wait_ge(sig("turned_read"), 3)
            blocks_turn(0, 0, 4, (2, 3), 5)
            unit_a(c + 3, 1, 4, False, True)
            unit_a(c + 4, 0, 0, True, False)
            pe.wait_ge(sig("gla_z_read"), 1)
            blocks_turn(1, 0, 4, (0, 1), 6)
            unit_a(c + 5, 0, 4, False, True)

            def diff_scores(h):
                if h:
                    pe.wait_ge(sig("biased"), h)
                for j in range(2):
                    for m in range(M):
                        mm = pe.matmul(aux[:, j, m * S:(m + 1) * S], aqT[64 * j:64 * j + 64, h, m * P:(m + 1) * P],
                                       akT[64 * j:64 * j + 64, h, :], start=True, stop=True)
                mm.then_inc(sig("diff_scored"), 1)

            def diff_turn(h):
                pe.wait_ge(sig("diff_w"), h + 1)
                if h:
                    pe.wait_ge(sig("dmapT_ready"), h)
                else:
                    pe.wait_ge(sig("rec_copied"), 1)
                for kt in range(M):
                    for m in range(M):
                        mm = pe.transpose(aux[:, 2, kt * S + m * P:kt * S + (m + 1) * P],
                                          dmap[:, 0, m, kt * P:(kt + 1) * P], ident[:, :])
                mm.then_inc(sig("diff_turned"), 1)

            def diff_values(h):
                pe.wait_ge(sig("dmapT_ready"), h + 1)
                if h:
                    pe.wait_ge(sig("oa_copied"), h)
                for m in range(M):
                    for kt in range(M):
                        mm = pe.matmul(aux[:, 3, m * P:(m + 1) * P], dmapT[:, kt, m * P:(m + 1) * P],
                                       av[:, kt, h * P:(h + 1) * P], start=(kt == 0), stop=(kt == 1))
                mm.then_inc(sig("diff_valued"), 1)

            def level_scores(n):
                pe.wait_ge(sig("qk_ready"), n + 1)
                if n == 0:
                    pe.wait_ge(sig("turned_read"), 5)
                else:
                    pe.wait_ge(sig("level_read"), n)
                for hh in HEAD_ORDER:
                    bank, kind, g, r, kd = head_place(hh)
                    for m in range(M):
                        km = 1 - m if n == LEVELS - 1 else m
                        col = kind * S + m * P
                        mm = pe.matmul(aux[:, bank, col:col + P], qkh[r:r + kd, n % 2, 1, g, km * P:(km + 1) * P],
                                       qkh[r:r + kd, n % 2, 0, g, m * P:(m + 1) * P], start=True, stop=True)
                mm.then_inc(sig("level_scored"), 1)

            def rec_values():
                pe.wait_ge(sig("far_ready"), 1)
                for hh in HEAD_ORDER:
                    bank, kind, g, r, kd = head_place(hh)
                    for m in range(M):
                        col = kind * S + m * P
                        dst = aux[:, 2 + m, hh * HD:(hh + 1) * HD]
                        pe.matmul(dst, near[:, bank, col:col + P], v2[:, m, hh * HD:(hh + 1) * HD],
                                  start=True, stop=False)
                        mm = pe.matmul(dst, far[:, bank, col:col + P], v2[:, 1 - m, hh * HD:(hh + 1) * HD],
                                       start=False, stop=True)
                mm.then_inc(sig("rec_valued"), 1)

            def gate_unit(s):
                j = s // 2
                if s == 0:
                    pe.wait_ge(sig("staged"), 6)
                elif s == 2:
                    pe.wait_ge(sig("staged"), 7)
                elif s % 2 == 0:
                    pe.wait_ge(sig("gates_raw"), j - 1)
                unit_a(U_GATES + s, (j + 1) % 2, 4 * (s % 2), s % 2 == 0, s % 2 == 1)

            level_scores(0)
            for s in range(12):
                gate_unit(s)
                if s + 1 < LEVELS:
                    level_scores(s + 1)
                else:
                    h = s + 1 - LEVELS
                    if h == 0:
                        rec_values()
                    diff_scores(h)
                    if h == DH - 1:
                        pe.wait_ge(sig("omix_ready"), 1)
                        pe.wait_ge(sig("gates_raw"), 5)
                        turn(lambda k, m: omix_r[:, m, k * P:(k + 1) * P], (0, 1), pj[:, 2:4, :])
                    if h >= 1:
                        diff_turn(h - 1)
                    if h >= 2:
                        diff_values(h - 2)
            assert 12 - LEVELS == DH - 1

            pe.wait_ge(sig("gates_raw"), 6)

            def branch_free(n):
                def free(h):
                    if n:
                        pe.wait_ge(sig("branch_read"), 2 * n - 1 if h else 2 * n)
                return free

            pe.wait_ge(sig("xT_lo"), 5 * KD + 4)
            unit_b(U_UP, xT_hi, xT_lo, 0, True, True)
            diff_turn(DH - 1)
            diff_values(DH - 2)
            diff_values(DH - 1)
            unit_b(U_UP + 1, xT_hi, xT_lo, 2, True, True, branch_free(1))
            pe.wait_ge(sig("omix_ready"), 2)
            turn(lambda k, m: omix_a[:, m, (k - 4) * P:(k - 3) * P], (2, 3))
            unit_b(U_UP + 2, xT_hi, xT_lo, 4, True, False, branch_free(2), operand=5 * KD + 4)
            unit_b(U_UP + 3, xT_hi, xT_lo, 6, False, True, operand=5 * KD + 6)
            pe.wait_ge(sig("merged"), 1)
            turn(lambda k, m: merged[:, m, k * P:(k + 1) * P], (2, 3))
            for d in range(4):
                if d == 1:
                    pe.wait_ge(sig("merged"), 2)
                    turn(lambda k, m: merged[:, m, k * P:(k + 1) * P], (0, 1))
                unit_b(U_OUT + d, xT_hi, xT_lo, 2 * ((d + 2) % 4), d == 0, d == 3,
                       (lambda h: pe.wait_ge(sig("branch_read"), 6 - h)) if d == 0 else None,
                       operand=6 * KD + 2 * d)

            turn_xn(3)

            def mlp_turn(par, i, n):
                pe.wait_ge(sig("sq_ready"), n + 2 * i)
                for j in range(4):
                    for m in range(M):
                        mm = pe.transpose(aux[:, 2 * par + j // 2, (j % 2) * S + m * P:(j % 2) * S + (m + 1) * P],
                                          chunk[:, par, m, j * P:(j + 1) * P], ident[:, :])
                mm.then_inc(sig("sq_turned"), 1)

            def mlp_jobs(i, first):
                for par in range(2):
                    c = U_W1 + 2 * par
                    prev = not (first and par == 0)
                    unit_a(c, par, 0, True, False, i=i, operand=None if prev else 7 * KD)
                    if prev:
                        mlp_turn(1 - par, i, par)
                    unit_a(c + 1, par, 4, False, True, i=i, operand=None if prev else 7 * KD + 4)

            mlp_jobs(0, True)
            with pe.Fori(1, KF2 // 8) as i:
                mlp_jobs(i, False)
            for d in range(KF2 // 2):
                if d == 1:
                    mlp_turn(1, 0, KF2 // 4)
                if d in (0, KF2 // 2 - 4, KF2 // 2 - 2):
                    pe.wait_ge(sig("sqT_lo"), max(KF2 // 4 - 2, d // 2 + 1))
                unit_b(U_W2 + d, hT_hi, hT_lo, 2 * d, d == 0, d == KF2 // 2 - 1,
                       (lambda h: pe.wait_ge(sig("relu_done"), KF2 // 4 - 1 + h)) if d == 0 else None,
                       order=(0, 1) if d == 0 else (1, 0))

        @block.scalar
        def _(act):
            steps = [0]

            def step(ins):
                steps[0] += 1
                ins.then_inc(sig("act_step"), 1)

            def settle():
                act.wait_ge(sig("act_step"), steps[0])

            def split(c, i=0):
                act.wait_ge(landed[c % RAW], 32 * (c // RAW + 1) + 32 * i)
                if c >= SPLIT or not isinstance(i, int):
                    act.wait_ge(unit_done, c + 4 * i - SPLIT + 1)
                n = width(c)
                act.activation(w_hi[:, c % SPLIT, 0:n], raw[:, c % RAW, 0:n], ACT.Copy).then_inc(hi_ready, 1)

            def operand(t, gain=None, bias=None, order=(0, 1, 2, 3), start=0, at_=aux):
                for n, b in enumerate(order, start):
                    act.wait_ge(sig("turned"), 4 * t + n + 1)
                    for k in (2 * b, 2 * b + 1):
                        src, dst = at_[:, b, (k % 2) * S:(k % 2 + 1) * S], xT_hi[:, k, :]
                        if bias is not None:
                            act.activation(biased[:, k, :], src, ACT.Identity, bias=bias[:, k:k + 1],
                                           scale=gain[:, k:k + 1]).then_inc(sig("biased_ready"), 1)
                            continue
                        if gain is not None:
                            ins = act.activation(dst, src, ACT.Copy, scale=gain[:, k:k + 1])
                        else:
                            ins = act.activation(dst, src, ACT.Copy)
                        ins.then_inc(sig("xT_hi"), 1)

            def squares(h, to=scratch):
                for m in range(M):
                    ins = act.activation(to[:, m, 512 * h:512 * h + 512], x[:, m, 512 * h:512 * h + 512],
                                         ACT.Square, accum_out=ss[:, 0, h, m:m + 1])
                return ins

            def root(n, src, dst=rms):
                act.wait_ge(sig("ss_ready"), n + 1)
                act.activation(dst[:, :], src, ACT.Sqrt, bias=eps[:, 0:1], scale=1.0 / D)\
                    .then_inc(sig("rms_ready"), 1)

            def stats(n):
                if n:
                    act.wait_ge(sig("ss_ready"), n)
                squares(1, xn)
                squares(0, xn).then_inc(sig("squared"), 1)
                root(n, tot[:, 0, :])

            def load_sqrt():
                act.activation(root_of_one[:, :], one[:, :], ACT.Sqrt)

            def stats_by_half(n, ready):
                load_sqrt()
                act.wait_ge(sig("x_ready"), ready)
                squares(1)
                act.wait_ge(sig("x_ready"), ready + 1)
                squares(0).then_inc(sig("squared"), 1)
                root(n, tot[:, 0, :])

            def ffn(f, u0, t_stats, between=None):
                n = (NFULL + 1) * f

                def silu(i, cols=512):
                    for m in range(M):
                        ins = act.activation(chunk[:, 0, m, 0:cols], pj[:, m, 0:cols], ACT.Silu,
                                             scale=rstd[:, m:m + 1])
                    ins.then_inc(sig("silu_done"), 1)

                def hidden(blocks, i):
                    act.wait_ge(sig("h_turned"), n + i)
                    start = 4 * i - 4
                    act.activation(fT_hi[:, bass.ds(start, blocks), :],
                                   aux[:, 0:2, :].rearrange("p b (k s) -> p (b k) s", k=2)[:, 0:blocks, :],
                                   ACT.Copy).then_inc(sig("hT_hi"), 1)

                split(u0 + 1)
                stats(t_stats)
                for n_, c in enumerate((u0 + 2, u0 + 3)):
                    if between:
                        between[n_]()
                    split(c)
                act.wait_ge(sig("rstd_ready"), t_stats + 1)
                silu(0)
                with act.Fori(1, NFULL) as i:
                    split(u0, i)
                    split(u0 + 1, i)
                    split(u0 + 2, i)
                    hidden(4, i)
                    split(u0 + 3, i)
                    act.wait_ge(sig("h_ready"), n + i)
                    silu(i)
                t = u0 + 4 * NFULL
                split(t)
                split(t + 1)
                hidden(4, NFULL)
                split(t + 2)
                act.wait_ge(unit_done, t + 2)
                act.wait_ge(sig("h_ready"), n + NFULL)
                silu(NFULL, 256)
                split(t + 3)
                hidden(2, NFULL + 1)
                for d in range(2, KF // 2):
                    split(t + 2 + d)

            act.wait_ge(sig("consts"), 1)
            act.wait_ge(sig("cols_ready"), 1)
            act.activation(cond[:, :], cols[:, R_C:R_C + KD], ACT.Silu).then_inc(sig("cond_ready"), 1)
            operand(0, cols[:, R_G1:R_G1 + KD], order=(0, 1))
            split(U_F1)
            operand(0, cols[:, R_G1:R_G1 + KD], order=(2, 3), start=2)

            def sines():
                act.wait_ge(sig("angles"), 1)
                ins = act.activation(trig[:, :, :, :].rearrange("p a m n -> p (a m n)"),
                                    ang[:, :, :, :].rearrange("p a m n -> p (a m n)"), ACT.Sin)
                ins.then_inc(sig("trig_ready"), 1)

            def logs():
                act.wait_ge(sig("logs_in"), 1)
                step(act.activation(lgt[:, :, :], lgt[:, :, :], ACT.Exp, scale=-1.0))
                step(act.activation(lams[:, 0:2], lams[:, 0:2], ACT.Exp))
                step(act.activation(lbt[:, :, :], lbt[:, :, :], ACT.Exp))
                settle()
                act.activation(lgt[:, :, :], lgt[:, :, :], ACT.Ln, bias=one[:, 0:1]).then_inc(sig("logs_out"), 1)

            ffn(0, U_F1, 0, (sines, logs))

            split(U_IN)
            operand(1, cols[:, R_MIX:R_MIX + KD], order=(2, 3, 0, 1))
            split(U_IN + 1)
            stats(1)
            split(U_IN + 2)
            split(U_IN + 3)

            def decay_exp(h):
                act.wait_ge(sig("decay_log"), h + 1)
                act.activation(decay[:, h % 2, :], decay[:, h % 2, :], ACT.Exp).then_inc(sig("decay_ready"), 1)

            split(U_IN + 4)
            split(U_IN + 5)
            act.wait_ge(sig("ret_turned"), 1)
            act.activation(rqkT[:, 0, :, :].rearrange("p g s -> p (g s)"),
                           aux[:, 0:2, :].rearrange("p b n -> p (b n)"), ACT.Copy).then_inc(sig("rqkT_q"), 1)
            split(U_IN + 6)
            act.wait_ge(unit_done, U_IN + 6)
            for m in range(M):
                ins = act.activation(rv[:, m, :], pj[:, m, :], ACT.Copy, scale=rstd[:, m:m + 1])
            ins.then_inc(sig("rv_ready"), 1)
            decay_exp(0)
            split(U_IN + 7)
            decay_exp(1)
            split(U_IN + 8)
            act.wait_ge(unit_done, U_IN + 8)
            for m in range(M):
                ins = act.activation(p0[:, m, :], pj[:, 2 + m, 0:C0], ACT.Copy, scale=rstd[:, m:m + 1])
            ins.then_inc(sig("p0_ready"), 1)
            act.wait_ge(sig("p0_ready"), 1)
            for m in range(M):
                step(act.activation(sgr[:, m, 0:QR], p0[:, m, 0:QR], ACT.Square, accum_out=cs[:, m, 0:1]))
                step(act.activation(sgr[:, m, QR:QR + KVR], p0[:, m, QR:QR + KVR], ACT.Square,
                                    accum_out=cs[:, m, 1:2]))
            settle()
            step(act.activation(crms[:, :, 0], cs[:, :, 0], ACT.Sqrt, bias=eps[:, 0:1], scale=1.0 / QR))
            act.activation(crms[:, :, 1], cs[:, :, 1], ACT.Sqrt, bias=eps[:, 0:1], scale=1.0 / KVR)\
                .then_inc(sig("crms_ready"), 1)
            decay_exp(2)
            split(U_IN + 9)
            act.wait_ge(sig("c_turned"), 1)
            for k in range(3):
                act.activation(cT_hi[:, k, :], pj[:, 2 + k // 2, (k % 2) * S:(k % 2 + 1) * S], ACT.Copy,
                               scale=cols[:, R_Q + k:R_Q + k + 1]).then_inc(sig("cT_hi"), 1)
            decay_exp(3)
            split(U_UQ)
            decay_exp(4)
            act.wait_ge(unit_done, U_UQ)
            for m in range(M):
                ins = act.activation(sgr[:, m, :], pj[:, m, :], ACT.Silu, scale=rstd[:, m:m + 1])
            ins.then_inc(sig("sgr_ready"), 1)
            split(U_UKV)
            decay_exp(5)
            act.wait_ge(sig("crstd_ready"), 1)
            act.wait_ge(unit_done, U_UKV)
            for m in range(M):
                ins = act.activation(qf[:, m, :].rearrange("p (h n) -> p h n", h=2), pj[:, m:4:2, 0:384], ACT.Copy,
                                    scale=crstd[:, m, 0:1])
            ins.then_inc(sig("qf_ready"), 1)
            decay_exp(6)
            decay_exp(7)
            act.wait_ge(unit_done, U_O)
            for m in range(M):
                src = pj[:, m:4:2, :].rearrange("p a (h n) -> p a h n", n=P)
                kdst = kf[:, m, :].rearrange("p (a h n) -> p a h n", a=2, n=QK)[:, :, :, 0:NOPE]
                vdst = v1[:, m, :].rearrange("p (a h n) -> p a h n", a=2, n=VD)
                ins = act.activation(kdst, src[:, :, :, 0:NOPE], ACT.Copy, scale=crstd[:, m, 1:2])
                ins = act.activation(vdst, src[:, :, :, NOPE:P], ACT.Copy, scale=crstd[:, m, 1:2])
            ins.then_inc(sig("kv_ready"), 1)
            for b in range(4):
                act.wait_ge(sig("mla_turned"), b + 1)
                act.activation(qT[0:QK, 2 * b:2 * b + 2, :].rearrange("p h s -> p (h s)"), aux[0:QK, b, :], ACT.Copy)\
                    .then_inc(sig("qT_ready"), 1)
            act.wait_ge(sig("centred"), 1)
            act.activation(tmp_r[:, :, :, :].rearrange("p a m s -> p (a m s)"),
                           mix_r[:, :, :].rearrange("p m n -> p (m n)"), ACT.Square).then_inc(sig("gn_square"), 1)
            act.wait_ge(sig("gvar_ready"), 1)
            act.activation(grms[:, :, :], gvar[:, :, :], ACT.Sqrt, bias=eps[:, 0:1], scale=1.0 / HD)\
                .then_inc(sig("grms_ready"), 1)
            for h in range(H):
                act.wait_ge(sig("mla_max"), h + 1)
                if h >= 2:
                    act.wait_ge(sig("prob_turned"), h - 1)
                for m in range(M):
                    ins = act.activation(prob[:, h % 2, m, :], aux[:, h % 2, m * S:(m + 1) * S], ACT.Exp,
                                         bias=mx[:, h % 2, m:m + 1], accum_out=rowsum[:, m, h:h + 1])
                ins.then_inc(sig("mla_exp"), 1)
                if h in (1, 4):
                    split(U_O + h // 4)
            operand(2, order=(0, 1))
            operand(2, order=(2, 3), start=2)
            split(U_O + 2)
            split(U_O + 3)

            split(U_F2)
            operand(3, cols[:, R_G2:R_G2 + KD], order=(2, 3, 0, 1))
            ffn(1, U_F2, 2)

            split(U_IN2)
            def gained_squares(h):
                for m in range(M):
                    ins_ = act.activation(scratch2[:, m, :], xn[:, m, 512 * h:512 * h + 512], ACT.Square,
                                          accum_out=ss[:, 1, h, m:m + 1])
                return ins_

            load_sqrt()
            act.wait_ge(sig("x_ready"), 5)
            squares(1)
            act.wait_ge(sig("xg_ready"), 1)
            step(gained_squares(1))
            act.wait_ge(sig("x_ready"), 6)
            squares(0)
            act.wait_ge(sig("xg_ready"), 2)
            settle()
            gained_squares(0).then_inc(sig("squared"), 1)
            act.wait_ge(sig("ss_ready"), 4)
            act.activation(rms2[:, :, :], ms[:, :, :], ACT.Sqrt).then_inc(sig("rms_ready"), 1)
            operand(4, scale_m[:, :], modc[:, 0, :])
            split(U_IN2 + 1)

            def stage(dst, pair, c0, c1, func=ACT.Copy):
                return act.activation(dst, pj[:, 2 * pair:2 * pair + 2, c0:c1], func)

            def softplus(g):
                act.wait_ge(sig("abs_z"), 1 if g.start == 0 else 2)
                step(act.activation(ee[:, :, g, :], ee[:, :, g, :], ACT.Exp, scale=-1.0))
                settle()
                act.activation(ee[:, :, g, :], ee[:, :, g, :], ACT.Ln, bias=one[:, 0:1])\
                    .then_inc(sig("softplus"), 1)

            c = U_IN2
            split(c + 2)
            split(c + 3)
            ins = stage(chunk[:, 0, :, :], 0, 0, 512)
            ins.then_inc(sig("staged"), 1)
            split(c + 4)
            split(c + 5)
            ins = stage(chunk[:, 1, :, 0:S], 1, 0, S)
            ins = stage(v2[:, :, 0:S], 1, S, 2 * S)
            ins.then_inc(sig("staged"), 1)
            act.wait_ge(sig("blocks_turned"), 1)
            act.activation(qt[:, 0:2, :].rearrange("p g s -> p (g s)"), aux[:, 0, :], ACT.Silu)\
                .then_inc(sig("q_silu"), 1)
            split(c + 6)
            split(c + 7)
            ins = stage(og[:, :, 0:S], 0, 0, S, ACT.Silu)
            ins = stage(chunk[:, 0, :, 0:S], 0, S, 2 * S)
            ins.then_inc(sig("staged"), 1)
            split(U_LR)
            softplus(slice(0, 2))
            split(U_ATT)
            ins = stage(v2[:, :, S:2 * S], 1, 0, S)
            ins = stage(og[:, :, S:2 * S], 1, S, 2 * S, ACT.Silu)
            ins.then_inc(sig("staged"), 1)
            split(U_ATT + 1)
            act.activation(lrT[:, :], aux[0:2 * LR, 0, 0:S], ACT.Copy).then_inc(sig("lrT_ready"), 1)
            act.wait_ge(sig("log_k"), 1)
            ins = act.activation(kk[:, :, 0:2, :], kk[:, :, 0:2, :], ACT.Exp)
            ins = act.activation(ee[:, :, 0:2, :], ee[:, :, 0:2, :], ACT.Exp)
            ins.then_inc(sig("k_exp"), 1)
            act.wait_ge(sig("lb_term"), 1)
            act.activation(ee[:, :, 0:2, :], ee[:, :, 0:2, :], ACT.Ln, bias=one[:, 0:1]).then_inc(sig("lb_log"), 1)
            split(U_ATT + 2)
            act.wait_ge(sig("gla_z"), 1)
            for d in range(2):
                ins = act.activation(zz[:, d, 2, :], aux[:, 1, d * S:(d + 1) * S], ACT.Identity,
                                    bias=cols[:, R_GB + d:R_GB + d + 1])
            ins.then_inc(sig("gla_z_read"), 1)

            def diff_exp(h):
                act.wait_ge(sig("diff_max"), h + 1)
                for j in range(2):
                    for m in range(M):
                        ins = act.activation(dmap[:, j, m, :], dmap[:, j, m, :], ACT.Exp, bias=dl[:, j, m:m + 1],
                                            accum_out=dr[:, j, m:m + 1])
                ins.then_inc(sig("diff_exp"), 1)

            def diff_copies(h):
                act.wait_ge(sig("diff_turned"), h + 1)
                if h:
                    act.wait_ge(sig("diff_valued"), h)
                act.activation(dmapT[:, :, :].rearrange("p k s -> p (k s)"), aux[:, 2, :], ACT.Copy)\
                    .then_inc(sig("dmapT_ready"), 1)

            def diff_out(h):
                act.wait_ge(sig("diff_valued"), h + 1)
                act.activation(omix_a[:, :, h * P:(h + 1) * P], aux[:, 3, 0:S].rearrange("p (m n) -> p m n", m=2),
                               ACT.Copy).then_inc(sig("oa_copied"), 1)

            def gates_copy(j):
                act.activation(gates[:, :, j * 512:(j + 1) * 512],
                               pj[:, 2 * ((j + 1) % 2):2 * ((j + 1) % 2) + 2, :], ACT.Copy)\
                    .then_inc(sig("gates_raw"), 1)

            def halves(t, lvl):
                v = t.rearrange("p g (b e n) -> p (g b) e n", e=2, n=2 ** (lvl - 1))
                return v[:, :, 0, :], v[:, :, 1, :]

            def level_exps(lvl):
                act.wait_ge(sig("sums_ready"), lvl)
                if lvl == 1:
                    act.wait_ge(sig("xx_zero"), 1)
                if lvl >= 2:
                    act.wait_ge(sig("qk_ready"), lvl)
                qe, ke = eqk[:, 0, :, :], eqk[:, 1, :, :]
                (pf_l, pf_r), (sb_l, sb_r) = halves(ll[:, 0, :, :], lvl), halves(ll[:, 1, :, :], lvl)
                (sf_l, sf_r), (pb_l, pb_r) = halves(xx[:, 0, :, :], lvl), halves(xx[:, 1, :, :], lvl)
                (q_l, q_r), (k_l, k_r) = halves(qe, lvl), halves(ke, lvl)
                for dst, src in ((q_r, pf_r), (q_l, sb_l), (k_l, sf_l), (k_r, pb_r)):
                    ins = act.activation(dst, src, ACT.Exp)
                ins.then_inc(sig("exps_ready"), 1)

            split(U_ATT + 3)
            act.wait_ge(sig("blocks_turned"), 3)
            stage(chunk[:, 0, :, :], 0, 0, 512).then_inc(sig("staged"), 1)
            softplus(slice(2, 3))
            split(U_ATT + 4)
            split(U_ATT + 5)
            stage(chunk[:, 1, :, :], 1, 0, 512).then_inc(sig("staged"), 1)
            for lvl in range(1, LEVELS):
                level_exps(lvl)
                split(U_GATES + lvl - 1)
                if lvl == 2:
                    stage(av[:, :, :], 0, 0, 512).then_inc(sig("staged"), 1)
                elif lvl % 2 == 0:
                    gates_copy(lvl // 2 - 2)
            split(U_GATES + 8)
            act.wait_ge(sig("level_scored"), LEVELS)
            for n in range(2):
                ins = act.activation(far[:, 2 * n:2 * n + 2, :], aux[:, 2 * n:2 * n + 2, :], ACT.Copy)
            ins.then_inc(sig("far_ready"), 1)
            split(U_GATES + 9)
            gates_copy(3)
            split(U_GATES + 10)
            diff_exp(0)
            act.wait_ge(sig("rec_valued"), 1)
            act.activation(omix_r[:, :, :], aux[:, 2:4, :], ACT.Copy).then_inc(sig("rec_copied"), 1)
            act.wait_ge(sig("rec_copied"), 1)
            act.activation(sq_r[:, :, :], omix_r[:, :, :], ACT.Square).then_inc(sig("head_square"), 1)
            split(U_GATES + 11)
            diff_copies(0)
            diff_exp(1)
            act.wait_ge(unit_done, U_GATES + 10)
            gates_copy(4)
            diff_copies(1)
            diff_out(0)
            diff_exp(2)
            act.wait_ge(sig("head_sums"), 1)
            act.activation(rinv[:, :, :], gsum[:, :, :], ACT.Sqrt, bias=eps[:, 0:1], scale=1.0 / HD)\
                .then_inc(sig("head_rms"), 1)
            split(U_UP)
            act.wait_ge(unit_done, U_UP)
            gates_copy(5)
            operand(5, order=(0, 1), at_=pj[:, 2:4, :])

            def sigmoid(n):
                v = gates[:, :, n * D:(n + 1) * D]
                act.activation(v, v, ACT.Sigmoid).then_inc(sig("gates_ready"), 1)

            act.wait_ge(sig("gates_raw"), 6)
            sigmoid(1)
            sigmoid(2)
            diff_copies(2)
            diff_exp(3)
            diff_out(1)
            split(U_UP + 1)
            diff_copies(3)
            diff_out(2)
            diff_out(3)
            act.wait_ge(sig("oa_copied"), DH)
            act.activation(sq_a[:, :, :], omix_a[:, :, :], ACT.Square).then_inc(sig("head_square"), 1)
            load_sqrt()
            act.wait_ge(sig("head_sums"), 2)
            act.activation(grms[:, :, 0:DH], gvar[:, :, 0:DH], ACT.Sqrt, bias=eps[:, 0:1], scale=1.0 / P)\
                .then_inc(sig("head_rms"), 1)
            split(U_UP + 2)
            operand(5, subg, order=(2, 3), start=2)
            split(U_UP + 3)
            sigmoid(0)
            split(U_OUT)
            operand(6, order=(2, 3))
            split(U_OUT + 1)
            operand(6, order=(0, 1), start=2)
            split(U_OUT + 2)
            split(U_OUT + 3)

            split(U_W1)
            stats_by_half(4, 7)
            operand(7, scale_f[:, :], modc[:, 3, :])
            split(U_W1 + 1)

            def relu(par):
                act.activation(chunk[:, par, :, :], pj[:, 2 * par:2 * par + 2, :], ACT.Relu)\
                    .then_inc(sig("relu_done"), 1)

            def sq_hi(par, i, n):
                act.wait_ge(sig("sq_turned"), n + 2 * i)
                act.activation(hT_hi[:, bass.ds(4 * (n + 2 * i) - 4, 4), :],
                               aux[:, 2 * par:2 * par + 2, :].rearrange("p b (k s) -> p (b k) s", k=2),
                               ACT.Copy).then_inc(sig("sqT_hi"), 1)

            def mlp_pair(i, first):
                for par in range(2):
                    c = U_W1 + 2 * par
                    if not (first and par == 0):
                        split(c, i)
                        act.wait_ge(unit_done, c + 4 * i)
                        if not (first and par == 1):
                            act.wait_ge(sig("sq_turned"), 2 * i + par - 1)
                        relu(1 - par)
                        split(c + 1, i)
                        sq_hi(1 - par, i, par)

            mlp_pair(0, True)
            with act.Fori(1, KF2 // 8) as i:
                mlp_pair(i, False)
            split(U_W2)
            act.wait_ge(unit_done, U_W2)
            act.wait_ge(sig("sq_turned"), KF2 // 4 - 1)
            relu(1)
            split(U_W2 + 1)
            sq_hi(1, 0, KF2 // 4)
            for d in range(2, KF2 // 2):
                split(U_W2 + d)
            stats_by_half(5, 9)

        @block.vector
        def _(dve):
            steps = [0]

            def step(ins):
                steps[0] += 1
                ins.then_inc(sig("dve_step"), 1)

            def settle():
                dve.wait_ge(sig("dve_step"), steps[0])

            def split(c, i=0):
                dve.wait_ge(hi_ready, c + 4 * i + 1)
                n = width(c)
                dve.tensor_tensor(w_lo[:, c % SPLIT, 0:n], raw[:, c % RAW, 0:n],
                                  w_hi[:, c % SPLIT, 0:n].bitcast(F32), ALU.subtract).then_inc(lo_ready, 1)

            def operand(t, gain=None, bias=False, order=(0, 1, 2, 3), start=0, at_=aux):
                n = 2 * start
                for b in order:
                    n += 2
                    ks = (2 * b, 2 * b + 1)
                    if bias:
                        dve.wait_ge(sig("biased_ready"), n if t == 4 else KD + n)
                        for k in ks:
                            dve.tensor_copy(xT_hi[:, k, :], biased[:, k, :]).then_inc(sig("xT_hi"), 1)
                    dve.wait_ge(sig("xT_hi"), KD * t + n)
                    for k in ks:
                        src = at_[:, b, (k % 2) * S:(k % 2 + 1) * S]
                        hi, dst = xT_hi[:, k, :].bitcast(F32), xT_lo[:, k, :]
                        if bias:
                            ins = dve.tensor_tensor(dst, biased[:, k, :], hi, ALU.subtract)
                        elif gain is not None:
                            ins = dve.scalar_tensor_tensor(dst, src, gain[:, k:k + 1], hi, ALU.mult, ALU.subtract)
                        else:
                            ins = dve.tensor_tensor(dst, src, hi, ALU.subtract)
                        ins.then_inc(sig("xT_lo"), 1)

            def rstd_of(n):
                dve.wait_ge(sig("squared"), n + 1)
                dve.tensor_tensor(tot[:, 0, :], ss[:, 0, 0, :], ss[:, 0, 1, :], ALU.add).then_inc(sig("ss_ready"), 1)
                dve.wait_ge(sig("rms_ready"), n + 1)
                dve.reciprocal(rstd[:, :], rms[:, :]).then_inc(sig("rstd_ready"), 1)

            def halves_of_x(h):
                return x[:, :, 512 * h:512 * h + 512], pj[:, 2 * h:2 * h + 2, :]

            def residual(n_half1, last_unit, factor, then=None):
                for h in (1, 0):
                    if h:
                        dve.wait_ge(sig("half1"), n_half1)
                    else:
                        dve.wait_ge(unit_done, last_unit + 1)
                    dst, src = halves_of_x(h)
                    dve.scalar_tensor_tensor(dst, src, factor, dst, ALU.mult, ALU.add).then_inc(sig("x_ready"), 1)
                    if then:
                        then(h)

            def modulation():
                dve.wait_ge(sig("mod_sum"), 1)
                for g in (0, 3):
                    ins = dve.tensor_tensor(modc[:, g:g + 2, :].rearrange("p g k -> p (g k)"),
                                            aux[:, 2, KD * g:KD * (g + 2)],
                                            cols[:, R_ADAB + KD * g:R_ADAB + KD * (g + 2)], ALU.add)
                step(ins)
                settle()
                for dst, g, r in ((scale_m, 1, R_GM2), (scale_f, 4, R_GF2)):
                    dve.scalar_tensor_tensor(dst[:, :], modc[:, g, :], 1.0, cols[:, r:r + KD], ALU.add, ALU.mult)

            def gate_rows(n):
                dve.wait_ge(sig("gains_in"), 16 * 3)
                dve.wait_ge(sig("gt_sum"), n + 1)
                dst = gt_row[:, n // 2, (n % 2) * 512:(n % 2) * 512 + 512]
                dve.tensor_tensor(dst, dst, aux[:, 3, :], ALU.add).then_inc(sig("gt_done"), 1)

            def ffn(f, u0, t_stats, between=None):
                n = (NFULL + 1) * f

                def product(i, cols=512, c0=0, pair=1):
                    dve.wait_ge(sig("silu_done"), n + i)
                    for m in range(M):
                        ins = dve.scalar_tensor_tensor(chunk[:, 1, m, 0:cols], pj[:, 2 * pair + m, c0:c0 + cols],
                                                       rstd[:, m:m + 1], chunk[:, 0, m, 0:cols], ALU.mult, ALU.mult)
                    ins.then_inc(sig("h_ready"), 1)

                def hidden(blocks, i):
                    dve.wait_ge(sig("hT_hi"), n + i)
                    start = 4 * i - 4
                    dve.tensor_tensor(fT_lo[:, bass.ds(start, blocks), :],
                                      aux[:, 0:2, :].rearrange("p b (k s) -> p (b k) s", k=2)[:, 0:blocks, :],
                                      fT_hi[:, bass.ds(start, blocks), :].bitcast(F32),
                                      ALU.subtract).then_inc(sig("hT_lo"), 1)

                def ada(q, k, count):
                    dve.wait_ge(sig(f"ada_landed{q % 2}"), 16 * count)
                    dst = acc[:, q * 1536:(q + 1) * 1536]
                    dve.scalar_tensor_tensor(dst, ada_raw[:, q % 2, :], cond[:, bass.ds(k, 1)], dst,
                                             ALU.mult, ALU.add).then_inc(sig("ada_free"), 1)

                def ada_tail(j):
                    ada(2 + j % 2, 4 * f + j // 2, 8 * f + 5 + j // 2)

                split(u0 + 1)
                rstd_of(t_stats)
                for n_, c in enumerate((u0 + 2, u0 + 3)):
                    if between:
                        between[n_]()
                    split(c)
                if between:
                    between[2]()
                with dve.Fori(1, NFULL) as i:
                    split(u0, i)
                    dve.wait_ge(unit_done, u0 + 4 * i)
                    product(i)
                    ada(0, 4 * f - 1 + i, 8 * f + i)
                    split(u0 + 1, i)
                    split(u0 + 2, i)
                    hidden(4, i)
                    ada(1, 4 * f - 1 + i, 8 * f + i)
                    split(u0 + 3, i)
                t = u0 + 4 * NFULL
                split(t)
                dve.wait_ge(unit_done, t)
                product(NFULL)
                ada_tail(0)
                split(t + 1)
                hidden(4, NFULL)
                ada_tail(1)
                split(t + 2)
                product(NFULL + 1, 256, 256, 0)
                ada_tail(2)
                split(t + 3)
                hidden(2, NFULL + 1)
                ada_tail(3)
                for d in range(2, KF // 2):
                    split(t + 2 + d)
                    if d < 6:
                        ada_tail(d + 2)
                    if f == 1 and d == 7:
                        modulation()
                    if f == 1 and d >= 7:
                        gate_rows(d - 7)

            dve.wait_ge(sig("pos_in"), 16)
            dve.tensor_copy(rows[R_POS:R_POS + M, :], pos_i[R_POS:R_POS + M, :]).then_inc(sig("pos_row"), 1)
            dve.wait_ge(sig("cols_turned"), 1)
            dve.tensor_copy(cols[:, :], pj[:, 0, 0:NROW]).then_inc(sig("cols_ready"), 1)
            operand(0, cols[:, R_G1:R_G1 + KD], order=(0, 1))
            split(U_F1)
            operand(0, cols[:, R_G1:R_G1 + KD], order=(2, 3), start=2)


            def make_angles():
                dve.wait_ge(sig("spread_in"), 16 * 6)
                for m in range(M):
                    for a_ in range(2):
                        ins = dve.tensor_scalar(ang[:, a_, m, :], inv[:, :], cols[:, R_POS + m:R_POS + m + 1], None, ALU.mult)
                step(ins)
                settle()
                step(dve.tensor_scalar(turns[:, 0, :, :], ang[:, 0, :, :], 1 / TURN, None, ALU.mult))
                step(dve.tensor_scalar(turns[:, 1, :, :], ang[:, 1, :, :], 1 / TURN, 0.25, ALU.mult, ALU.add))
                settle()
                step(dve.tensor_scalar(nturn[:, :, :, :], turns[:, :, :, :], ROUND, None, ALU.add))
                settle()
                step(dve.tensor_scalar(nturn[:, :, :, :], nturn[:, :, :, :], -ROUND, None, ALU.add))
                settle()
                for part_of_turn in (TURN1, TURN2, TURN3):
                    step(dve.scalar_tensor_tensor(ang[:, :, :, :], nturn[:, :, :, :], -part_of_turn, ang[:, :, :, :],
                                                  ALU.mult, ALU.add))
                    settle()
                step(dve.tensor_scalar(ang[:, 1, :, :], ang[:, 1, :, :], float(np.pi / 2), None, ALU.add))
                settle()
                dve.tensor_scalar(ang[:, :, :, :], ang[:, :, :, :], 3.1415925, -3.1415925, ALU.min, ALU.max)\
                    .then_inc(sig("angles"), 1)

            def logs():
                dve.scalar_tensor_tensor(lgt[:, :, :], lgd[:, :, :], -1.0, lgd[:, :, :], ALU.mult, ALU.max)
                step(dve.tensor_tensor(lamt[:, :, :], lamp[:, 0:4:2, :], lamp[:, 1:4:2, :], ALU.mult))
                lb_cols = cols[:, R_LB:R_LB + 4].rearrange("p (d g) -> p d g", d=2)
                dve.tensor_tensor(lbt[:, :, :], lb_cols, lb_cols, ALU.subtract)
                settle()
                dve.tensor_reduce(lams[:, 0:2], lamt[:, :, :], AX.X, ALU.add).then_inc(sig("logs_in"), 1)
            def masks_and_bounds():
                dve.wait_ge(sig("ramps"), 1)
                dve.scalar_tensor_tensor(dist[:, :, :], dist_r[:, :, :], -1.0, dist_r[:, :, :], ALU.mult, ALU.max)
                dve.tensor_scalar(reach[:, 0, :], rel[:, :], 0.0, None, ALU.max)
                dve.tensor_scalar(reach[:, 1, :], rel[:, :], -1.0, 0.0, ALU.mult, ALU.max)
                dve.tensor_scalar(subg[:, 4:KD], cols[:, R_SUB:R_SUB + 1].to_broadcast([P, 4]), 1.0 - LAM_INIT, None,
                                  ALU.mult)
                step(dve.tensor_tensor(idx_x[:, :], idx_i[:, 0, :], idx_i[:, 1, :], ALU.bitwise_xor))
                settle()
                for lvl in range(7):
                    dve.tensor_scalar(masks[:, lvl, :], idx_x[:, :], float(2 ** lvl), None, ALU.is_ge)
                dve.wait_ge(sig("logs_out"), 1)
                step(dve.scalar_tensor_tensor(lgd[:, :, :], lgd[:, :, :], 0.0, lgt[:, :, :], ALU.min, ALU.subtract))
                dve.scalar_tensor_tensor(lams[:, 2:3], lams[:, 1:2], -LAM_INIT, lams[:, 0:1], ALU.add, ALU.subtract)
                step(dve.reciprocal(lb1[:, :, :], lbt[:, :, :]))
                settle()
                step(dve.tensor_tensor(lbt[:, :, :], lbt[:, :, :], lb1[:, :, :], ALU.mult))
                settle()
                step(dve.tensor_tensor(lb[:, :, :], lbt[:, :, :], lbt[:, :, :], ALU.subtract))
                settle()
                step(dve.tensor_scalar(lb1[:, :, :], lb[:, :, :], -1.0, 1.0, ALU.mult, ALU.add))
                dve.wait_ge(sig("cond_ready"), 1)

            ffn(0, U_F1, 0, (make_angles, logs, masks_and_bounds))

            split(U_IN)
            residual(1, U_IN - 1, 0.5)
            operand(1, cols[:, R_MIX:R_MIX + KD], order=(2, 3, 0, 1))
            split(U_IN + 1)
            rstd_of(1)
            dve.wait_ge(sig("trig_ready"), 1)
            dve.wait_ge(sig("rstd_ready"), 2)
            for m in range(M):
                ins = dve.tensor_scalar(trig_r[:, :, m, :], trig[:, :, m, 0:32], rstd[:, m:m + 1], None, ALU.mult)
            step(ins)
            split(U_IN + 2)

            def rotate(o1, o2, x1, x2, sin, cos, t1, t2):
                settle()
                step(dve.tensor_tensor(t1, x2, sin, ALU.mult))
                step(dve.tensor_tensor(t2, x1, sin, ALU.mult))
                settle()
                step(dve.tensor_tensor(o1, x1, cos, ALU.mult))
                step(dve.tensor_tensor(o2, x2, cos, ALU.mult))
                settle()
                dve.tensor_tensor(o1, o1, t1, ALU.subtract)
                return dve.tensor_tensor(o2, o2, t2, ALU.add)

            def rotate_ret(n):
                src = pj[:, 2 * n:2 * n + 2, :]
                s4 = src.rearrange("p m (h n) -> p m h n", n=HD)
                o4 = rqk[:, n, :, :].rearrange("p m (h n) -> p m h n", n=HD)

                def heads(t):
                    return t.unsqueeze(2).to_broadcast([P, M, H, 32])

                def temp(k):
                    return tmp_r[:, k, :, :].rearrange("p m (h n) -> p m h n", n=32)

                rotate(o4[:, :, :, 0:32], o4[:, :, :, 32:64], s4[:, :, :, 0:32], s4[:, :, :, 32:64],
                       heads(trig_r[:, 0, :, :]), heads(trig_r[:, 1, :, :]), temp(0), temp(1)).then_inc(sig("rot"), 1)

            def decay_log(h):
                step(dve.tensor_scalar(decay[:, h % 2, :], reach[:, 0, :], lgd[:, 0, h:h + 1], None, ALU.mult))
                settle()
                dve.scalar_tensor_tensor(decay[:, h % 2, :], reach[:, 1, :], lgd[:, 1, h:h + 1], decay[:, h % 2, :],
                                         ALU.mult, ALU.add).then_inc(sig("decay_log"), 1)

            def decayed(h):
                dve.wait_ge(sig("decay_ready"), h + 1)
                dve.wait_ge(sig("ret_scored"), h + 1)
                if h >= 2:
                    dve.wait_ge(sig("ret_valued"), h - 1)
                for jt in range(M):
                    ins_ = dve.scalar_tensor_tensor(rpT[:, h % 2, jt, :], aux[:, h % 2, jt * S:(jt + 1) * S],
                                                    HD ** -0.5, decay[:, h % 2, P * (1 - jt):P * (1 - jt) + S],
                                                    ALU.mult, ALU.mult)
                ins_.then_inc(sig("rpT_ready"), 1)
                if h + 2 < H:
                    dve.wait_ge(sig("rpT_ready"), h + 1)
                    decay_log(h + 2)

            def heads64(t):
                return t.unsqueeze(3).to_broadcast([P, M, H, HD])

            r4 = aux[:, 2:4, :].rearrange("p m (h n) -> p m h n", n=HD)
            mr4 = mix_r[:, :, :].rearrange("p m (h n) -> p m h n", n=HD)
            def centre():
                dve.wait_ge(sig("ret_valued"), H)
                dve.wait_ge(sig("q_rot"), 1)
                step(dve.tensor_reduce(gsum[:, :, :], r4, AX.X, ALU.add))
                settle()
                step(dve.tensor_scalar(gsum[:, :, :], gsum[:, :, :], -1.0 / HD, None, ALU.mult))
                settle()
                dve.tensor_tensor(mr4, r4, heads64(gsum[:, :, :]), ALU.add).then_inc(sig("centred"), 1)

            dve.wait_ge(unit_done, U_IN + 2)
            rotate_ret(0)
            split(U_IN + 3)
            split(U_IN + 4)
            dve.wait_ge(unit_done, U_IN + 4)
            dve.wait_ge(sig("rot"), 1)
            rotate_ret(1)
            split(U_IN + 5)
            decay_log(0)
            decay_log(1)
            split(U_IN + 6)
            dve.wait_ge(sig("ret_turned"), 2)
            dve.tensor_copy(rqkT[:, 1, :, :].rearrange("p g s -> p (g s)"),
                            aux[:, 2:4, :].rearrange("p b n -> p (b n)")).then_inc(sig("rqkT_k"), 1)
            split(U_IN + 7)
            dve.wait_ge(sig("rot"), 2)
            decayed(0)
            split(U_IN + 8)
            decayed(1)
            dve.wait_ge(sig("p0_ready"), 1)
            k1, k2 = p0[:, :, QR + KVR:QR + KVR + 16], p0[:, :, QR + KVR + 16:C0]
            step(rotate(k1, k2, k1, k2, trig[:, 0, :, 32:48], trig[:, 1, :, 32:48], mix_r[:, :, 0:16],
                        mix_r[:, :, 256:272]))
            dve.wait_ge(sig("crms_ready"), 1)
            step(dve.reciprocal(crstd[:, :, :], crms[:, :, :]))
            settle()
            dve.tensor_scalar(crstd[:, :, 0], crstd[:, :, 0], MLA_SCALE, None, ALU.mult).then_inc(sig("crstd_ready"), 1)
            split(U_IN + 9)
            for k in range(3):
                dve.wait_ge(sig("cT_hi"), max(k + 1, 2))
                dve.scalar_tensor_tensor(cT_lo[:, k, :], pj[:, 2 + k // 2, (k % 2) * S:(k % 2 + 1) * S],
                                         cols[:, R_Q + k:R_Q + k + 1], cT_hi[:, k, :].bitcast(F32),
                                         ALU.mult, ALU.subtract).then_inc(sig("cT_lo"), 1)
            decayed(2)
            split(U_UQ)
            decayed(3)
            split(U_UKV)
            decayed(4)
            decayed(5)
            decayed(6)
            decayed(7)
            dve.wait_ge(sig("qf_ready"), 1)
            q4 = qf[:, :, :].rearrange("p m (h n) -> p m h n", n=QK)

            def mla_heads(t):
                return t.unsqueeze(2).to_broadcast([P, M, H, 16])

            def mla_temp(k):
                return mix_r[:, :, 256 * k:256 * k + 128].rearrange("p m (h n) -> p m h n", n=16)

            q1, q2 = q4[:, :, :, NOPE:NOPE + 16], q4[:, :, :, NOPE + 16:QK]
            rotate(q1, q2, q1, q2, mla_heads(trig[:, 0, :, 32:48]), mla_heads(trig[:, 1, :, 32:48]),
                   mla_temp(0), mla_temp(1)).then_inc(sig("q_rot"), 1)
            centre()
            dve.wait_ge(sig("kv_ready"), 1)
            dve.tensor_copy(kf[:, :, :].rearrange("p m (h n) -> p m h n", n=QK)[:, :, :, NOPE:QK],
                            p0[:, :, QR + KVR:C0].unsqueeze(2).to_broadcast([P, M, H, ROPE]))\
                .then_inc(sig("kf_ready"), 1)

            for b in range(4):
                dve.wait_ge(sig("mla_turned"), 5 + b)
                dve.tensor_copy(kT[0:QK, 2 * b:2 * b + 2, :].rearrange("p h s -> p (h s)"), aux[0:QK, b, :])\
                    .then_inc(sig("kT_ready"), 1)
            dve.wait_ge(sig("gn_square"), 1)
            dve.tensor_reduce(gvar[:, :, :].rearrange("p m h -> p (m h)"),
                              tmp_r[:, :, :, :].rearrange("p a m s -> p (a m s)").rearrange("p (x n) -> p x n", n=HD),
                              AX.X, ALU.add).then_inc(sig("gvar_ready"), 1)

            def mla_max(h):
                dve.wait_ge(sig("mla_scored"), h + 1)
                dve.tensor_reduce(mx[:, h % 2, :], aux[:, h % 2, :].rearrange("p (m s) -> p m s", m=M), AX.X, ALU.max,
                                  negate=True).then_inc(sig("mla_max"), 1)

            def mla_prob(h):
                dve.wait_ge(sig("prob_turned"), h + 1)
                if h >= 2:
                    dve.wait_ge(sig("mla_valued"), h - 1)
                dve.tensor_copy(probT[:, h % 2, :, :].rearrange("p k s -> p (k s)"), aux[:, 2 + h % 2, :])\
                    .then_inc(sig("probT_ready"), 1)

            for s in range(H + 1):
                if s < H:
                    mla_max(s)
                if s >= 1:
                    mla_prob(s - 1)
                if s in (2, 5):
                    split(U_O + s // 5)
                if s == 1:
                    dve.wait_ge(sig("grms_ready"), 1)
                    dve.wait_ge(sig("centred"), 1)
                    step(dve.reciprocal(grstd[:, :, :], grms[:, :, :]))
                    settle()
                    step(dve.tensor_tensor(mr4, mr4, heads64(grstd[:, :, :]), ALU.mult))
                if s == 4:
                    settle()
                    dve.tensor_tensor(mix_r[:, :, :], mix_r[:, :, :], sgr[:, :, :], ALU.mult)\
                        .then_inc(sig("mix_ready"), 1)
            dve.wait_ge(sig("mla_exp"), H)
            step(dve.reciprocal(rinv[:, :, :], rowsum[:, :, :]))
            operand(2, order=(0, 1))
            dve.wait_ge(sig("mla_valued"), H)
            settle()
            dve.tensor_tensor(mix_a[:, :, :].rearrange("p m (h n) -> p m h n", n=HD),
                              pj[:, 0:2, :].rearrange("p m (h n) -> p m h n", n=HD), heads64(rinv[:, :, :]),
                              ALU.mult).then_inc(sig("mix_ready"), 1)
            operand(2, order=(2, 3), start=2)
            split(U_O + 2)
            split(U_O + 3)
            split(U_F2)
            residual(4, U_O + 3, 1.0)

            operand(3, cols[:, R_G2:R_G2 + KD], order=(2, 3, 0, 1))
            ffn(1, U_F2, 2)

            split(U_IN2)

            dve.wait_ge(sig("gains_in"), 16 * 3)

            def gained(h):
                dve.wait_ge(sig("x_ready"), 5 + (h == 0))
                cols_h = slice(512 * h, 512 * h + 512)
                dve.tensor_tensor(xn[:, :, cols_h], x[:, :, cols_h],
                                  norm_row[:, cols_h].unsqueeze(1).to_broadcast([P, M, 512]), ALU.mult)\
                    .then_inc(sig("xg_ready"), 1)

            residual(5, U_IN2 - 1, 0.5, gained)
            dve.wait_ge(sig("squared"), 4)
            step(dve.tensor_tensor(tot[:, :, :], ss[:, :, 0, :], ss[:, :, 1, :], ALU.add))
            settle()
            step(dve.tensor_scalar(ms[:, 0, :], tot[:, 0, :], 1.0 / D, EPS, ALU.mult, ALU.add))
            settle()
            step(dve.reciprocal(rstd2[:, 0, :], ms[:, 0, :]))
            settle()
            step(dve.scalar_tensor_tensor(ms[:, 1, :], tot[:, 1, :], 1.0 / D, rstd2[:, 0, :], ALU.mult, ALU.mult))
            settle()
            dve.tensor_scalar(ms[:, 1, :], ms[:, 1, :], EPS, None, ALU.add).then_inc(sig("ss_ready"), 1)
            dve.wait_ge(sig("rms_ready"), 4)
            step(dve.reciprocal(rstd2[:, :, :], rms2[:, :, :]))
            settle()
            dve.tensor_tensor(rstd[:, :], rstd2[:, 0, :], rstd2[:, 1, :], ALU.mult).then_inc(sig("rstd_ready"), 1)
            dve.wait_ge(sig("rstd_ready"), 4)
            for m in range(M):
                dve.tensor_scalar(xn[:, m, :], xn[:, m, :], rstd[:, m:m + 1], None, ALU.mult)\
                    .then_inc(sig("xn_ready"), 1)
            for m in range(M):
                ins = dve.scalar_tensor_tensor(x[:, m, :], x[:, m, :], rstd2[:, 0, m:m + 1], norm_row[:, :], ALU.mult,
                                               ALU.mult)
            ins.then_inc(sig("normed"), 1)

            def normalise(n):
                rstd_of(n)
                dve.wait_ge(sig("rstd_ready"), n + 1)
                for m in range(M):
                    dve.tensor_scalar(xn[:, m, :], x[:, m, :], rstd[:, m:m + 1], None, ALU.mult)\
                        .then_inc(sig("xn_ready"), 1)

            operand(4, bias=True)
            c = U_IN2
            for n in range(1, 6):
                split(c + n)

            def banks(b):
                return aux[:, b:b + 2, :].rearrange("p b n -> p (b n)")

            dve.wait_ge(sig("blocks_turned"), 1)
            dve.tensor_copy(zz[:, 0, 0:2, :].rearrange("p g s -> p (g s)"), aux[:, 1, :])
            dve.wait_ge(sig("q_silu"), 1)
            dve.tensor_scalar(qt[:, 0:2, :], qt[:, 0:2, :], HD ** -0.5, None, ALU.mult).then_inc(sig("turned_read"), 1)
            split(c + 6)
            split(c + 7)
            dve.wait_ge(sig("blocks_turned"), 2)
            dve.tensor_copy(zz[:, 1, 0:2, :].rearrange("p g s -> p (g s)"), aux[:, 2, :])\
                .then_inc(sig("turned_read"), 1)
            dve.wait_ge(sig("turned_read"), 2)
            dve.scalar_tensor_tensor(ee[:, :, 0:2, :], zz[:, :, 0:2, :], -1.0, zz[:, :, 0:2, :], ALU.mult, ALU.max)\
                .then_inc(sig("abs_z"), 1)
            split(U_LR)
            dve.wait_ge(sig("softplus"), 1)
            step(dve.scalar_tensor_tensor(ll[:, :, 0:2, :], zz[:, :, 0:2, :], 0.0, ee[:, :, 0:2, :], ALU.min,
                                          ALU.subtract))
            split(U_ATT)
            settle()
            dve.tensor_tensor(kk[:, :, 0:2, :], ll[:, :, 0:2, :], zz[:, :, 0:2, :], ALU.subtract)
            dve.tensor_scalar(ee[:, :, 0:2, :], zz[:, :, 0:2, :], -1.0, 80.0, ALU.mult, ALU.min)\
                .then_inc(sig("log_k"), 1)
            split(U_ATT + 1)
            dve.wait_ge(sig("k_exp"), 1)
            for dst, by, last in ((kk, lb1, False), (ee, lb, True)):
                for d in range(2):
                    ins = dve.tensor_tensor(dst[:, d, 0:2, :], dst[:, d, 0:2, :],
                                            by[:, d, :].unsqueeze(2).to_broadcast([P, 2, S]), ALU.mult)
                if last:
                    ins.then_inc(sig("lb_term"), 1)
                else:
                    step(ins)
            dve.wait_ge(sig("blocks_turned"), 3)
            dve.tensor_scalar(qt[:, 2, :], aux[:, 3, 0:S], 32 ** -0.5, None, ALU.mult)
            for d in range(2):
                ins = dve.tensor_copy(kk[:, d, 2, :], aux[:, 3, S:2 * S])
            ins.then_inc(sig("turned_read"), 1)
            dve.wait_ge(sig("turned_read"), 3)
            step(dve.tensor_copy(qkh[:, 0, 0, :, :], qt[:, :, :]))
            dve.tensor_tensor(qkh[:, 0, 1, :, :], kk[:, 0, :, :], kk[:, 1, :, :], ALU.add).then_inc(sig("qk_ready"), 1)
            dve.wait_ge(sig("lb_log"), 1)
            step(dve.tensor_tensor(ll[:, :, 0:2, :], ll[:, :, 0:2, :], ee[:, :, 0:2, :], ALU.add))
            split(U_ATT + 2)
            dve.wait_ge(sig("gla_z_read"), 1)
            dve.scalar_tensor_tensor(ee[:, :, 2, :], zz[:, :, 2, :], -1.0, zz[:, :, 2, :], ALU.mult, ALU.max)\
                .then_inc(sig("abs_z"), 1)
            split(U_ATT + 3)
            dve.wait_ge(sig("softplus"), 2)
            dve.scalar_tensor_tensor(ll[:, :, 2, :], zz[:, :, 2, :], 0.0, ee[:, :, 2, :], ALU.min, ALU.subtract)\
                .then_inc(sig("zz_used"), 1)
            dve.wait_ge(sig("zz_used"), 1)
            dve.tensor_scalar(ll[:, :, 2, :], ll[:, :, 2, :], 1.0 / 16.0, None, ALU.mult).then_inc(sig("sums_ready"), 1)
            split(U_ATT + 4)
            dve.wait_ge(sig("blocks_turned"), 4)
            dve.tensor_scalar(aqT[:, :, :].rearrange("p h s -> p (h s)"), banks(2), HD ** -0.5, None, ALU.mult)\
                .then_inc(sig("turned_read"), 1)
            split(U_ATT + 5)
            dve.wait_ge(sig("normed"), 1)
            dve.wait_ge(sig("blocks_turned"), 5)
            dve.tensor_copy(akT[:, :, :].rearrange("p h s -> p (h s)"), banks(0)).then_inc(sig("turned_read"), 1)

            def diff_bias(h):
                dve.wait_ge(sig("diff_scored"), h + 1)
                if h:
                    dve.wait_ge(sig("diff_turned"), h)
                dve.scalar_tensor_tensor(dmap[:, :, :, :].rearrange("p j m s -> p j (m s)"),
                                         dist[:, :, :].rearrange("p m s -> p (m s)").unsqueeze(1)
                                         .to_broadcast([P, 2, M * S]),
                                         -(2.0 ** (-8.0 * (h + 1) / DH)), aux[:, 0:2, :], ALU.mult, ALU.add)\
                    .then_inc(sig("biased"), 1)
                dve.wait_ge(sig("biased"), h + 1)
                dve.tensor_reduce(dl[:, :, :], dmap[:, :, :, :], AX.X, ALU.max, negate=True)\
                    .then_inc(sig("diff_max"), 1)

            def diff_combine(h):
                dve.wait_ge(sig("diff_exp"), h + 1)
                step(dve.reciprocal(dr[:, :, :], dr[:, :, :]))
                settle()
                step(dve.tensor_scalar(dr[:, 1, :], dr[:, 1, :], lams[:, 2:3], None, ALU.mult))
                for m in range(M):
                    step(dve.tensor_scalar(dmap[:, 0, m, :], dmap[:, 0, m, :], dr[:, 0, m:m + 1], None, ALU.mult))
                settle()
                for m in range(M):
                    ins_ = dve.scalar_tensor_tensor(dmap[:, 0, m, :], dmap[:, 1, m, :], dr[:, 1, m:m + 1],
                                                    dmap[:, 0, m, :], ALU.mult, ALU.add)
                ins_.then_inc(sig("diff_w"), 1)

            def read_level(n):
                dve.wait_ge(sig("level_scored"), n + 1)
                if n == 0:
                    ins_ = dve.tensor_copy(near[:, :, :], aux[:, :, :])
                else:
                    dve.wait_ge(sig("level_read"), n)
                    ins_ = dve.copy_predicated(near[:, :, :].rearrange("p b (x t) -> p (b x) t", t=P),
                                               masks[:, n - 1, :].unsqueeze(1).to_broadcast([P, 16, P]),
                                               aux[:, :, :].rearrange("p b (x t) -> p (b x) t", t=P))
                ins_.then_inc(sig("level_read"), 1)

            def halves(t, lvl):
                v = t.rearrange("p g (b e n) -> p (g b) e n", e=2, n=2 ** (lvl - 1))
                return v[:, :, 0, :], v[:, :, 1, :]

            for lvl in range(1, LEVELS):
                dve.wait_ge(sig("exps_ready"), lvl)
                if lvl >= 2:
                    dve.wait_ge(sig("level_scored"), lvl - 1)
                b = lvl % 2
                dve.tensor_tensor(qkh[:, b, 0, :, :], qt[:, :, :], eqk[:, 0, :, :], ALU.mult)
                (o_l, o_r), (e_l, e_r) = halves(qkh[:, b, 1, :, :], lvl), halves(eqk[:, 1, :, :], lvl)
                dve.tensor_tensor(o_l, halves(kk[:, 0, :, :], lvl)[0], e_l, ALU.mult)
                dve.tensor_tensor(o_r, halves(kk[:, 1, :, :], lvl)[1], e_r, ALU.mult).then_inc(sig("qk_ready"), 1)
                split(U_GATES + lvl - 1)
                read_level(lvl - 1)
            split(U_GATES + 8)

            for n in range(2):
                v = og[:, :, n * S:(n + 1) * S].rearrange("p m (h n) -> p m h n", n=HD)
                ins = dve.tensor_tensor(v, v, headg[:, n, :].unsqueeze(1).unsqueeze(1).to_broadcast([P, M, DH, HD]),
                                        ALU.mult)
            step(ins)
            split(U_GATES + 9)
            split(U_GATES + 10)
            diff_bias(0)
            diff_combine(0)
            diff_bias(1)
            split(U_GATES + 11)
            diff_combine(1)
            diff_bias(2)
            dve.wait_ge(sig("head_square"), 1)
            dve.tensor_reduce(gsum[:, :, :], sq_r[:, :, :].rearrange("p m (h n) -> p m h n", n=HD), AX.X, ALU.add)\
                .then_inc(sig("head_sums"), 1)
            dve.wait_ge(sig("head_rms"), 1)
            step(dve.reciprocal(grstd[:, :, :], rinv[:, :, :]))
            settle()
            orec = omix_r[:, :, :].rearrange("p m (h n) -> p m h n", n=HD)
            step(dve.tensor_tensor(orec, orec, heads64(grstd[:, :, :]), ALU.mult))
            settle()
            dve.tensor_tensor(omix_r[:, :, :], omix_r[:, :, :], og[:, :, :], ALU.mult).then_inc(sig("omix_ready"), 1)
            diff_combine(2)
            operand(5, order=(0, 1), at_=pj[:, 2:4, :])
            split(U_UP)
            diff_bias(3)
            diff_combine(3)
            split(U_UP + 1)

            def branch_gate(i, n, h):
                if h:
                    dve.wait_ge(sig("gates_ready"), i + 1)
                    dve.wait_ge(sig("half1"), 6 + i)
                else:
                    dve.wait_ge(unit_done, (U_UP + 1, U_UP + 2, U_UP + 4)[i])
                g = gates[:, :, n * D + 512 * h:n * D + 512 * h + 512]
                dst = merged[:, :, 512 * h:512 * h + 512] if i == 0 else g
                dve.tensor_tensor(dst, pj[:, 2 * h:2 * h + 2, :], g, ALU.mult).then_inc(sig("branch_read"), 1)

            def branch_add(i, n, h):
                dve.wait_ge(sig("branch_read"), 2 * i + (h == 0) + 1)
                dst = merged[:, :, 512 * h:512 * h + 512]
                return dve.tensor_tensor(dst, dst, gates[:, :, n * D + 512 * h:n * D + 512 * h + 512], ALU.add)

            branch_gate(0, 1, 1)
            branch_gate(0, 1, 0)
            dve.wait_ge(sig("head_square"), 2)
            dve.tensor_reduce(gvar[:, :, 0:DH], sq_a[:, :, :].rearrange("p m (h n) -> p m h n", n=P), AX.X, ALU.add)\
                .then_inc(sig("head_sums"), 1)
            dve.wait_ge(sig("head_rms"), 2)
            step(dve.reciprocal(grstd[:, :, 0:DH], grms[:, :, 0:DH]))
            settle()
            oa = omix_a[:, :, :].rearrange("p m (h n) -> p m h n", n=P)
            dve.tensor_tensor(oa, oa, grstd[:, :, 0:DH].unsqueeze(3).to_broadcast([P, M, DH, P]), ALU.mult)\
                .then_inc(sig("omix_ready"), 1)
            branch_gate(1, 2, 1)
            split(U_UP + 2)
            operand(5, subg, order=(2, 3), start=2)
            branch_gate(1, 2, 0)
            split(U_UP + 3)
            step(branch_add(1, 2, 1))
            step(branch_add(1, 2, 0))
            settle()
            split(U_OUT)
            for h in (1, 0):
                branch_gate(2, 0, h)
                branch_add(2, 0, h).then_inc(sig("merged"), 1)
            operand(6, order=(2, 3))
            split(U_OUT + 1)
            operand(6, order=(0, 1), start=2)
            for d in range(2, 4):
                split(U_OUT + d)
            split(U_W1)

            def gated_residual(n, n_half1, last_unit, temp):
                for h in (1, 0):
                    if h:
                        dve.wait_ge(sig("half1"), n_half1)
                    else:
                        dve.wait_ge(unit_done, last_unit + 1)
                    dst, src = halves_of_x(h)
                    t = temp[:, :, 512 * h:512 * h + 512]
                    g = gt_row[:, n, 512 * h:512 * h + 512].unsqueeze(1).to_broadcast([P, M, 512])
                    step(dve.tensor_tensor(t, src, g, ALU.mult))
                    settle()
                    dve.tensor_tensor(dst, dst, t, ALU.add).then_inc(sig("x_ready"), 1)

            gated_residual(0, 9, U_OUT + 3, part)

            normalise(4)
            operand(7, bias=True)
            split(U_W1 + 1)

            def square(par, i, n):
                dve.wait_ge(sig("relu_done"), n + 2 * i)
                v = chunk[:, par, :, :]
                dve.tensor_tensor(v, v, v, ALU.mult).then_inc(sig("sq_ready"), 1)

            def sq_lo(par, i, n):
                dve.wait_ge(sig("sqT_hi"), n + 2 * i)
                at_ = bass.ds(4 * (n + 2 * i) - 4, 4)
                dve.tensor_tensor(hT_lo[:, at_, :],
                                  aux[:, 2 * par:2 * par + 2, :].rearrange("p b (k s) -> p (b k) s", k=2),
                                  hT_hi[:, at_, :].bitcast(F32), ALU.subtract).then_inc(sig("sqT_lo"), 1)

            def mlp_pair(i, first):
                for par in range(2):
                    c_ = U_W1 + 2 * par
                    if not (first and par == 0):
                        split(c_, i)
                        square(1 - par, i, par)
                        split(c_ + 1, i)
                        sq_lo(1 - par, i, par)

            mlp_pair(0, True)
            with dve.Fori(1, KF2 // 8) as i:
                mlp_pair(i, False)
            split(U_W2)
            square(1, 0, KF2 // 4)
            split(U_W2 + 1)
            sq_lo(1, 0, KF2 // 4)
            for d in range(2, KF2 // 2):
                split(U_W2 + d)
            gated_residual(1, 10, U_W2 + KF2 // 2 - 1, part2)
            rstd_of(5)
            dve.wait_ge(sig("rstd_ready"), 6)
            dve.wait_ge(sig("row2_in"), 16)
            for m in range(M):
                ins = dve.scalar_tensor_tensor(x[:, m, :], x[:, m, :], rstd[:, m:m + 1], norm_row[:, :], ALU.mult,
                                               ALU.mult)
            ins.then_inc(sig("y_ready"), 1)

        @block.gpsimd
        def _(pool):
            steps = [0]

            def step(ins):
                steps[0] += 1
                ins.then_inc(sig("pool_step"), 1)

            def settle():
                pool.wait_ge(sig("pool_step"), steps[0])

            pool.memset(ident[:, :], 1.0).then_inc(sig("ident_ready"), 1)
            pool.wait_ge(sig("ident_ready"), 1)
            pool.affine_select(ident[:, :], ident[:, :], pattern=[[-1, P]], compare_op=ALU.is_equal, fill=0.0, base=0,
                               channel_multiplier=1).then_inc(sig("ident_ready"), 1)
            pool.memset(ones[:, :], 1.0)
            pool.memset(one[:, :], 1.0)
            pool.memset(eps[:, :], EPS).then_inc(sig("consts"), 1)
            pool.memset(gate2[:, :, :], 0.0).then_inc(sig("gate2_zero"), 1)
            pool.iota(rel[:, :], pattern=[[1, 3 * P]], base=-P, channel_multiplier=-1,
                      allow_small_or_imprecise_dtypes=True)
            pool.iota(dist_r[:, :, :], pattern=[[-P, M], [1, S]], base=0, channel_multiplier=-1,
                      allow_small_or_imprecise_dtypes=True)
            pool.iota(idx_i[:, 0, :], pattern=[[0, P]], base=0, channel_multiplier=1)
            pool.iota(idx_i[:, 1, :], pattern=[[1, P]], base=0, channel_multiplier=0).then_inc(sig("ramps"), 1)
            pool.memset(acc[:, :], 0.0).then_inc(sig("ada_free"), 2)

            def halves(t, lvl):
                v = t.rearrange("p g (b e n) -> p (g b) e n", e=2, n=2 ** (lvl - 1))
                return v[:, :, 0, :], v[:, :, 1, :]

            pool.wait_ge(sig("zz_used"), 1)
            pool.memset(xx[:, :, :, :], 0.0).then_inc(sig("xx_zero"), 1)
            for lvl in range(1, LEVELS - 1):
                n = 2 ** (lvl - 1)
                pool.wait_ge(sig("exps_ready"), lvl)
                (f_l, f_r), (b_l, b_r) = halves(ll[:, 0, :, :], lvl), halves(ll[:, 1, :, :], lvl)
                xf_l, xb_r = halves(xx[:, 0, :, :], lvl)[0], halves(xx[:, 1, :, :], lvl)[1]
                shape = [P, 3 * S // (2 * n), n]
                pool.tensor_tensor(xf_l, xf_l, f_r[:, :, n - 1:n].to_broadcast(shape), ALU.add)
                step(pool.tensor_tensor(xb_r, xb_r, b_l[:, :, 0:1].to_broadcast(shape), ALU.add))
                settle()
                pool.tensor_tensor(f_r, f_r, f_l[:, :, n - 1:n].to_broadcast(shape), ALU.add)
                pool.tensor_tensor(b_l, b_l, b_r[:, :, 0:1].to_broadcast(shape), ALU.add)\
                    .then_inc(sig("sums_ready"), 1)


_INS = [
    "x", "positions", "ffn1_norm", "ffn1_w_gate", "ffn1_w_up", "ffn1_w_down", "mix_norm", "w_in", "q_norm",
    "w_uq", "kv_norm", "w_ukv", "ret_decay_fwd", "ret_decay_bwd", "w_o", "ffn2_norm", "ffn2_w_gate",
    "ffn2_w_up", "ffn2_w_down", "final_norm", "c_2", "ada_w_2", "ada_b_2", "norm_mix_g_2", "norm_mlp_g_2",
    "w_in_2", "diff_lambda_2", "diff_subln_g_2", "hgrn_lb_logits_2", "hgrn_norm_g_2", "gla_gate_w2_2",
    "gla_gate_b_2", "gla_norm_g_2", "w_up_a_2", "w_up_b_2", "w_up_c_2", "w_out_2", "mlp_w1_2", "mlp_w2_2",
    "final_norm_g_2", "inv_freq"]


def kernel(**inputs):
    import numpy as _np
    import concourse.bacc as _bacc
    from concourse import mybir as _mybir
    from concourse.bass_utils import run_bass_kernel_spmd as _run

    inv_freq = _np.concatenate([_np.float32(ROPE_THETA) ** (-_np.arange(n, dtype=_np.float32) / _np.float32(n))
                                for n in (HD // 2, ROPE // 2)]).astype(_np.float32)[None, :]
    nc = _bacc.Bacc("TRN2", target_bir_lowering=False, num_devices=1)
    arrays, args = {}, {}
    for name in _INS:
        v = inv_freq if name == "inv_freq" else _np.ascontiguousarray(inputs[name])
        arrays[f"in_{name}_dram"] = v
        args[name] = nc.dram_tensor(f"in_{name}_dram", v.shape, _mybir.dt.from_np(v.dtype), kind="ExternalInput").ap()
    out = nc.dram_tensor("out_0_dram", (1, S, D), F32, kind="ExternalOutput").ap()
    build(nc, args, out)
    r = _run(nc, [arrays], core_ids=[0])
    return r.results[0]["out_0_dram"]
```
